# Optimizing a Trainium2 kernel written in Bass

```python
import jax, jax.numpy as jnp
from jax import lax
import numpy as np

D_MODEL = 1024
BATCH = 1
SEQ = 2048
DEPTH = 1

CHUNK = 64
HEAD_DIM = 64
EPS = 1e-6
A_HEADS = 8
A_KV_HEADS = 2
A_GROUP = A_HEADS // A_KV_HEADS
WINDOW = 128
WINDOW_CHUNKS = WINDOW // CHUNK
B_HEADS = 8
Q_RANK = 256
KV_RANK = 128
IDX_HEADS = 4
IDX_DIM = 64
TOPK_MAX = 256
B_QBLOCK = 128
D_MIX = A_HEADS * HEAD_DIM + B_HEADS * HEAD_DIM
D_FF = -(-8 * D_MODEL // (3 * 256)) * 256
IN_SIZES = (A_HEADS * HEAD_DIM,
            A_KV_HEADS * HEAD_DIM,
            A_KV_HEADS * HEAD_DIM,
            Q_RANK,
            KV_RANK,
            IDX_DIM,
            IDX_HEADS)
D_IN = sum(IN_SIZES)

kernel_name = "hymba_swa_sink_dsa_alibi_sandwich_adaln"

def rms_norm(x, g):
    xf = x.astype(jnp.float32)
    y = xf * lax.rsqrt(jnp.mean(xf * xf, axis=-1, keepdims=True) + EPS)
    return (y * g.astype(jnp.float32)).astype(x.dtype)

def alibi_slopes(n):
    return 2.0 ** (-8.0 * jnp.arange(1, n + 1, dtype=jnp.float32) / n)

def sliding_window_sink_attention(q, k, v, sinks, slopes):
    B, T = q.shape[:2]
    NC = T // CHUNK
    W = WINDOW_CHUNKS
    qc = q.reshape(B, NC, CHUNK, A_KV_HEADS, A_GROUP, HEAD_DIM)

    def band(t):
        tc = t.reshape(B, NC, CHUNK, A_KV_HEADS, HEAD_DIM)
        tp = jnp.pad(tc, ((0, 0), (W - 1, 0), (0, 0), (0, 0), (0, 0)))
        return jnp.concatenate([tp[:, i:i + NC] for i in range(W)], axis=2)

    kb, vb = band(k), band(v)
    logits = jnp.einsum('bnqgrd,bnkgd->bngrqk', qc, kb).astype(jnp.float32) * (HEAD_DIM ** -0.5)
    qi = jnp.arange(CHUNK)
    kj = jnp.arange(W * CHUNK)
    dist = jnp.abs((W - 1) * CHUNK + qi[:, None] - kj[None, :]).astype(jnp.float32)
    logits = logits - slopes.reshape(A_KV_HEADS, A_GROUP)[:, :, None, None] * dist
    valid = (jnp.arange(NC)[:, None] * CHUNK + kj[None, :]) >= (W - 1) * CHUNK
    logits = jnp.where(valid[None, :, None, None, None, :], logits, -jnp.inf)
    sink = sinks.astype(jnp.float32).reshape(A_KV_HEADS, A_GROUP)[None, None, :, :, None, None]
    m = jnp.maximum(jnp.max(logits, axis=-1, keepdims=True), sink)
    p = jnp.exp(logits - m)
    denom = jnp.sum(p, axis=-1, keepdims=True) + jnp.exp(sink - m)
    probs = (p / denom).astype(v.dtype)
    out = jnp.einsum('bngrqk,bnkgd->bnqgrd', probs, vb)
    return out.reshape(B, T, A_HEADS * HEAD_DIM)

def dsa_sparse_attention(q, k, v, q_idx, k_idx, w_idx, slopes):
    B, T = q.shape[:2]
    L = T
    topk = min(TOPK_MAX, L // 4)
    nb = T // B_QBLOCK
    key_pos = jnp.arange(T)

    def to_blocks(a):
        return jnp.moveaxis(a.reshape(B, nb, B_QBLOCK, *a.shape[2:]), 1, 0)

    def block(args):
        blk, qb, qib, wb = args
        t_pos = blk * B_QBLOCK + jnp.arange(B_QBLOCK)
        chunk_end = (t_pos // CHUNK + 1) * CHUNK
        visible = key_pos[None, :] < chunk_end[:, None]
        dots = jax.nn.relu(jnp.einsum('bqhd,bsd->bqhs', qib, k_idx).astype(jnp.float32))
        score = jnp.einsum('bqh,bqhs->bqs', wb.astype(jnp.float32), dots)
        score = jnp.where(visible[None], score, -jnp.inf)
        _, idx = lax.top_k(score, topk)
        sel_valid = idx < chunk_end[None, :, None]
        kg = jax.vmap(lambda kk, ii: kk[ii])(k, idx)
        vg = jax.vmap(lambda vv, ii: vv[ii])(v, idx)
        logits = jnp.einsum('bqhd,bqkd->bhqk', qb, kg).astype(jnp.float32) * (HEAD_DIM ** -0.5)
        dist = jnp.abs(t_pos[None, :, None] - idx).astype(jnp.float32)
        logits = logits - slopes[None, :, None, None] * dist[:, None]
        logits = jnp.where(sel_valid[:, None], logits, -jnp.inf)
        probs = jax.nn.softmax(logits, axis=-1).astype(v.dtype)
        return jnp.einsum('bhqk,bqkd->bqhd', probs, vg)

    out = lax.map(block, (jnp.arange(nb), to_blocks(q), to_blocks(q_idx), to_blocks(w_idx)))
    return jnp.moveaxis(out, 0, 1).reshape(B, T, B_HEADS * HEAD_DIM)

def setup_inputs(seed: int = 0) -> dict:
    key = jax.random.key(seed)
    ks = jax.random.split(key, 20)
    f32 = jnp.float32

    def nrm(k, shape, scale):
        return jax.random.normal(k, shape, f32) * scale

    def gain(k, n):
        return 1.0 + 0.05 * jax.random.normal(k, (DEPTH, n), f32)

    return {
        "x": jax.random.normal(ks[0], (BATCH, SEQ, D_MODEL), f32),
        "c": jax.random.normal(ks[1], (BATCH, D_MODEL), f32),
        "w_ada": nrm(ks[2], (DEPTH, D_MODEL, 6 * D_MODEL), 0.5 * D_MODEL ** -0.5),
        "b_ada": nrm(ks[3], (DEPTH, 6 * D_MODEL), 0.01),
        "g_pre_mix": gain(ks[4], D_MODEL),
        "g_post_mix": gain(ks[5], D_MODEL),
        "w_in": nrm(ks[6], (DEPTH, D_MODEL, D_IN), D_MODEL ** -0.5),
        "q_norm_g": gain(ks[7], Q_RANK),
        "kv_norm_g": gain(ks[8], KV_RANK),
        "w_uq": nrm(ks[9], (DEPTH, Q_RANK, B_HEADS * HEAD_DIM), Q_RANK ** -0.5),
        "w_qidx": nrm(ks[10], (DEPTH, Q_RANK, IDX_HEADS * IDX_DIM), Q_RANK ** -0.5),
        "w_ukv": nrm(ks[11], (DEPTH, KV_RANK, 2 * HEAD_DIM), KV_RANK ** -0.5),
        "a_sinks": nrm(ks[12], (DEPTH, A_HEADS), 0.5),
        "w_o": nrm(ks[13], (DEPTH, D_MIX, D_MODEL), D_MIX ** -0.5),
        "g_pre_ffn": gain(ks[14], D_MODEL),
        "g_post_ffn": gain(ks[15], D_MODEL),
        "w_gate_up": nrm(ks[16], (DEPTH, D_MODEL, 2 * D_FF), D_MODEL ** -0.5),
        "w_down": nrm(ks[17], (DEPTH, D_FF, D_MODEL), D_FF ** -0.5),
    }

def reference(x, c, w_ada, b_ada, g_pre_mix, g_post_mix, w_in, q_norm_g, kv_norm_g,
              w_uq, w_qidx, w_ukv, a_sinks, w_o, g_pre_ffn, g_post_ffn, w_gate_up, w_down):
    B, T, _ = x.shape
    slopes_a = alibi_slopes(A_HEADS)
    slopes_b = alibi_slopes(B_HEADS)
    split_points = np.cumsum(IN_SIZES)[:-1]
    c_act = jax.nn.silu(c)
    for l in range(DEPTH):
        mod = c_act @ w_ada[l] + b_ada[l]
        sh1, sc1, gt1, sh2, sc2, gt2 = [m[:, None, :] for m in jnp.split(mod, 6, axis=-1)]

        h = rms_norm(x, g_pre_mix[l]) * (1.0 + sc1) + sh1
        proj = h @ w_in[l]
        qa, ka, va, cq, ckv, kidx, widx = jnp.split(proj, split_points, axis=-1)
        qa = qa.reshape(B, T, A_HEADS, HEAD_DIM)
        ka = ka.reshape(B, T, A_KV_HEADS, HEAD_DIM)
        va = va.reshape(B, T, A_KV_HEADS, HEAD_DIM)
        out_a = sliding_window_sink_attention(qa, ka, va, a_sinks[l], slopes_a)

        cq = rms_norm(cq, q_norm_g[l])
        qb = (cq @ w_uq[l]).reshape(B, T, B_HEADS, HEAD_DIM)
        qidx = (cq @ w_qidx[l]).reshape(B, T, IDX_HEADS, IDX_DIM)
        kvb = rms_norm(ckv, kv_norm_g[l]) @ w_ukv[l]
        kb, vb = kvb[..., :HEAD_DIM], kvb[..., HEAD_DIM:]
        widx = widx * (IDX_HEADS ** -0.5 * IDX_DIM ** -0.5)
        out_b = dsa_sparse_attention(qb, kb, vb, qidx, kidx, widx, slopes_b)

        mix = jnp.concatenate([out_a, out_b], axis=-1) @ w_o[l]
        x = x + gt1 * rms_norm(mix, g_post_mix[l])

        h2 = rms_norm(x, g_pre_ffn[l]) * (1.0 + sc2) + sh2
        gate, up = jnp.split(h2 @ w_gate_up[l], 2, axis=-1)
        f = (jax.nn.silu(gate) * up) @ w_down[l]
        x = x + gt2 * rms_norm(f, g_post_ffn[l])
    return x


_drawn_inputs = setup_inputs


def setup_inputs(seed=0):
    import zlib

    import numpy as np

    out = dict(_drawn_inputs(seed))
    spreads = {}
    factors = {'g_post_mix': 3.341,
     'kv_norm_g': 4.01,
     'a_sinks': 8.0,
     'g_pre_ffn': 3.076,
     'g_post_ffn': 3.94}
    for name, (base, spread) in spreads.items():
        noise = np.random.default_rng([zlib.crc32(name.encode()), seed]).standard_normal(out[name].shape)
        drawn = base * np.exp(spread * noise) if base else spread * noise
        out[name] = __import__('jax').numpy.asarray(drawn.astype(out[name].dtype))
    for name, factor in factors.items():
        out[name] = (out[name] * factor).astype(out[name].dtype)
    return out
```

```python
from contextlib import ExitStack

import concourse.bass as bass
from concourse import mybir

F32 = mybir.dt.float32
F32R = mybir.dt.float32r
BF16 = mybir.dt.bfloat16
F16 = mybir.dt.float16
I32 = mybir.dt.int32
ALU = mybir.AluOpType
ACT = mybir.ActivationFunctionType
AX = mybir.AxisListType

P = 128
D = 1024
T = 2048
KD = D // P
CHUNK = 64
HD = 64
HEADS = 8
A_KV = 2
Q_RANK = 256
KV_RANK = 128
IDX_HEADS = 4
TOPK = 256
D_FF = 2816
KF = D_FF // P
D_IN = 1220
NB = T // P
EPS = 1e-6
SCALE = HD ** -0.5
IDX_SCALE = IDX_HEADS ** -0.5 * HD ** -0.5
BIG = 2.0 ** 100
LOWEST = -3.0e38
C_KA, C_VA, C_CQ, C_CKV, C_KI, C_WI = 512, 640, 768, 1024, 1152, 1216
BANK = 512
SLOPES = [2.0 ** (-8.0 * (h + 1) / HEADS) for h in range(HEADS)]
TOK = 512
NCHUNK = T // TOK
TPC = TOK // P


def modulation(nc, w):
    with ExitStack() as ctx:
        def sb(name, shape, dt=F32):
            return ctx.enter_context(nc.sbuf_tensor(name, shape, dt))

        def sem(name):
            return ctx.enter_context(nc.semaphore(name))

        NCH = 6 * D // BANK
        ccol = sb("ccol", [P, KD])
        cth = sb("cth", [P, KD])
        chalf = sb("chalf", [P, KD])
        cact = sb("cact", [P, KD])
        ones = sb("ones_mod", [P, P])
        cwide = sb("cwide", [P, KD, P])
        wada = sb("wada", [P, 2, KD, BANK])
        brow = sb("brow", [P, 6 * D])
        gains = sb("gains", [P, 4, D])
        mod = sb("mod", [P, 6 * D])
        out = sb("modout", [P, 6, D])
        ps = ctx.enter_context(nc.psum_tensor("mod_ps", [P, 2, BANK], F32))
        small_in = sem("mod_small_in")
        wada_in = [sem("wada_in0"), sem("wada_in1")]
        c_tanh = sem("c_tanh")
        c_steps = sem("c_steps")
        wide = sem("c_wide")
        prod = sem("mod_prod")
        summed = sem("mod_summed")
        scaled = sem("mod_scaled")
        stored = sem("mod_stored")
        block = ctx.enter_context(nc.Block())

        @block.sync
        def _(sp):
            with nc.allow_non_contiguous_dma(reason="c as one column per 128 channels: 4 KB"):
                sp.dma_start(ccol[:], w["c"].rearrange("a (k p) -> (a p) k", p=P)).then_inc(small_in, 16)
            sp.dma_start(brow[:], w["b_ada"].partition_broadcast(P)).then_inc(small_in, 16)
            for i, g in enumerate(("g_pre_mix", "g_post_mix", "g_pre_ffn", "g_post_ffn")):
                sp.dma_start(gains[:, i, :], w[g].partition_broadcast(P)).then_inc(small_in, 16)
            wa = w["w_ada"].rearrange("(k p) n -> p k n", p=P)
            for n in range(NCH):
                if n >= 2:
                    sp.wait_ge(prod, n - 1)
                sp.dma_start(wada[:, n % 2], wa[:, :, n * BANK:(n + 1) * BANK]).then_inc(wada_in[n % 2], 16)
            sp.wait_ge(scaled, 6)
            sp.dma_start(w["mods"].rearrange("a (p n) -> p a n", p=1), out[0:1, :, :]).then_inc(stored, 16)
            sp.wait_ge(stored, 16)

        @block.scalar
        def _(act):
            act.wait_ge(small_in, 96)
            nc.scalar.activation(cth[:], ccol[:], ACT.Tanh, scale=0.5).then_inc(c_tanh, 1)

        @block.vector
        def _(dve):
            nc.vector.memset(ones[:], 1.0).then_inc(c_steps, 1)
            dve.wait_ge(small_in, 96)
            nc.vector.tensor_scalar(chalf[:], ccol[:], 0.5, None, ALU.mult).then_inc(c_steps, 1)
            dve.wait_ge(c_steps, 2)
            dve.wait_ge(c_tanh, 1)
            nc.vector.scalar_tensor_tensor(cact[:], cth[:], 1.0, chalf[:], ALU.add, ALU.mult).then_inc(c_steps, 1)
            dve.wait_ge(c_steps, 3)
            for k in range(KD):
                nc.vector.tensor_scalar(cwide[:, k, :], ones[:], cact[:, k:k + 1], None, ALU.mult).then_inc(wide, 1)
            for n in range(NCH):
                dve.wait_ge(prod, n + 1)
                nc.vector.tensor_tensor(mod[:, n * BANK:(n + 1) * BANK], ps[:, n % 2, :],
                                        brow[:, n * BANK:(n + 1) * BANK], ALU.add).then_inc(summed, 1)
            dve.wait_ge(summed, NCH)
            for half in range(2):
                sh, sc, gt = (mod[:, (3 * half + i) * D:(3 * half + i + 1) * D] for i in range(3))
                nc.vector.scalar_tensor_tensor(out[:, 3 * half, :], sc, 1.0, gains[:, 2 * half, :],
                                               ALU.add, ALU.mult).then_inc(scaled, 1)
                nc.vector.tensor_copy(out[:, 3 * half + 1, :], sh).then_inc(scaled, 1)
                nc.vector.tensor_tensor(out[:, 3 * half + 2, :], gt, gains[:, 2 * half + 1, :],
                                        ALU.mult).then_inc(scaled, 1)

        @block.tensor
        def _(pe):
            pe.wait_ge(wide, KD)
            for n in range(NCH):
                pe.wait_ge(wada_in[n % 2], 16 * (n // 2 + 1))
                if n >= 2:
                    pe.wait_ge(summed, n - 1)
                for k in range(KD):
                    mm = nc.tensor.matmul(ps[:, n % 2, :], cwide[:, k, :], wada[:, n % 2, k, :],
                                          start=(k == 0), stop=(k == KD - 1))
                mm.then_inc(prod, 1)



def mixing_steps():
    steps = [(s, b) for b in range(2) for s in ("norm", "proj", "latent")]
    steps += [("head", "A", 0, h) for h in range(HEADS)]
    for b in range(NB):
        nxt = b + 1 < NB
        chosen = nxt and P * (b + 2) > TOPK
        if chosen:
            steps.append(("scores", b + 1))
        for h in range(HEADS):
            if chosen:
                steps.append(("select", b + 1, range(4 * h, 4 * h + 4)))
            steps.append(("head", "B", b, h))
            if nxt:
                steps.append(("head", "A", b + 1, h))
            if h in FRONT and b + 2 < NB:
                steps.append((FRONT[h], b + 2))
        if chosen:
            steps.append(("ties", b + 1))
    return steps


def key_tiles(kind, b):
    if kind == "B":
        return list(range(b + 1))
    return [b - 1, b] if b else [0]


def key_chunks(kind, b):
    cols = P * len(key_tiles(kind, b))
    return [(o, min(BANK, cols - o)) for o in range(0, cols, BANK)]


class Plan:

    def __init__(self):
        self.steps = mixing_steps()
        self.heads = [s[1:] for s in self.steps if s[0] == "head"]
        self.head_no = {h: i for i, h in enumerate(self.heads)}
        self.chunk0, self.group0 = [], []
        m = t = 0
        for kind, b, h in self.heads:
            self.chunk0.append(m)
            self.group0.append(t)
            m += len(key_chunks(kind, b))
            t += -(-len(key_tiles(kind, b)) // 4)
        self.chunk0.append(m)
        self.group0.append(t)
        self.work0, self.score0 = {}, {}
        u = r = 0
        for s in self.steps:
            if s[0] in PROJ_USES:
                self.work0[s] = u
                u += PROJ_USES[s[0]]
            elif s[0] == "scores":
                self.work0["s", s[1]] = u
                self.score0[s[1]] = r
                n = IDX_HEADS * len(key_chunks("B", s[1]))
                u += n
                r += n

    def last_piece(self, kind, b):
        return self.chunk0[self.head_no[kind, b, HEADS - 1] + 1]


FRONT = {0: "norm", 2: "proj", 4: "latent"}
PROJ_USES = {"proj": 5, "latent": 5}


def mixing(nc, w):
    plan = Plan()
    with ExitStack() as ctx:
        def sb(name, shape, dt=F32):
            return ctx.enter_context(nc.sbuf_tensor(name, shape, dt))

        def psum(name, shape):
            return ctx.enter_context(nc.psum_tensor(name, shape, F32))

        def sem(name):
            return ctx.enter_context(nc.semaphore(name))

        w_in = sb("w_in", [P, KD, D_IN])
        w_uq = sb("w_uq", [P, Q_RANK // P, HEADS * HD])
        w_qi = sb("w_qi", [P, Q_RANK // P, IDX_HEADS * HD])
        w_uk2 = sb("w_uk2", [P, 2 * HD])
        w_uv = sb("w_uv", [P, HD])
        pre = sb("pre", [P, 2, D])
        gq = sb("gq", [P, Q_RANK])
        gkv = sb("gkv", [P, KV_RANK])
        sink = sb("sink", [P, HEADS])
        ident = sb("ident", [P, P])
        slope_id = sb("slope_id", [P, HEADS, P], F32R)
        neg_half = sb("neg_half", [P, 1])
        ndist = sb("ndist", [P, T], F16)
        bias_a = sb("bias_a", [P, 2 * P], F32R)
        bias_v = sb("bias_v", [P, 2 * P], F32R)
        bias_b = sb("bias_b", [P, T], F32R)
        ka = sb("ka", [P, A_KV, 4, P])
        va = sb("va", [P, 4, P])
        ki = sb("ki", [P, T])
        kb = sb("kb", [P, T])
        vb = sb("vb", [P, NB, HD])
        x_in = sb("x_in", [P, D])
        h_tok = sb("h_tok", [P, D])
        h_T = sb("h_T", [P, KD, P])
        pj = sb("pj", [P, D_IN])
        kk = sb("kk", [P, 3, 2, HD])
        lat = sb("lat", [P, Q_RANK + KV_RANK])
        latT = sb("latT", [P, 3, P])
        qa = sb("qa", [P, 2, 4, P])
        qb = sb("qb", [P, 3, 4, P])
        qi = sb("qi", [P, 2, 2, P])
        widx = sb("widx", [P, 2, IDX_HEADS])
        sq_junk = sb("sq_junk", [P, D], BF16)
        ssq = sb("ssq", [P, 3])
        rstd = sb("rstd", [P, 3])
        relu = sb("relu", [P, 2, BANK])
        score = sb("score", [P, T])
        above = sb("above", [P, T], BF16)
        equal = sb("equal", [P, T], BF16)
        rank = sb("rank", [P, T], F16)
        cand = sb("cand", [P, 1], I32)
        reject = sb("reject", [P, 1], I32)
        count = sb("count", [P, 1])
        need = sb("need", [P, 1])
        logit = sb("logit", [P, 2, T + 4])
        prob = sb("prob", [P, 3, T + 4])
        probT = sb("probT", [P, 2, BANK])
        mx = sb("mx", [P, 2, 5])
        negmax = sb("negmax", [P, 4])
        total = sb("total", [P, 4])
        rtotal = sb("rtotal", [P, 4])
        oT = sb("oT", [P, 2, 4, P])

        work = [psum("work0", [P, BANK]), psum("work1", [P, BANK])]
        lbank = [psum("lbank0", [P, BANK]), psum("lbank1", [P, BANK])]
        tbank = [psum("tbank0", [P, BANK]), psum("tbank1", [P, BANK])]
        obank = {"A": psum("obank_a", [P, 4, P]), "B": psum("obank_b", [P, 4, P])}

        weights_in = sem("weights_in")
        dist_made = sem("dist_made")
        consts = sem("consts")
        x_loaded = sem("x_loaded")
        x_ssq = sem("x_ssq")
        x_rstd = sem("x_rstd")
        h_scaled = sem("h_scaled")
        h_ready = sem("h_ready")
        work_full = sem("work_full")
        work_free = sem("work_free")
        key_twice = sem("key_twice")
        lat_ssq = sem("lat_ssq")
        lat_rstd = sem("lat_rstd")
        lat_ready = sem("lat_ready")
        relu_used = sem("relu_used")
        piece_full = sem("piece_full")
        piece_read = sem("piece_read")
        max_ready = sem("max_ready")
        exp_done = sem("exp_done")
        total_inv = sem("total_inv")
        prob_ready = sem("prob_ready")
        pt_full = sem("pt_full")
        pt_ready = sem("pt_ready")
        pv_done = sem("pv_done")
        bias_ready = sem("bias_ready")
        o_copied = sem("o_copied")
        o_stored = [sem("o_stored_a"), sem("o_stored_b")]
        dve_step = sem("dve_step")
        pool_step = sem("pool_step")
        act_step = sem("act_step")
        block = ctx.enter_context(nc.Block())

        N_W = 11

        def queries(kind, b, h):
            t, n = (qa, 2) if kind == "A" else (qb, 3)
            lo = HD * (h % 2)
            return t[lo:lo + HD, b % n, h // 2, :]

        def bias_of(kind, b, o, n):
            if kind == "A":
                return bias_a[:, (2 * P - n if b == 0 else 0) + o:][:, 0:n]
            if b < 2:
                return bias_v[:, 2 * P - P * (b + 1) + o:][:, 0:n]
            return bias_b[:, o:o + n]

        @block.sync
        def _(sp):
            wi = w["w_in"].rearrange("(k p) n -> p k n", p=P)
            sp.dma_start(pre[:, 0, :], w["mods"][0:1, :].partition_broadcast(P)).then_inc(weights_in, 16)
            sp.dma_start(pre[:, 1, :], w["mods"][1:2, :].partition_broadcast(P)).then_inc(weights_in, 16)
            sp.dma_start(w_in[:], wi).then_inc(weights_in, 16)
            sp.dma_start(w_uq[:], w["w_uq"].rearrange("(k p) n -> p k n", p=P)).then_inc(weights_in, 16)
            sp.dma_start(w_qi[:], w["w_qidx"].rearrange("(k p) n -> p k n", p=P)).then_inc(weights_in, 16)
            for i in range(2):
                sp.dma_start(w_uk2[:, i * HD:(i + 1) * HD], w["w_ukv"][:, 0:HD]).then_inc(weights_in, 16)
            sp.dma_start(w_uv[:], w["w_ukv"][:, HD:]).then_inc(weights_in, 16)
            sp.dma_start(gq[:], w["q_norm_g"].partition_broadcast(P)).then_inc(weights_in, 16)
            sp.dma_start(gkv[:], w["kv_norm_g"].partition_broadcast(P)).then_inc(weights_in, 16)
            sp.dma_start(sink[:], w["a_sinks"].partition_broadcast(P)).then_inc(weights_in, 16)

            def load_x(b):
                if b >= 1:
                    sp.wait_ge(x_ssq, b)
                    sp.wait_ge(h_scaled, b)
                sp.dma_start(x_in[:], w["x"][b * P:(b + 1) * P, :]).then_inc(x_loaded, 16)

            for b in range(3):
                load_x(b)
            for i, (kind, b) in enumerate(OUT_ORDER):
                if kind == "B" and b + 3 < NB:
                    load_x(b + 3)
                sp.wait_ge(o_copied, i + 1)
                row0 = 0 if kind == "A" else HEADS * HD
                sp.dma_start(
                    w["mixT"][row0:row0 + HEADS * HD, b * P:(b + 1) * P].rearrange("(j p) t -> p j t", p=P),
                    oT[:, i % 2, :, :]).then_inc(o_stored[i % 2], 16)
            for i in range(2):
                sp.wait_ge(o_stored[i], 16 * NB)

        @block.gpsimd
        def _(pool):
            step = [0]

            def link(ins):
                step[0] += 1
                ins.then_inc(pool_step, 1)
                pool.wait_ge(pool_step, step[0])

            link(nc.gpsimd.memset(ident[:], 0.0))
            nc.gpsimd.affine_select(out=ident[:], in_=ident[:], compare_op=ALU.not_equal, fill=1.0, base=0,
                                    pattern=[[-1, P]], channel_multiplier=1).then_inc(dist_made, 1)
            nc.gpsimd.iota(score[:], [[-1, T]], base=T - P, channel_multiplier=1,
                           allow_small_or_imprecise_dtypes=True).then_inc(dist_made, 1)
            link(nc.gpsimd.memset(neg_half[:], -0.5))
            pool.wait_ge(weights_in, 16 * N_W)
            for s in plan.steps:
                if s[0] not in ("norm", "latent"):
                    continue
                b = s[1]
                for done, out_ready, lo, hi, scales in (
                        (x_ssq, x_rstd, 0, 1, (1.0 / D,)) if s[0] == "norm" else
                        (lat_ssq, lat_rstd, 1, 3, (1.0 / Q_RANK, 1.0 / KV_RANK)),):
                    pool.wait_ge(done, (b + 1))
                    for j, sc in zip(range(lo, hi), scales):
                        link(nc.gpsimd.tensor_scalar(rstd[:, j:j + 1], ssq[:, j:j + 1], sc, EPS,
                                                     ALU.mult, ALU.add))
                    for j in range(lo, hi):
                        ins = nc.gpsimd.tensor_tensor(rstd[:, j:j + 1], rstd[:, j:j + 1], neg_half[:], ALU.pow)
                        if j == hi - 1:
                            ins.then_inc(out_ready, 1)
                        else:
                            link(ins)
                    if lo == 0:
                        pool.wait_ge(h_scaled, b + 1)
                        nc.gpsimd.tensor_tensor(h_tok[:], h_tok[:], pre[:, 1, :], ALU.add).then_inc(h_ready, 1)

        @block.tensor
        def _(pe):
            def next_work(u):
                if u >= 2:
                    pe.wait_ge(work_free, u - 1)
                return work[u % 2]

            def proj(b):
                u = plan.work0["proj", b]
                pe.wait_ge(h_ready, b + 1)
                for half in range(2):
                    ps = next_work(u + half)
                    for j in range(4):
                        k = 4 * half + j
                        mm = nc.tensor.transpose(ps[:, j * P:(j + 1) * P], h_tok[:, k * P:(k + 1) * P], ident[:])
                    mm.then_inc(work_full, 1)
                pe.wait_ge(work_free, u + 2)
                for c in range(3):
                    ps = next_work(u + 2 + c)
                    n0, n1 = c * BANK, min((c + 1) * BANK, D_IN)
                    for k in range(KD):
                        mm = nc.tensor.matmul(ps[:, 0:n1 - n0], h_T[:, k, :], w_in[:, k, n0:n1],
                                              start=(k == 0), stop=(k == KD - 1))
                    mm.then_inc(work_full, 1)

            def latent(b):
                u = plan.work0["latent", b] - 5
                pe.wait_ge(work_free, plan.work0["proj", b] + 5)
                ps = next_work(u + 5)
                for j in range(4):
                    mm = nc.tensor.transpose(ps[:, j * P:(j + 1) * P], pj[:, j * P:(j + 1) * P], ident[:])
                mm.then_inc(work_full, 1)
                ps = next_work(u + 6)
                pe.wait_ge(key_twice, 2 * (b + 1))
                for j in range(3):
                    nc.tensor.transpose(ps[:, j * P:(j + 1) * P], kk[:, j, :, :].rearrange("p a d -> p (a d)"),
                                        ident[:])
                pe.wait_ge(lat_ready, 2 * (b + 1))
                mm = nc.tensor.transpose(ps[:, 3 * P:4 * P], lat[:, Q_RANK:], ident[:])
                mm.then_inc(work_full, 1)
                ps = next_work(u + 7)
                for j in range(2):
                    mm = nc.tensor.transpose(ps[:, j * P:(j + 1) * P], lat[:, j * P:(j + 1) * P], ident[:])
                mm.then_inc(work_full, 1)
                pe.wait_ge(work_free, u + 8)
                ps = next_work(u + 8)
                for n in range(4):
                    for k in range(2):
                        mm = nc.tensor.matmul(ps[:, n * P:(n + 1) * P], w_uq[:, k, n * P:(n + 1) * P],
                                              latT[:, k, :], start=(k == 0), stop=(k == 1))
                mm.then_inc(work_full, 1)
                ps = next_work(u + 9)
                for n in range(2):
                    for k in range(2):
                        nc.tensor.matmul(ps[:, n * P:(n + 1) * P], w_qi[:, k, n * P:(n + 1) * P],
                                         latT[:, k, :], start=(k == 0), stop=(k == 1))
                nc.tensor.matmul(ps[:, 2 * P:3 * P], w_uk2[:], latT[:, 2, :], start=True, stop=True)
                mm = nc.tensor.matmul(ps[:, 3 * P:3 * P + HD], latT[:, 2, :], w_uv[:], start=True, stop=True)
                mm.then_inc(work_full, 1)

            def scores(b):
                u = plan.work0["s", b]
                for o, n in key_chunks("B", b):
                    for h in range(IDX_HEADS):
                        ps = next_work(u)
                        lo = HD * (h % 2)
                        nc.tensor.matmul(ps[:, 0:n], qi[lo:lo + HD, b % 2, h // 2, :], ki[lo:lo + HD, o:o + n],
                                         start=True, stop=True).then_inc(work_full, 1)
                        u += 1

            def logits(i):
                kind, b, h = plan.heads[i]
                lo = HD * (h % 2)
                g = h // (HEADS // A_KV)
                if kind == "B" and b >= 2 and h == 0:
                    pe.wait_ge(bias_ready, b - 1)
                for c, (o, n) in enumerate(key_chunks(kind, b)):
                    m = plan.chunk0[i] + c
                    if m >= 2:
                        pe.wait_ge(piece_read, m - 1)
                    ps = lbank[m % 2]
                    if kind == "B":
                        nc.tensor.matmul(ps[:, 0:n], queries(kind, b, h), kb[lo:lo + HD, o:o + n],
                                         start=True, stop=False)
                        nc.tensor.matmul(ps[:, 0:n], slope_id[:, h, :], bias_of(kind, b, o, n),
                                         start=False, stop=True).then_inc(piece_full, 1)
                        continue
                    for j, t in enumerate(key_tiles(kind, b)):
                        nc.tensor.matmul(ps[:, j * P:(j + 1) * P], queries(kind, b, h),
                                         ka[lo:lo + HD, g, t % 4, :], start=True, stop=False)
                        mm = nc.tensor.matmul(ps[:, j * P:(j + 1) * P], slope_id[:, h, :],
                                              bias_of(kind, b, o, n)[:, j * P:(j + 1) * P],
                                              start=False, stop=True)
                    mm.then_inc(piece_full, 1)

            def weighted_values(i, g, tiles, last):
                kind, b, h = plan.heads[i]
                t = plan.group0[i] + g
                lo = HD * (h % 2)
                pe.wait_ge(pt_ready, t + 1)
                if g == 0 and h == 0:
                    if b:
                        pe.wait_ge(o_copied, OUT_ORDER.index((kind, b - 1)) + 1)
                for j, kt in enumerate(tiles):
                    v = vb[:, kt, :] if kind == "B" else va[:, kt % 4, HD * (h // 4):HD * (h // 4 + 1)]
                    mm = nc.tensor.matmul(obank[kind][lo:lo + HD, h // 2, :], v, probT[:, t % 2, j * P:(j + 1) * P],
                                          start=(g == 0 and j == 0), stop=(last and j == len(tiles) - 1))
                mm.then_inc(pv_done, 1)

            def values(i):
                kind, b, h = plan.heads[i]
                pe.wait_ge(prob_ready, i + 1)
                tiles = key_tiles(kind, b)
                groups = [tiles[j:j + 4] for j in range(0, len(tiles), 4)]
                for g, ts in enumerate(groups):
                    t = plan.group0[i] + g
                    if t >= 2:
                        pe.wait_ge(pt_ready, t - 1)
                    for j in range(len(ts)):
                        c = (4 * g + j) * P
                        mm = nc.tensor.transpose(tbank[t % 2][:, j * P:(j + 1) * P], prob[:, i % 3, c:c + P], ident[:])
                    mm.then_inc(pt_full, 1)
                    if g:
                        weighted_values(i, g - 1, groups[g - 1], False)
                weighted_values(i, len(groups) - 1, groups[-1], True)

            pe.wait_ge(weights_in, 16 * N_W)
            pe.wait_ge(dist_made, 2)
            pe.wait_ge(consts, N_CONST)
            i = 0
            for s in plan.steps:
                if s[0] == "proj":
                    proj(s[1])
                elif s[0] == "latent":
                    latent(s[1])
                elif s[0] == "scores":
                    scores(s[1])
                elif s[0] == "head":
                    logits(i)
                    if i >= 2:
                        values(i - 2)
                    i += 1
            values(i - 2)
            values(i - 1)

        @block.scalar
        def _(act):
            def copy_out(out, src, scale=1.0, last=True):
                ins = nc.scalar.activation(out, src, ACT.Copy, scale=scale)
                if last:
                    ins.then_inc(work_free, 1)
                return ins

            def norm(b):
                act.wait_ge(x_loaded, 16 * (b + 1))
                if b:
                    act.wait_ge(lat_rstd, b)
                nc.scalar.activation(sq_junk[:], x_in[:], ACT.Square, accum_out=ssq[:, 0:1]).then_inc(x_ssq, 1)

            def proj(b):
                u = plan.work0["proj", b]
                for half in range(2):
                    act.wait_ge(work_full, u + half + 1)
                    copy_out(h_T[:, 4 * half:4 * half + 4, :],
                             work[(u + half) % 2][:].rearrange("p (j t) -> p j t", j=4))
                if b:
                    act.wait_ge(lat_ready, 2 * b)
                for c in range(3):
                    act.wait_ge(work_full, u + 3 + c)
                    n0, n1 = c * BANK, min((c + 1) * BANK, D_IN)
                    copy_out(pj[:, n0:n1], work[(u + 2 + c) % 2][:, 0:n1 - n0])

            def latent(b):
                u = plan.work0["latent", b] - 5
                act.wait_ge(work_free, plan.work0["proj", b] + 5)
                act.wait_ge(x_ssq, b + 1)
                nc.scalar.activation(kk[:, 0:2, :, :],
                                     pj[:, C_KA:C_KA + P].rearrange("p (g d) -> p g d", g=2).unsqueeze(2)
                                     .to_broadcast([P, 2, 2, HD]), ACT.Copy).then_inc(key_twice, 1)
                nc.scalar.activation(kk[:, 2, :, :], pj[:, C_KI:C_KI + HD].unsqueeze(1).to_broadcast([P, 2, HD]),
                                     ACT.Copy).then_inc(key_twice, 1)
                nc.scalar.activation(sq_junk[:, 0:Q_RANK], pj[:, C_CQ:C_CQ + Q_RANK], ACT.Square,
                                     accum_out=ssq[:, 1:2]).then_inc(act_step, 1)
                act.wait_ge(act_step, b + 1)
                nc.scalar.activation(sq_junk[:, 0:KV_RANK], pj[:, C_CKV:C_CKV + KV_RANK], ACT.Square,
                                     accum_out=ssq[:, 2:3]).then_inc(lat_ssq, 1)
                if b >= 4:
                    act.wait_ge(pv_done, plan.group0[plan.head_no["A", b - 3, HEADS - 1] + 1])
                if b >= 2:
                    act.wait_ge(piece_full, plan.last_piece("A", b - 2))
                nc.scalar.activation(va[:, b % 4, :], pj[:, C_VA:C_VA + P], ACT.Copy)
                if b >= 2 and ("s", b - 2) in plan.work0:
                    act.wait_ge(relu_used, plan.score0[b - 2] + IDX_HEADS * len(key_chunks("B", b - 2)))
                nc.scalar.activation(widx[:, b % 2, :], pj[:, C_WI:C_WI + IDX_HEADS], ACT.Copy, scale=IDX_SCALE)
                act.wait_ge(work_full, u + 6)
                copy_out(qa[:, b % 2], work[(u + 5) % 2][:].rearrange("p (j t) -> p j t", j=4), SCALE)
                act.wait_ge(work_full, u + 7)
                ps = work[(u + 6) % 2]
                nc.scalar.activation(ka[:, :, b % 4, :], ps[:, 0:2 * P].rearrange("p (g t) -> p g t", g=2), ACT.Copy)
                nc.scalar.activation(ki[:, b * P:(b + 1) * P], ps[:, 2 * P:3 * P], ACT.Copy)
                copy_out(latT[:, 2, :], ps[:, 3 * P:4 * P])
                act.wait_ge(work_full, u + 8)
                copy_out(latT[:, 0:2, :], work[(u + 7) % 2][:, 0:2 * P].rearrange("p (j t) -> p j t", j=2))
                act.wait_ge(work_full, u + 9)
                if b >= 3:
                    act.wait_ge(piece_full, plan.last_piece("B", b - 3))
                copy_out(qb[:, b % 3], work[(u + 8) % 2][:].rearrange("p (j t) -> p j t", j=4), SCALE)
                act.wait_ge(work_full, u + 10)
                ps = work[(u + 9) % 2]
                nc.scalar.activation(qi[:, b % 2], ps[:, 0:2 * P].rearrange("p (j t) -> p j t", j=2), ACT.Copy)
                nc.scalar.activation(kb[:, b * P:(b + 1) * P], ps[:, 2 * P:3 * P], ACT.Copy)
                copy_out(vb[:, b, :], ps[:, 3 * P:3 * P + HD])

            def scores(b):
                u = plan.work0["s", b]
                r = plan.score0[b]
                for o, n in key_chunks("B", b):
                    for h in range(IDX_HEADS):
                        act.wait_ge(work_full, u + 1)
                        if r >= 2:
                            act.wait_ge(relu_used, r - 1)
                        nc.scalar.activation(relu[:, r % 2, 0:n], work[u % 2][:, 0:n], ACT.Relu).then_inc(work_free, 1)
                        u += 1
                        r += 1

            def exponent(i):
                kind, b, h = plan.heads[i]
                n = P * len(key_tiles(kind, b)) + (kind == "A")
                act.wait_ge(max_ready, i + 1)
                if i >= 3:
                    act.wait_ge(pt_full, plan.group0[i - 2])
                nc.scalar.activation(prob[:, i % 3, 0:n], logit[:, i % 2, 0:n], ACT.Exp,
                                     bias=negmax[:, i % 4:i % 4 + 1],
                                     accum_out=total[:, i % 4:i % 4 + 1]).then_inc(exp_done, 1)

            def normalise(i):
                kind, b, h = plan.heads[i]
                n = P * len(key_tiles(kind, b))
                act.wait_ge(total_inv, i + 1)
                nc.scalar.activation(prob[:, i % 3, 0:n], prob[:, i % 3, 0:n], ACT.Copy,
                                     scale=rtotal[:, i % 4:i % 4 + 1]).then_inc(prob_ready, 1)

            def copy_transposed(i):
                kind, b, h = plan.heads[i]
                tiles = key_tiles(kind, b)
                for g in range(-(-len(tiles) // 4)):
                    t = plan.group0[i] + g
                    n = P * min(4, len(tiles) - 4 * g)
                    act.wait_ge(pt_full, t + 1)
                    if t >= 2:
                        act.wait_ge(pv_done, t - 1)
                    nc.scalar.activation(probT[:, t % 2, 0:n], tbank[t % 2][:, 0:n], ACT.Copy).then_inc(pt_ready, 1)
                if h == HEADS - 1:
                    o = OUT_ORDER.index((kind, b))
                    act.wait_ge(pv_done, plan.group0[i + 1])
                    if o >= 2:
                        act.wait_ge(o_stored[o % 2], 16 * (o // 2))
                    nc.scalar.activation(oT[:, o % 2], obank[kind][:], ACT.Copy).then_inc(o_copied, 1)

            act.wait_ge(weights_in, 16 * N_W)
            i = 0
            for s in plan.steps:
                if s[0] == "norm":
                    norm(s[1])
                elif s[0] == "proj":
                    proj(s[1])
                elif s[0] == "latent":
                    latent(s[1])
                elif s[0] == "scores":
                    scores(s[1])
                elif s[0] == "head":
                    exponent(i)
                    if i >= 1:
                        normalise(i - 1)
                    if i >= 2:
                        copy_transposed(i - 2)
                    i += 1
            normalise(i - 1)
            copy_transposed(i - 2)
            copy_transposed(i - 1)

        @block.vector
        def _(dve):
            step = [0]

            def link(ins):
                step[0] += 1
                ins.then_inc(dve_step, 1)
                dve.wait_ge(dve_step, step[0])

            def norm(b):
                dve.wait_ge(x_rstd, b + 1)
                if b:
                    dve.wait_ge(work_full, plan.work0["proj", b - 1] + 2)
                dve.wait_ge(x_loaded, 16 * (b + 1))
                nc.vector.scalar_tensor_tensor(h_tok[:], x_in[:], rstd[:, 0:1], pre[:, 0, :],
                                               ALU.mult, ALU.mult).then_inc(h_scaled, 1)

            def latent(b):
                dve.wait_ge(work_free, plan.work0["proj", b] + 5)
                dve.wait_ge(lat_rstd, b + 1)
                nc.vector.scalar_tensor_tensor(lat[:, 0:Q_RANK], pj[:, C_CQ:C_CQ + Q_RANK], rstd[:, 1:2], gq[:],
                                               ALU.mult, ALU.mult).then_inc(lat_ready, 1)
                nc.vector.scalar_tensor_tensor(lat[:, Q_RANK:], pj[:, C_CKV:C_CKV + KV_RANK], rstd[:, 2:3], gkv[:],
                                               ALU.mult, ALU.mult).then_inc(lat_ready, 1)

            def scores(b):
                r = plan.score0[b]
                u = plan.work0["s", b]
                for o, n in key_chunks("B", b):
                    for h in range(IDX_HEADS):
                        dve.wait_ge(work_free, u + 1)
                        wh = widx[:, b % 2, h:h + 1]
                        if h == 0:
                            ins = nc.vector.tensor_scalar(score[:, o:o + n], relu[:, r % 2, 0:n], wh, None, ALU.mult)
                        else:
                            ins = nc.vector.scalar_tensor_tensor(score[:, o:o + n], relu[:, r % 2, 0:n], wh,
                                                                 score[:, o:o + n], ALU.mult, ALU.add)
                        ins.then_inc(relu_used, 1)
                        r += 1
                        u += 1
                        dve.wait_ge(relu_used, r)
                L = P * (b + 1)
                link(nc.vector.memset(score[0:CHUNK, L - CHUNK:L], LOWEST))
                link(nc.vector.memset(cand[:], 0))

            def select(b, bits):
                L = P * (b + 1)
                for j in bits:
                    link(nc.vector.tensor_scalar(above[:, 0:L], score[:, 0:L], cand[:].bitcast(F32), None,
                                                 ALU.is_ge, ALU.add, accum_out=count[:]))
                    bit = -1.0 if j == 0 else 2.0 ** (31 - j)
                    following = 0 if j == 31 else 1 << (30 - j)
                    link(nc.vector.tensor_scalar(reject[:], count[:], float(TOPK), bit, ALU.is_lt, ALU.mult))
                    link(nc.vector.scalar_tensor_tensor(cand[:], cand[:], following, reject[:],
                                                        ALU.bitwise_xor, ALU.bitwise_xor))

            def ties(b):
                L = P * (b + 1)
                thr = cand[:].bitcast(F32)
                nc.vector.tensor_scalar(equal[:, 0:L], score[:, 0:L], thr, None, ALU.is_equal)
                link(nc.vector.tensor_scalar(above[:, 0:L], score[:, 0:L], thr, None,
                                             ALU.is_gt, ALU.add, accum_out=count[:]))
                nc.vector.tensor_scalar(need[:], count[:], -1.0, float(TOPK), ALU.mult, ALU.add)
                link(nc.vector.tensor_tensor_scan(rank[:, 0:L], equal[:, 0:L], equal[:, 0:L], 0.0,
                                                  ALU.add, ALU.max))
                link(nc.vector.scalar_tensor_tensor(equal[:, 0:L], rank[:, 0:L], need[:], equal[:, 0:L],
                                                    ALU.is_le, ALU.mult))
                link(nc.vector.scalar_tensor_tensor(above[:, 0:L], above[:, 0:L], -1.0, equal[:, 0:L],
                                                    ALU.add, ALU.add))
                if b > 2:
                    dve.wait_ge(piece_full, plan.last_piece("B", b - 1))
                nc.vector.scalar_tensor_tensor(bias_b[:, 0:L], above[:, 0:L], BIG, ndist[:, T - L:],
                                               ALU.mult, ALU.add).then_inc(bias_ready, 1)

            def maximum(i):
                kind, b, h = plan.heads[i]
                chunks = key_chunks(kind, b)
                s = i % 2
                if i >= 2:
                    dve.wait_ge(exp_done, i - 1)
                for c, (o, n) in enumerate(chunks):
                    m = plan.chunk0[i] + c
                    dve.wait_ge(piece_full, m + 1)
                    nc.vector.tensor_scalar(logit[:, s, o:o + n], lbank[m % 2][:, 0:n], 1.0, None,
                                            ALU.mult, ALU.max, accum_out=mx[:, s, c:c + 1]).then_inc(piece_read, 1)
                cols = len(chunks)
                if kind == "A":
                    L = P * len(key_tiles(kind, b))
                    nc.vector.tensor_copy(logit[:, s, L:L + 1], sink[:, h:h + 1])
                    link(nc.vector.tensor_copy(mx[:, s, cols:cols + 1], sink[:, h:h + 1]))
                    cols += 1
                dve.wait_ge(piece_read, plan.chunk0[i + 1])
                nc.vector.tensor_reduce(negmax[:, i % 4:i % 4 + 1], mx[:, s, 0:cols], AX.X, ALU.max,
                                        negate=True).then_inc(max_ready, 1)
                dve.wait_ge(max_ready, i + 1)

            def invert_total(i):
                dve.wait_ge(exp_done, i + 1)
                nc.vector.reciprocal(rtotal[:, i % 4:i % 4 + 1], total[:, i % 4:i % 4 + 1]).then_inc(total_inv, 1)

            dve.wait_ge(weights_in, 16 * N_W)
            dve.wait_ge(dist_made, 2)
            link(nc.vector.tensor_scalar(logit[:, 0, 0:T], score[:], -1.0, None, ALU.mult))
            link(nc.vector.tensor_tensor(score[:], score[:], logit[:, 0, 0:T], ALU.min))
            nc.vector.tensor_copy(ndist[:], score[:]).then_inc(consts, 1)
            link(nc.vector.tensor_copy(bias_a[:], score[:, T - 2 * P:]))
            link(nc.vector.tensor_copy(bias_v[:], score[:, T - 2 * P:]))
            nc.vector.memset(bias_a[CHUNK:P, 0:P].bitcast(F32), -BIG).then_inc(consts, 1)
            nc.vector.memset(bias_a[0:CHUNK, 0:CHUNK].bitcast(F32), -BIG).then_inc(consts, 1)
            nc.vector.memset(bias_a[0:CHUNK, 2 * P - CHUNK:].bitcast(F32), -BIG).then_inc(consts, 1)
            nc.vector.memset(bias_v[0:CHUNK, 2 * P - CHUNK:].bitcast(F32), -BIG).then_inc(consts, 1)
            for h in range(HEADS):
                nc.vector.tensor_scalar(slope_id[:, h, :], ident[:], SLOPES[h], None, ALU.mult).then_inc(consts, 1)
            dve.wait_ge(consts, N_CONST)
            i = 0
            for s in plan.steps:
                if s[0] == "norm":
                    norm(s[1])
                elif s[0] == "latent":
                    latent(s[1])
                elif s[0] == "scores":
                    scores(s[1])
                elif s[0] == "select":
                    select(s[1], s[2])
                elif s[0] == "ties":
                    ties(s[1])
                elif s[0] == "head":
                    maximum(i)
                    if i >= 1:
                        invert_total(i - 1)
                    i += 1
            invert_total(i - 1)


OUT_ORDER = [("A", 0)] + [(k, b + (k == "A")) for b in range(NB) for k in "BA" if b + (k == "A") < NB]
N_CONST = 5 + HEADS


def output_and_ffn(nc, w):
    NO = D // P
    HALF = KF // 2
    PANELS = NO + 2 * KF + 2 * NO
    with ExitStack() as ctx:
        def sb(name, shape, dt=F32):
            return ctx.enter_context(nc.sbuf_tensor(name, shape, dt))

        def psum(name, shape):
            return ctx.enter_context(nc.psum_tensor(name, shape, F32))

        def sem(name):
            return ctx.enter_context(nc.semaphore(name))

        x_hi = sb("x_hi", [P, KD, TOK], F32R)
        x_lo = sb("x_lo", [P, KD, TOK], F32R)
        a_hi = sb("a_hi", [P, KF, TOK], F32R)
        a_lo = sb("a_lo", [P, KF, TOK], F32R)
        yT = sb("yT", [P, KD, TOK])
        raw = sb("raw", [P, 2, HALF, P])
        p_hi = sb("p_hi", [P, 2, HALF, P], F32R)
        p_lo = sb("p_lo", [P, 2, HALF, P], F32R)
        rows = sb("rows", [P, 4, D])
        res = sb("res", [P, D])
        cur = sb("cur", [P, D])
        ident = sb("ident3", [P, P])
        cols = sb("cols", [P, 3])
        ssq = sb("ssq3", [P, 1])
        rstd = sb("rstd3", [P, 1])
        th = sb("th", [P, TOK])
        act32 = sb("act32", [P, TOK])

        gbank = psum("gbank", [P, TOK])
        ubank = psum("ubank", [P, TOK])
        ybank = [psum("ybank0", [P, TOK]), psum("ybank1", [P, TOK])]
        tbank = [psum("tb0", [P, KD, P]), psum("tb1", [P, KD, P])]

        consts = sem("f_consts")
        rows_in = sem("rows_in")
        mix_in = sem("mix_in")
        x_split = sem("x_split")
        x_high = sem("x_high")
        raw_in = [sem("raw_in0"), sem("raw_in1")]
        raw_given = sem("raw_given")
        panel_used = sem("panel_used")
        panel_high = sem("panel_high")
        panel_ready = sem("panel_ready")
        y_given = sem("y_given")
        tanh_done = sem("tanh_done")
        gated = sem("gated")
        act_made = sem("act_made")
        act_high = sem("act_high")
        act_ready = sem("act_ready")
        t_full = sem("t_full")
        res_in = sem("res_in")
        res_read = sem("res_read")
        sq_done = sem("sq_done")
        root_done = sem("root_done")
        cur_step = sem("cur_step")
        stored = sem("stored")
        pool_step = sem("f_pool_step")
        block = ctx.enter_context(nc.Block())

        NORMS = 3 * TPC

        def used(engine, c, number):
            engine.wait_ge(panel_used, c * PANELS + number + 3)


        @block.sync
        def _(sp):
            nc.sync.sem_inc(stored, 16)
            for i, r in enumerate((2, 3, 4, 5)):
                sp.dma_start(rows[:, i, :], w["mods"][r:r + 1, :].partition_broadcast(P)).then_inc(rows_in, 16)
            wo = w["w_o"].rearrange("(k p) n -> p k n", p=P)
            wgu = w["w_gate_up"].rearrange("(k p) n -> p k n", p=P)
            wd = w["w_down"].rearrange("(s k p) n -> s p k n", p=P, s=2)

            def panel(slot, c, number, kt, src):
                sp.wait_ge(raw_given, c * PANELS + number + 1)
                sp.dma_start(raw[:, slot, 0:kt, :], src).then_inc(raw_in[slot], 16)

            def residual(c, t, phase, src):
                sp.wait_ge(res_read, 1 + (c * 2 + phase) * TPC + t)
                sp.dma_start(res[:], src).then_inc(res_in, 16)

            def store(c, t, phase, dst):
                sp.wait_ge(cur_step, 1 + c * STEPS_C + (STEPS_1 * t + 2 if phase == 0 else STEPS_1 * TPC + STEPS_2 * (t + 1)))
                sp.dma_start(dst, cur[:]).then_inc(stored, 16)

            with sp.Fori(0, NCHUNK) as c:
                sp.wait_ge(t_full, 1 + c * 3 * TPC)
                sp.dma_start(yT[:], w["mixT"].rearrange("(k p) t -> p k t", p=P)[:, :, bass.ts(c, TOK)]
                             ).then_inc(mix_in, 16)
                with sp.Fori(0, NO // 2) as j:
                    for s in range(2):
                        panel(s, c, j * 2 + s, KD, wo[:, :, bass.ts(j * 2 + s, P)])
                panel(0, c, NO, KD, wgu[:, :, 0:P])
                panel(1, c, NO + 1, KD, wgu[:, :, D_FF:D_FF + P])
                for t in range(TPC):
                    residual(c, t, 0, w["x"][bass.ds(c * TOK + t * P, P), :])
                    store(c, t, 0, w["x1"][bass.ds(c * TOK + t * P, P), :])
                with sp.Fori(1, KF) as j:
                    panel(0, c, NO + j * 2, KD, wgu[:, :, bass.ts(j, P)])
                    panel(1, c, NO + j * 2 + 1, KD, wgu[:, :, bass.ds(j * P + D_FF, P)])
                with sp.Fori(0, NO) as j:
                    for s in range(2):
                        panel(s, c, NO + 2 * KF + j * 2 + s, HALF, wd[s][:, :, bass.ts(j, P)])
                sp.wait_ge(stored, 16 + c * (16 * 2 * TPC) + 16 * TPC)
                for t in range(TPC):
                    residual(c, t, 1, w["x1"][bass.ds(c * TOK + t * P, P), :])
                    store(c, t, 1, w["out"][bass.ds(c * TOK + t * P, P), :])
            sp.wait_ge(stored, 16 + 16 * 2 * TPC * NCHUNK)

        @block.gpsimd
        def _(pool):
            nc.gpsimd.memset(ident[:], 0.0).then_inc(pool_step, 1)
            for j, v in enumerate((-0.5, 1.0 / D, EPS)):
                nc.gpsimd.memset(cols[:, j:j + 1], v).then_inc(pool_step, 1)
            pool.wait_ge(pool_step, 4)
            nc.gpsimd.affine_select(out=ident[:], in_=ident[:], compare_op=ALU.not_equal, fill=1.0, base=0,
                                    pattern=[[-1, P]], channel_multiplier=1).then_inc(consts, 1)
            with pool.Fori(0, NCHUNK * NORMS) as n:
                pool.wait_ge(sq_done, n + 1)
                nc.gpsimd.tensor_tensor(rstd[:], ssq[:], cols[:, 1:2], ALU.mult).then_inc(pool_step, 1)
                pool.wait_ge(pool_step, 2 * n + 5)
                nc.gpsimd.tensor_tensor(rstd[:], rstd[:], cols[:, 2:3], ALU.add).then_inc(pool_step, 1)
                pool.wait_ge(pool_step, 2 * n + 6)
                nc.gpsimd.tensor_tensor(rstd[:], rstd[:], cols[:, 0:1], ALU.pow).then_inc(root_done, 1)

        @block.tensor
        def _(pe):
            def product(bank, slot, kt, hi, lo, k0, first, last):
                for k in range(kt):
                    rh, rl = hi[:, k0 + k, :], lo[:, k0 + k, :]
                    wh, wl = p_hi[:, slot, k, :], p_lo[:, slot, k, :]
                    nc.tensor.matmul(bank[:], wh, rh, start=(first and k == 0), stop=False)
                    nc.tensor.matmul(bank[:], wh, rl, start=False, stop=False)
                    mm = nc.tensor.matmul(bank[:], wl, rh, start=False, stop=(last and k == kt - 1))
                return mm.then_inc(panel_used, 1)

            def panel_wait(c, number):
                pe.wait_ge(panel_ready, c * PANELS + number + 1)

            def tokens_first(c, t, order):
                for k in range(KD):
                    mm = nc.tensor.transpose(tbank[t % 2][:, k, :], yT[:, k, t * P:(t + 1) * P], ident[:])
                mm.then_inc(t_full, 1)

            pe.wait_ge(consts, 1)
            nc.tensor.sem_inc(panel_used, 2)
            nc.tensor.sem_inc(t_full, 1)
            with pe.Fori(0, NCHUNK) as c:
                with pe.Fori(0, NO // 2) as j:
                    pe.wait_ge(x_split, c * (2 + TPC) + 2)
                    for s in range(2):
                        panel_wait(c, j * 2 + s)
                        pe.wait_ge(y_given, c * 2 * NO + j * 2 + s + 1)
                        product(ybank[s], s, KD, x_hi, x_lo, 0, True, True)
                pe.wait_ge(y_given, c * 2 * NO + NO + 2)
                for t in range(TPC):
                    pe.wait_ge(x_split, c * (2 + TPC) + 2 + t)
                    pe.wait_ge(cur_step, 1 + c * STEPS_C + STEPS_1 * t)
                    tokens_first(c, t, t)
                    pe.wait_ge(cur_step, 1 + c * STEPS_C + STEPS_1 * (t + 1))
                    for k in range(KD):
                        mm = nc.tensor.transpose(tbank[(t + 1) % 2][:, k, :], cur[:, k * P:(k + 1) * P], ident[:])
                    mm.then_inc(t_full, 1)
                with pe.Fori(0, KF) as j:
                    pe.wait_ge(x_split, (c + 1) * (2 + TPC))
                    panel_wait(c, NO + j * 2)
                    pe.wait_ge(gated, 1 + c * KF + j)
                    product(gbank, 0, KD, x_hi, x_lo, 0, True, True)
                    panel_wait(c, NO + j * 2 + 1)
                    pe.wait_ge(act_made, 1 + c * KF + j)
                    product(ubank, 1, KD, x_hi, x_lo, 0, True, True)
                with pe.Fori(0, NO // 2) as j:
                    pe.wait_ge(act_ready, 1 + (c + 1) * KF)
                    for s in range(2):
                        for half in range(2):
                            panel_wait(c, NO + 2 * KF + j * 4 + 2 * s + half)
                            if half == 0:
                                pe.wait_ge(y_given, c * 2 * NO + NO + j * 2 + s + 1)
                            product(ybank[s], half, HALF, a_hi, a_lo, half * HALF, half == 0, half == 1)
                pe.wait_ge(y_given, (c + 1) * 2 * NO + 2)
                for t in range(TPC):
                    pe.wait_ge(cur_step, 1 + c * STEPS_C + STEPS_1 * TPC + STEPS_2 * t)
                    tokens_first(c, t, t)

        @block.scalar
        def _(act):
            def high_part(c, number, slot, kt, seen):
                act.wait_ge(raw_in[slot], 16 * seen)
                act.wait_ge(panel_used, c * PANELS + number + 1)
                nc.scalar.activation(p_hi[:, slot, 0:kt, :], raw[:, slot, 0:kt, :], ACT.Copy).then_inc(panel_high, 1)

            def empty_y(c, last_panel, out, s):
                used(act, c, last_panel)
                nc.scalar.activation(out, ybank[s][:], ACT.Copy).then_inc(y_given, 1)

            def square(src):
                nc.scalar.activation(sq_out, src, ACT.Square, accum_out=ssq[:]).then_inc(sq_done, 1)

            sq_out = th[:].bitcast(BF16)
            nc.scalar.sem_inc(y_given, 2)
            with act.Fori(0, NCHUNK) as c:
                act.wait_ge(mix_in, (c + 1) * 16)
                act.wait_ge(panel_used, c * PANELS + 2)
                nc.scalar.activation(x_hi[:], yT[:], ACT.Copy).then_inc(x_high, 1)
                seen = c * (PANELS // 2)

                def wo_panel(n, slot, pair):
                    high_part(c, n, slot, KD, seen + pair + 1)

                def wo_tile(n, s):
                    empty_y(c, n, yT[:, bass.ds(n, 1), :].rearrange("p a n -> p (a n)"), s)

                for s in range(2):
                    wo_panel(s, s, 0)
                act.wait_ge(x_split, c * (2 + TPC) + 2)
                with act.Fori(0, NO // 2 - 1) as j:
                    for s in range(2):
                        wo_panel(j * 2 + 2 + s, s, j + 1)
                        wo_tile(j * 2 + s, s)
                for s in range(2):
                    high_part(c, NO + s, s, KD, seen + NO // 2 + 1)
                    wo_tile(NO - 2 + s, s)
                for t in range(TPC):
                    act.wait_ge(t_full, 1 + c * 3 * TPC + 2 * t + 1)
                    square(tbank[t % 2][:].rearrange("p k t -> p (k t)"))
                    act.wait_ge(cur_step, 1 + c * STEPS_C + STEPS_1 * t + 2)
                    act.wait_ge(root_done, c * NORMS + 2 * t + 1)
                    square(cur[:])
                    act.wait_ge(t_full, 1 + c * 3 * TPC + 2 * t + 2)
                    nc.scalar.activation(x_hi[:, :, t * P:(t + 1) * P], tbank[(t + 1) % 2][:], ACT.Copy
                                         ).then_inc(x_high, 1)

                def tanh(j):
                    used(act, c, NO + 2 * j)
                    act.wait_ge(gated, 1 + c * KF + j)
                    nc.scalar.activation(th[:], gbank[:], ACT.Tanh, scale=0.5).then_inc(tanh_done, 1)

                def act_high_part(j):
                    act.wait_ge(act_made, 1 + c * KF + j + 1)
                    nc.scalar.activation(a_hi[:, bass.ds(j, 1), :].rearrange("p a n -> p (a n)"), act32[:],
                                         ACT.Copy).then_inc(act_high, 1)

                with act.Fori(0, KF - 1) as j:
                    tanh(j)
                    for s in range(2):
                        high_part(c, NO + 2 + j * 2 + s, s, KD, seen + NO // 2 + j + 2)
                    act_high_part(j)
                down0 = NO + 2 * KF
                seen_down = seen + NO // 2 + KF
                tanh(KF - 1)
                high_part(c, down0, 0, HALF, seen_down + 1)
                high_part(c, down0 + 1, 1, HALF, seen_down + 1)
                act_high_part(KF - 1)

                def down_tile(n, s):
                    empty_y(c, down0 + 2 * n + 1, yT[:, bass.ds(n, 1), :].rearrange("p a n -> p (a n)"), s)

                with act.Fori(0, NO // 2 - 1) as j:
                    for s in range(2):
                        for half in range(2):
                            high_part(c, down0 + j * 4 + 2 * s + half + 2, half, HALF, seen_down + j * 2 + s + 2)
                        down_tile(j * 2 + s, s)
                for half in range(2):
                    high_part(c, down0 + 2 * NO - 2 + half, half, HALF, seen_down + NO)
                for s in range(2):
                    down_tile(NO - 2 + s, s)
                for t in range(TPC):
                    act.wait_ge(t_full, 1 + c * 3 * TPC + 2 * TPC + t + 1)
                    if t:
                        act.wait_ge(root_done, c * NORMS + 2 * TPC + t)
                    square(tbank[t % 2][:].rearrange("p k t -> p (k t)"))

        @block.vector
        def _(dve):
            def low_part(c, number, slot, kt):
                dve.wait_ge(panel_high, c * PANELS + number + 1)
                nc.vector.tensor_tensor(p_lo[:, slot, 0:kt, :], raw[:, slot, 0:kt, :],
                                        p_hi[:, slot, 0:kt, :].bitcast(F32), ALU.subtract).then_inc(panel_ready, 1)
                dve.wait_ge(panel_ready, c * PANELS + number + 1)
                nc.vector.sem_inc(raw_given, 1)

            def scaled_rows(c, base, t, norm_no, bank, row, res_no):
                src = tbank[bank][:].rearrange("p k t -> p (k t)")
                dve.wait_ge(root_done, norm_no)
                dve.wait_ge(stored, 16 + 16 * res_no)
                nc.vector.scalar_tensor_tensor(cur[:], src, rstd[:], rows[:, row, :], ALU.mult, ALU.mult
                                               ).then_inc(cur_step, 1)
                dve.wait_ge(cur_step, 1 + base + 1)
                dve.wait_ge(res_in, 16 * (res_no + 1))
                nc.vector.tensor_tensor(cur[:], cur[:], res[:], ALU.add).then_inc(cur_step, 1)
                dve.wait_ge(cur_step, 1 + base + 2)
                nc.vector.sem_inc(res_read, 1)

            dve.wait_ge(rows_in, 64)
            nc.vector.sem_inc(raw_given, 2)
            for counter in (res_read, cur_step, gated, act_made, act_ready):
                nc.vector.sem_inc(counter, 1)
            with dve.Fori(0, NCHUNK) as c:
                dve.wait_ge(x_high, c * (1 + TPC) + 1)
                for half in range(2):
                    k0, k1 = half * KD // 2, (half + 1) * KD // 2
                    nc.vector.tensor_tensor(x_lo[:, k0:k1, :], yT[:, k0:k1, :], x_hi[:, k0:k1, :].bitcast(F32),
                                            ALU.subtract).then_inc(x_split, 1)
                with dve.Fori(0, NO // 2) as j:
                    for s in range(2):
                        low_part(c, j * 2 + s, s, KD)
                for s in range(2):
                    low_part(c, NO + s, s, KD)
                for t in range(TPC):
                    base = c * STEPS_C + STEPS_1 * t
                    scaled_rows(c, base, t, c * NORMS + 2 * t + 1, t % 2, 0, c * 2 * TPC + t)
                    dve.wait_ge(root_done, c * NORMS + 2 * t + 2)
                    dve.wait_ge(stored, 16 + 16 * (c * 2 * TPC + t + 1))
                    nc.vector.scalar_tensor_tensor(cur[:], cur[:], rstd[:], rows[:, 1, :], ALU.mult, ALU.mult
                                                   ).then_inc(cur_step, 1)
                    dve.wait_ge(cur_step, 1 + base + 3)
                    nc.vector.tensor_tensor(cur[:], cur[:], rows[:, 2, :], ALU.add).then_inc(cur_step, 1)
                    dve.wait_ge(x_high, c * (1 + TPC) + 2 + t)
                    nc.vector.tensor_tensor(x_lo[:, :, t * P:(t + 1) * P], tbank[(t + 1) % 2][:],
                                            x_hi[:, :, t * P:(t + 1) * P].bitcast(F32), ALU.subtract
                                            ).then_inc(x_split, 1)

                def gate(j):
                    dve.wait_ge(tanh_done, c * KF + j + 1)
                    dve.wait_ge(act_ready, 1 + c * KF + j)
                    nc.vector.scalar_tensor_tensor(act32[:], th[:], 1.0, gbank[:], ALU.add, ALU.mult
                                                   ).then_inc(gated, 1)

                def times_up(j):
                    dve.wait_ge(gated, 1 + c * KF + j + 1)
                    used(dve, c, NO + 2 * j + 1)
                    nc.vector.scalar_tensor_tensor(act32[:], act32[:], 0.5, ubank[:], ALU.mult, ALU.mult
                                                   ).then_inc(act_made, 1)

                def act_low_part(j):
                    dve.wait_ge(act_high, c * KF + j + 1)
                    nc.vector.tensor_tensor(a_lo[:, bass.ds(j, 1), :].rearrange("p a n -> p (a n)"), act32[:],
                                            a_hi[:, bass.ds(j, 1), :].rearrange("p a n -> p (a n)").bitcast(F32),
                                            ALU.subtract).then_inc(act_ready, 1)

                with dve.Fori(0, KF - 1) as j:
                    gate(j)
                    low_part(c, NO + 2 + j * 2, 0, KD)
                    times_up(j)
                    low_part(c, NO + 2 + j * 2 + 1, 1, KD)
                    act_low_part(j)
                gate(KF - 1)
                low_part(c, NO + 2 * KF, 0, HALF)
                times_up(KF - 1)
                low_part(c, NO + 2 * KF + 1, 1, HALF)
                act_low_part(KF - 1)
                with dve.Fori(1, NO) as j:
                    for half in range(2):
                        low_part(c, NO + 2 * KF + j * 2 + half, half, HALF)
                for t in range(TPC):
                    base = c * STEPS_C + STEPS_1 * TPC + STEPS_2 * t
                    scaled_rows(c, base, t, c * NORMS + 2 * TPC + t + 1, t % 2, 3, c * 2 * TPC + TPC + t)


STEPS_1 = 4
STEPS_2 = 2
STEPS_C = TPC * (STEPS_1 + STEPS_2)


_INS = ["x", "c", "w_ada", "b_ada", "g_pre_mix", "g_post_mix", "w_in", "q_norm_g", "kv_norm_g", "w_uq",
        "w_qidx", "w_ukv", "a_sinks", "w_o", "g_pre_ffn", "g_post_ffn", "w_gate_up", "w_down"]


def kernel(**inputs):
    import numpy as _np
    import concourse.bacc as _bacc
    from concourse import mybir as _mybir
    from concourse.bass_utils import run_bass_kernel_spmd as _run

    nc = _bacc.Bacc("TRN2", target_bir_lowering=False, num_devices=1)
    arrays, w = {}, {}
    for name in _INS:
        a = _np.ascontiguousarray(inputs[name])
        if a.ndim == 3:
            a = a[0]
        arrays[f"in_{name}"] = a
        w[name] = nc.dram_tensor(f"in_{name}", a.shape, _mybir.dt.from_np(a.dtype), kind="ExternalInput").ap()
    w["out"] = nc.dram_tensor("out_0", (T, D), F32, kind="ExternalOutput").ap()
    w["mods"] = nc.dram_tensor("mods", (6, D), F32).ap()
    w["mixT"] = nc.dram_tensor("mixT", (D, T), F32).ap()
    w["x1"] = nc.dram_tensor("x1", (T, D), F32).ap()
    modulation(nc, w)
    mixing(nc, w)
    output_and_ffn(nc, w)
    r = _run(nc, [arrays], core_ids=[0])
    return _np.reshape(r.results[0]["out_0"], (1, T, D))
```

```python
from contextlib import ExitStack

import concourse.bass as bass
from concourse import mybir

F32 = mybir.dt.float32
F32R = mybir.dt.float32r
BF16 = mybir.dt.bfloat16
F16 = mybir.dt.float16
I32 = mybir.dt.int32
ALU = mybir.AluOpType
ACT = mybir.ActivationFunctionType
AX = mybir.AxisListType

P = 128
D = 1024
T = 2048
KD = D // P
CHUNK = 64
HD = 64
HEADS = 8
A_KV = 2
Q_RANK = 256
KV_RANK = 128
IDX_HEADS = 4
TOPK = 256
D_FF = 2816
KF = D_FF // P
D_IN = 1220
NB = T // P
EPS = 1e-6
SCALE = HD ** -0.5
IDX_SCALE = IDX_HEADS ** -0.5 * HD ** -0.5
BIG = 2.0 ** 100
LOWEST = -3.0e38
C_KA, C_VA, C_CQ, C_CKV, C_KI, C_WI = 512, 640, 768, 1024, 1152, 1216
BANK = 512
SLOPES = [2.0 ** (-8.0 * (h + 1) / HEADS) for h in range(HEADS)]
TOK = 512
NCHUNK = T // TOK
TPC = TOK // P


def modulation(nc, w):
    with ExitStack() as ctx:
        def sb(name, shape, dt=F32):
            return ctx.enter_context(nc.sbuf_tensor(name, shape, dt))

        def sem(name):
            return ctx.enter_context(nc.semaphore(name))

        NCH = 6 * D // BANK
        ccol = sb("ccol", [P, KD])
        cth = sb("cth", [P, KD])
        chalf = sb("chalf", [P, KD])
        cact = sb("cact", [P, KD])
        ones = sb("ones_mod", [P, P])
        cwide = sb("cwide", [P, KD, P])
        wada = sb("wada", [P, 2, KD, BANK])
        brow = sb("brow", [P, 6 * D])
        gains = sb("gains", [P, 4, D])
        mod = sb("mod", [P, 6 * D])
        out = sb("modout", [P, 6, D])
        ps = ctx.enter_context(nc.psum_tensor("mod_ps", [P, 2, BANK], F32))
        small_in = sem("mod_small_in")
        wada_in = [sem("wada_in0"), sem("wada_in1")]
        c_tanh = sem("c_tanh")
        c_steps = sem("c_steps")
        wide = sem("c_wide")
        prod = sem("mod_prod")
        summed = sem("mod_summed")
        scaled = sem("mod_scaled")
        stored = sem("mod_stored")
        block = ctx.enter_context(nc.Block())

        @block.sync
        def _(sp):
            with nc.allow_non_contiguous_dma(reason="c as one column per 128 channels: 4 KB"):
                sp.dma_start(ccol[:], w["c"].rearrange("a (k p) -> (a p) k", p=P)).then_inc(small_in, 16)
            sp.dma_start(brow[:], w["b_ada"].partition_broadcast(P)).then_inc(small_in, 16)
            for i, g in enumerate(("g_pre_mix", "g_post_mix", "g_pre_ffn", "g_post_ffn")):
                sp.dma_start(gains[:, i, :], w[g].partition_broadcast(P)).then_inc(small_in, 16)
            wa = w["w_ada"].rearrange("(k p) n -> p k n", p=P)
            for n in range(NCH):
                if n >= 2:
                    sp.wait_ge(prod, n - 1)
                sp.dma_start(wada[:, n % 2], wa[:, :, n * BANK:(n + 1) * BANK]).then_inc(wada_in[n % 2], 16)
            sp.wait_ge(scaled, 6)
            sp.dma_start(w["mods"].rearrange("a (p n) -> p a n", p=1), out[0:1, :, :]).then_inc(stored, 16)
            sp.wait_ge(stored, 16)

        @block.scalar
        def _(act):
            act.wait_ge(small_in, 96)
            nc.scalar.activation(cth[:], ccol[:], ACT.Tanh, scale=0.5).then_inc(c_tanh, 1)

        @block.vector
        def _(dve):
            nc.vector.memset(ones[:], 1.0).then_inc(c_steps, 1)
            dve.wait_ge(small_in, 96)
            nc.vector.tensor_scalar(chalf[:], ccol[:], 0.5, None, ALU.mult).then_inc(c_steps, 1)
            dve.wait_ge(c_steps, 2)
            dve.wait_ge(c_tanh, 1)
            nc.vector.scalar_tensor_tensor(cact[:], cth[:], 1.0, chalf[:], ALU.add, ALU.mult).then_inc(c_steps, 1)
            dve.wait_ge(c_steps, 3)
            for k in range(KD):
                nc.vector.tensor_scalar(cwide[:, k, :], ones[:], cact[:, k:k + 1], None, ALU.mult).then_inc(wide, 1)
            for n in range(NCH):
                dve.wait_ge(prod, n + 1)
                nc.vector.tensor_tensor(mod[:, n * BANK:(n + 1) * BANK], ps[:, n % 2, :],
                                        brow[:, n * BANK:(n + 1) * BANK], ALU.add).then_inc(summed, 1)
            dve.wait_ge(summed, NCH)
            for half in range(2):
                sh, sc, gt = (mod[:, (3 * half + i) * D:(3 * half + i + 1) * D] for i in range(3))
                nc.vector.scalar_tensor_tensor(out[:, 3 * half, :], sc, 1.0, gains[:, 2 * half, :],
                                               ALU.add, ALU.mult).then_inc(scaled, 1)
                nc.vector.tensor_copy(out[:, 3 * half + 1, :], sh).then_inc(scaled, 1)
                nc.vector.tensor_tensor(out[:, 3 * half + 2, :], gt, gains[:, 2 * half + 1, :],
                                        ALU.mult).then_inc(scaled, 1)

        @block.tensor
        def _(pe):
            pe.wait_ge(wide, KD)
            for n in range(NCH):
                pe.wait_ge(wada_in[n % 2], 16 * (n // 2 + 1))
                if n >= 2:
                    pe.wait_ge(summed, n - 1)
                for k in range(KD):
                    mm = nc.tensor.matmul(ps[:, n % 2, :], cwide[:, k, :], wada[:, n % 2, k, :],
                                          start=(k == 0), stop=(k == KD - 1))
                mm.then_inc(prod, 1)



SEARCH = ([("whole", 0), ("shorten",)] + [("high", j) for j in range(1, 16)] + [("rebase",), ("shorten",)]
          + [("low", k) for k in range(8)] + [("last_digits",)] + [("low", k) for k in range(8, 16)]
          + [("ties", 0), ("ties", 1)])
BESIDE_A = [2, 2, 2, 2, 2, 2, 2, 2]
BESIDE_B = [3, 3, 3, 3, 3, 3, 2, 2]
assert sum(BESIDE_A) + sum(BESIDE_B) == len(SEARCH)


def mixing_steps():
    steps = ([("norm", 0), ("transposes", 0)] + [("proj", 0, c) for c in range(5)]
             + [("queries", "A", 0), ("gains", 0), ("latent", 0), ("latent_up", 0), ("norm", 1)])
    beside = set()

    def add(*side):
        steps.extend(side)
        beside.update(side)

    def front_a(b, h):
        add(*{0: [("transposes", b)], 2: [("proj", b, 0)], 3: [("proj", b, 1)], 4: [("proj", b, 2)],
              5: [("proj", b, 3)], 6: [("proj", b, 4)]}.get(h, []))

    for h in range(HEADS):
        steps.append(("head", "A", 0, h, None, range(0)))
        front_a(1, h)
    steps += [("queries", "A", 1), ("gains", 1), ("latent", 1), ("latent_up", 1), ("norm", 2)]
    for b in range(NB):
        nxt = b + 1 if b + 1 < NB else None
        chosen = nxt if nxt and P * (nxt + 1) > TOPK else None
        done = 0
        if chosen:
            steps.append(("scores", chosen))
        if not nxt:
            steps.append(("queries", "B", b))
        for h in range(HEADS if nxt else 0):
            steps.append(("head", "A", nxt, h, chosen, range(done, done + BESIDE_A[h])))
            done += BESIDE_A[h]
            if b + 2 < NB:
                front_a(b + 2, h)
            if h == 3:
                add(("queries", "B", b))
        for h in range(HEADS):
            steps.append(("head", "B", b, h, chosen, range(done, done + BESIDE_B[h])))
            done += BESIDE_B[h]
            if b + 2 < NB:
                add(*{0: [("queries", "A", b + 2), ("gains", b + 2)], 2: [("latent", b + 2)],
                      4: [("latent_up", b + 2)]}.get(h, []))
            if b + 3 < NB and h == 6:
                add(("norm", b + 3))
    return steps, beside


LAG = {"scalar": {"transposes": 1, "proj": 1, "latent": 1, "latent_up": 1, "queries": 1},
       "vector": {"norm": 1, "latent": 2, "latent_up": 2, "queries": 2}}
WORK_USES = {"transposes": lambda s: 2, "proj": lambda s: (s[2] + 1) % 2, "latent": lambda s: 2,
             "latent_up": lambda s: 1, "queries": lambda s: 1,
             "scores": lambda s: IDX_HEADS * len(key_chunks("B", s[1]))}
SPLITS = {"latent": 2, "latent_up": 3, "queries": 2}


def engine_order(engine):
    steps, beside = mixing_steps()
    out, late = [], []
    for s in steps:
        lag = LAG[engine].get(s[0], 0)
        if s in beside:
            if lag:
                late.append((lag, s))
            else:
                out.append(s)
            continue
        if s[0] != "head":
            out += [x for _, x in late]
            late = []
        out.append(s)
        late = [(n - 1, x) for n, x in late]
        out += [x for n, x in late if n == 0]
        late = [(n, x) for n, x in late if n > 0]
    return out + [x for _, x in late]


def key_tiles(kind, b):
    if kind == "B":
        return list(range(b + 1))
    return [b - 1, b] if b else [0]


def key_chunks(kind, b):
    cols = P * len(key_tiles(kind, b))
    return [(o, min(BANK, cols - o)) for o in range(0, cols, BANK)]


class Plan:

    def __init__(self):
        self.steps = mixing_steps()[0]
        self.heads = [s[1:4] for s in self.steps if s[0] == "head"]
        self.head_no = {h: i for i, h in enumerate(self.heads)}
        self.chunk0, self.group0 = [], []
        m = t = 0
        for kind, b, h in self.heads:
            self.chunk0.append(m)
            self.group0.append(t)
            m += len(key_chunks(kind, b))
            t += -(-len(key_tiles(kind, b)) // 4)
        self.chunk0.append(m)
        self.group0.append(t)
        self.work0, self.score0, self.split0 = {}, {}, {}
        u = r = v = 0
        for s in self.steps:
            if s[0] in WORK_USES:
                self.work0[s] = u
                u += WORK_USES[s[0]](s)
            if s[0] == "scores":
                self.score0[s[1]] = r
                r += IDX_HEADS * len(key_chunks("B", s[1]))
            if s[0] in SPLITS:
                self.split0[s] = v
                v += SPLITS[s[0]]

    def last_piece(self, kind, b):
        return self.chunk0[self.head_no[kind, b, HEADS - 1] + 1]

    def groups(self, i):
        tiles = key_tiles(*self.heads[i][0:2])
        return [tiles[j:j + 4] for j in range(0, len(tiles), 4)]


def mixing(nc, w):
    plan = Plan()
    with ExitStack() as ctx:
        def sb(name, shape, dt=F32):
            return ctx.enter_context(nc.sbuf_tensor(name, shape, dt))

        def psum(name, shape):
            return ctx.enter_context(nc.psum_tensor(name, shape, F32))

        def sem(name):
            return ctx.enter_context(nc.semaphore(name))

        w_in = sb("w_in", [P, KD, D_IN])
        w_uq = sb("w_uq", [P, Q_RANK // P, HEADS * HD])
        w_qi = sb("w_qi", [P, Q_RANK // P, IDX_HEADS * HD])
        w_uk2 = sb("w_uk2", [P, 2 * HD])
        w_uv = sb("w_uv", [P, HD])
        pre = sb("pre", [P, 2, D])
        gq = sb("gq", [P, Q_RANK])
        gkv = sb("gkv", [P, KV_RANK])
        sink = sb("sink", [P, HEADS])
        ident = sb("ident", [P, P])
        slope_id = sb("slope_id", [P, HEADS, P], F32R)
        neg_half = sb("neg_half", [P, 1])
        ndist = sb("ndist", [P, T], F16)
        bias_a = sb("bias_a", [P, 2 * P], F32R)
        bias_v = sb("bias_v", [P, 2 * P], F32R)
        bias_b = sb("bias_b", [P, T], F32R)
        ka = sb("ka", [P, A_KV, 4, P], F32R)
        ki = sb("ki", [P, T], F32R)
        kb = sb("kb", [P, T], F32R)
        va = sb("va", [P, 4, P])
        vb = sb("vb", [P, NB, HD])
        q_hi = {"A": sb("qa_hi", [P, HEADS, P], F32R), "B": sb("qb_hi", [P, HEADS, P], F32R)}
        q_lo = {"A": sb("qa_lo", [P, HEADS, P], F32R), "B": sb("qb_lo", [P, HEADS, P], F32R)}
        qi_hi = sb("qi_hi", [P, IDX_HEADS, P], F32R)
        qi_lo = sb("qi_lo", [P, IDX_HEADS, P], F32R)
        raw = sb("raw_heads", [P, 4, P])
        k_hi = sb("k_hi", [P, 3, P], F32R)
        x_in = sb("x_in", [P, D])
        h_T = sb("h_T", [P, KD, P])
        pj = sb("pj", [P, D_IN])
        kk = sb("kk", [P, 3, 2, HD])
        lat = sb("lat", [P, Q_RANK + KV_RANK])
        latT = sb("latT", [P, 2, 3, P])
        widx = sb("widx", [P, 2, IDX_HEADS])
        ssq = sb("ssq", [P, 3])
        rstd = sb("rstd", [P, 3])
        relu = sb("relu", [P, 2, BANK])
        score = sb("score", [P, T])
        above = sb("above", [P, T], BF16)
        equal = sb("equal", [P, T], BF16)
        rank = sb("rank", [P, T], F16)
        powers = sb("powers", [P, 17])
        digit = sb("digit", [P, 17])
        cand = sb("cand", [P, 1], I32)
        above_it = sb("above_it", [P, 1], I32)
        unit = sb("unit", [P, 1])
        reject = sb("reject", [P, 1], I32)
        count = sb("count", [P, 1])
        need = sb("need", [P, 1])
        logit = sb("logit", [P, 2, T + 4])
        prob = sb("prob", [P, 2, T + 4])
        probT = sb("probT", [P, 2, BANK])
        mx = sb("mx", [P, 2, 5])
        negmax = sb("negmax", [P, 4])
        total = sb("total", [P, 4])
        rtotal = sb("rtotal", [P, 4])
        oT = sb("oT", [P, 2, 4, P])
        squares = h_T[:].rearrange("p k t -> p (k t)")
        short = rank[:].bitcast(BF16)

        work = [psum("work0", [P, BANK]), psum("work1", [P, BANK])]
        lbank = [psum("lbank0", [P, BANK]), psum("lbank1", [P, BANK])]
        tbank = [psum("tbank0", [P, BANK]), psum("tbank1", [P, BANK])]
        obank = {"A": psum("obank_a", [P, 4, P]), "B": psum("obank_b", [P, 4, P])}

        weights_in = sem("weights_in")
        dist_made = sem("dist_made")
        consts = sem("consts")
        x_loaded = sem("x_loaded")
        x_ssq = sem("x_ssq")
        x_rstd = sem("x_rstd")
        h_scaled = sem("h_scaled")
        h_ready = sem("h_ready")
        work_full = sem("work_full")
        work_free = sem("work_free")
        key_twice = sem("key_twice")
        raw_ready = sem("raw_ready")
        split_done = sem("split_done")
        lat_ssq = sem("lat_ssq")
        lat_rstd = sem("lat_rstd")
        lat_ready = sem("lat_ready")
        relu_used = sem("relu_used")
        piece_full = sem("piece_full")
        piece_read = sem("piece_read")
        max_ready = sem("max_ready")
        exp_done = sem("exp_done")
        total_inv = sem("total_inv")
        prob_ready = sem("prob_ready")
        pt_full = sem("pt_full")
        pt_ready = sem("pt_ready")
        pv_done = sem("pv_done")
        bias_ready = sem("bias_ready")
        o_copied = sem("o_copied")
        o_stored = [sem("o_stored_a"), sem("o_stored_b")]
        dve_step = sem("dve_step")
        pool_step = sem("pool_step")
        act_step = sem("act_step")
        block = ctx.enter_context(nc.Block())

        N_W = 11

        def bias_of(kind, b, o, n):
            if kind == "A":
                return bias_a[:, (P if b == 0 else 0) + o:][:, 0:n]
            if b < 2:
                return bias_v[:, 2 * P - P * (b + 1) + o:][:, 0:n]
            return bias_b[:, o:o + n]

        @block.sync
        def _(sp):
            wi = w["w_in"].rearrange("(k p) n -> p k n", p=P)
            sp.dma_start(x_in[:], w["x"][0:P, :]).then_inc(x_loaded, 16)
            sp.dma_start(pre[:, 0, :], w["mods"][0:1, :].partition_broadcast(P)).then_inc(weights_in, 16)
            sp.dma_start(pre[:, 1, :], w["mods"][1:2, :].partition_broadcast(P)).then_inc(weights_in, 16)
            sp.dma_start(w_in[:], wi).then_inc(weights_in, 16)
            sp.dma_start(w_uq[:], w["w_uq"].rearrange("(k p) n -> p k n", p=P)).then_inc(weights_in, 16)
            sp.dma_start(w_qi[:], w["w_qidx"].rearrange("(k p) n -> p k n", p=P)).then_inc(weights_in, 16)
            for i in range(2):
                sp.dma_start(w_uk2[:, i * HD:(i + 1) * HD], w["w_ukv"][:, 0:HD]).then_inc(weights_in, 16)
            sp.dma_start(w_uv[:], w["w_ukv"][:, HD:]).then_inc(weights_in, 16)
            sp.dma_start(gq[:], w["q_norm_g"].partition_broadcast(P)).then_inc(weights_in, 16)
            sp.dma_start(gkv[:], w["kv_norm_g"].partition_broadcast(P)).then_inc(weights_in, 16)
            sp.dma_start(sink[:], w["a_sinks"].partition_broadcast(P)).then_inc(weights_in, 16)

            def load_x(b):
                sp.wait_ge(work_full, plan.work0["transposes", b - 1] + 2)
                sp.dma_start(x_in[:], w["x"][b * P:(b + 1) * P, :]).then_inc(x_loaded, 16)

            for b in (1, 2):
                load_x(b)
            for i, (kind, b) in enumerate(OUT_ORDER):
                if kind == "A" and 1 <= b and b + 2 < NB:
                    load_x(b + 2)
                sp.wait_ge(o_copied, i + 1)
                row0 = 0 if kind == "A" else HEADS * HD
                sp.dma_start(
                    w["mixT"][row0:row0 + HEADS * HD, b * P:(b + 1) * P].rearrange("(j p) t -> p j t", p=P),
                    oT[:, i % 2, :, :]).then_inc(o_stored[i % 2], 16)
            for i in range(2):
                sp.wait_ge(o_stored[i], 16 * NB)

        @block.gpsimd
        def _(pool):
            step = [0]

            def link(ins):
                step[0] += 1
                ins.then_inc(pool_step, 1)
                pool.wait_ge(pool_step, step[0])

            link(nc.gpsimd.memset(ident[:], 0.0))
            nc.gpsimd.affine_select(out=ident[:], in_=ident[:], compare_op=ALU.not_equal, fill=1.0, base=0,
                                    pattern=[[-1, P]], channel_multiplier=1).then_inc(dist_made, 1)
            nc.gpsimd.iota(score[:], [[-1, T]], base=T - P, channel_multiplier=1,
                           allow_small_or_imprecise_dtypes=True).then_inc(dist_made, 1)
            link(nc.gpsimd.memset(neg_half[:], -0.5))
            pool.wait_ge(weights_in, 16 * N_W)
            for s in plan.steps:
                if s[0] not in ("norm", "gains"):
                    continue
                b = s[1]
                if s[0] == "norm":
                    done, out_ready, jobs = x_ssq, x_rstd, ((0, D),)
                else:
                    done, out_ready, jobs = lat_ssq, lat_rstd, ((1, Q_RANK), (2, KV_RANK))
                pool.wait_ge(done, b + 1)
                for j, width in jobs:
                    link(nc.gpsimd.tensor_scalar(rstd[:, j:j + 1], ssq[:, j:j + 1], 1.0 / width, EPS,
                                                 ALU.mult, ALU.add))
                for j, width in jobs:
                    ins = nc.gpsimd.tensor_tensor(rstd[:, j:j + 1], rstd[:, j:j + 1], neg_half[:], ALU.pow)
                    if j == jobs[-1][0]:
                        ins.then_inc(out_ready, 1)
                    else:
                        link(ins)
                if s[0] == "norm":
                    pool.wait_ge(h_scaled, b + 1)
                    nc.gpsimd.tensor_tensor(x_in[:], x_in[:], pre[:, 1, :], ALU.add).then_inc(h_ready, 1)

        @block.tensor
        def _(pe):
            def next_work(u):
                if u >= 2:
                    pe.wait_ge(work_free, u - 1)
                return work[u % 2]

            def transposes(s):
                b = s[1]
                u = plan.work0[s]
                pe.wait_ge(h_ready, b + 1)
                for half in range(2):
                    ps = next_work(u)
                    for j in range(4):
                        k = 4 * half + j
                        mm = nc.tensor.transpose(ps[:, j * P:(j + 1) * P], x_in[:, k * P:(k + 1) * P], ident[:])
                    mm.then_inc(work_full, 1)
                    u += 1

            def proj(s):
                _, b, part = s
                c = part // 2
                u = plan.work0["proj", b, 2 * c]
                if part == 0:
                    pe.wait_ge(work_free, u)
                ps = next_work(u) if part % 2 == 0 else work[u % 2]
                n0, n1 = c * BANK, min((c + 1) * BANK, D_IN)
                for k in range(KD) if c == 2 else range(4 * (part % 2), 4 * (part % 2) + 4):
                    mm = nc.tensor.matmul(ps[:, 0:n1 - n0], h_T[:, k, :], w_in[:, k, n0:n1],
                                          start=(k == 0), stop=(k == KD - 1))
                if part != 0 and part != 2:
                    mm.then_inc(work_full, 1)

            def latent(s):
                b = s[1]
                u = plan.work0[s]
                pe.wait_ge(key_twice, 2 * (b + 1))
                ps = next_work(u)
                for j in range(3):
                    nc.tensor.transpose(ps[:, j * P:(j + 1) * P], kk[:, j, :, :].rearrange("p a d -> p (a d)"),
                                        ident[:])
                pe.wait_ge(lat_ready, 2 * (b + 1))
                mm = nc.tensor.transpose(ps[:, 3 * P:4 * P], lat[:, Q_RANK:], ident[:])
                mm.then_inc(work_full, 1)
                ps = next_work(u + 1)
                for j in range(2):
                    mm = nc.tensor.transpose(ps[:, j * P:(j + 1) * P], lat[:, j * P:(j + 1) * P], ident[:])
                mm.then_inc(work_full, 1)

            def latent_up(s):
                b = s[1]
                u = plan.work0[s]
                pe.wait_ge(work_free, plan.work0["latent", b] + 2)
                ps = next_work(u)
                for n in range(2):
                    for k in range(2):
                        nc.tensor.matmul(ps[:, n * P:(n + 1) * P], w_qi[:, k, n * P:(n + 1) * P],
                                         latT[:, b % 2, k, :], start=(k == 0), stop=(k == 1))
                nc.tensor.matmul(ps[:, 2 * P:3 * P], w_uk2[:], latT[:, b % 2, 2, :], start=True, stop=True)
                mm = nc.tensor.matmul(ps[:, 3 * P:3 * P + HD], latT[:, b % 2, 2, :], w_uv[:], start=True, stop=True)
                mm.then_inc(work_full, 1)

            def queries(s):
                _, kind, b = s
                u = plan.work0[s]
                ps = next_work(u)
                for n in range(4):
                    if kind == "A":
                        pe.wait_ge(work_free, plan.work0["proj", b, 0] + 1)
                        mm = nc.tensor.transpose(ps[:, n * P:(n + 1) * P], pj[:, n * P:(n + 1) * P], ident[:])
                        continue
                    for k in range(2):
                        mm = nc.tensor.matmul(ps[:, n * P:(n + 1) * P], w_uq[:, k, n * P:(n + 1) * P],
                                              latT[:, b % 2, k, :], start=(k == 0), stop=(k == 1))
                mm.then_inc(work_full, 1)

            def scores(s):
                b = s[1]
                u = plan.work0[s]
                pe.wait_ge(split_done, plan.split0["latent_up", b] + SPLITS["latent_up"])
                for o, n in key_chunks("B", b):
                    for h in range(IDX_HEADS):
                        ps = next_work(u)
                        nc.tensor.matmul(ps[:, 0:n], qi_hi[:, h, :], ki[:, o:o + n], start=True, stop=False)
                        nc.tensor.matmul(ps[:, 0:n], qi_lo[:, h, :], ki[:, o:o + n],
                                         start=False, stop=True).then_inc(work_full, 1)
                        u += 1

            def piece(i, c):
                kind, b, h = plan.heads[i]
                g = h // (HEADS // A_KV)
                if c == 0 and h == 0:
                    last = ("latent_up", b) if kind == "A" else ("queries", "B", b)
                    pe.wait_ge(split_done, plan.split0[last] + SPLITS[last[0]])
                    if kind == "B" and b >= 2:
                        pe.wait_ge(bias_ready, b - 1)
                o, n = key_chunks(kind, b)[c]
                m = plan.chunk0[i] + c
                if m >= 2:
                    pe.wait_ge(piece_read, m - 1)
                ps = lbank[m % 2]
                if kind == "B":
                    spans = [(0, n, kb[:, o:o + n])]
                else:
                    spans = [(j * P, P, ka[:, g, t % 4, :]) for j, t in enumerate(key_tiles(kind, b))]
                for at, width, keys in spans:
                    out = ps[:, at:at + width]
                    nc.tensor.matmul(out, q_hi[kind][:, h, :], keys, start=True, stop=False)
                    nc.tensor.matmul(out, q_lo[kind][:, h, :], keys, start=False, stop=False)
                    mm = nc.tensor.matmul(out, slope_id[:, h, :], bias_of(kind, b, o, n)[:, at:at + width],
                                          start=False, stop=True)
                mm.then_inc(piece_full, 1)

            def transpose_group(i, g):
                tiles = plan.groups(i)[g]
                t = plan.group0[i] + g
                if g == 0:
                    pe.wait_ge(prob_ready, i + 1)
                if t >= 2:
                    pe.wait_ge(pt_ready, t - 1)
                for j in range(len(tiles)):
                    c = (4 * g + j) * P
                    mm = nc.tensor.transpose(tbank[t % 2][:, j * P:(j + 1) * P], prob[:, i % 2, c:c + P], ident[:])
                mm.then_inc(pt_full, 1)

            def weighted_values(i, g):
                kind, b, h = plan.heads[i]
                tiles = plan.groups(i)[g]
                last = g == len(plan.groups(i)) - 1
                t = plan.group0[i] + g
                lo = HD * (h % 2)
                pe.wait_ge(pt_ready, t + 1)
                if g == 0 and h == 0 and b:
                    pe.wait_ge(o_copied, OUT_ORDER.index((kind, b - 1)) + 1)
                for j, kt in enumerate(tiles):
                    v = vb[:, kt, :] if kind == "B" else va[:, kt % 4, HD * (h // 4):HD * (h // 4 + 1)]
                    mm = nc.tensor.matmul(obank[kind][lo:lo + HD, h // 2, :], v, probT[:, t % 2, j * P:(j + 1) * P],
                                          start=(g == 0 and j == 0), stop=(last and j == len(tiles) - 1))
                mm.then_inc(pv_done, 1)

            def head(i):
                pieces = len(key_chunks(*plan.heads[i][0:2])) if i < len(plan.heads) else 0
                groups = len(plan.groups(i - 2)) if 2 <= i < len(plan.heads) + 2 else 0
                for c in range(max(pieces, groups, 1)):
                    if c < pieces:
                        piece(i, c)
                    if c < groups:
                        transpose_group(i - 2, c)
                    if c == 0 and i >= 3:
                        weighted_values(i - 3, len(plan.groups(i - 3)) - 1)
                    if 1 <= c < groups:
                        weighted_values(i - 2, c - 1)

            pe.wait_ge(weights_in, 16 * N_W)
            pe.wait_ge(dist_made, 2)
            pe.wait_ge(consts, N_CONST)
            i = 0
            for s in plan.steps:
                if s[0] == "transposes":
                    transposes(s)
                elif s[0] == "proj":
                    proj(s)
                elif s[0] == "latent":
                    latent(s)
                elif s[0] == "latent_up":
                    latent_up(s)
                elif s[0] == "queries":
                    queries(s)
                elif s[0] == "scores":
                    scores(s)
                elif s[0] == "head":
                    head(i)
                    i += 1
            for j in range(3):
                head(i + j)

        @block.scalar
        def _(act):
            def copy_out(out, src, scale=1.0):
                nc.scalar.activation(out, src, ACT.Copy, scale=scale).then_inc(work_free, 1)

            def pairs(ap):
                return ap.rearrange("p (j t) -> p j t", t=P)

            def norm(s):
                b = s[1]
                act.wait_ge(x_loaded, 16 * (b + 1))
                if b:
                    act.wait_ge(lat_rstd, b)
                    act.wait_ge(work_full, plan.work0["proj", b - 1, 4] + 1)
                nc.scalar.activation(squares, x_in[:], ACT.Square, accum_out=ssq[:, 0:1]).then_inc(x_ssq, 1)

            def transposes(s):
                u = plan.work0[s]
                for half in range(2):
                    act.wait_ge(work_full, u + half + 1)
                    copy_out(h_T[:, 4 * half:4 * half + 4, :], pairs(work[(u + half) % 2][:]))

            def proj(s):
                _, b, part = s
                if part == 0 or part == 2:
                    return
                c = part // 2
                u = plan.work0["proj", b, 2 * c]
                if c == 0:
                    if b:
                        act.wait_ge(lat_ready, 2 * b)
                        act.wait_ge(work_full, plan.work0["queries", "A", b - 1] + 1)
                act.wait_ge(work_full, u + 1)
                n0, n1 = c * BANK, min((c + 1) * BANK, D_IN)
                copy_out(pj[:, n0:n1], work[u % 2][:, 0:n1 - n0])
                if c < 2:
                    return
                act.wait_ge(work_free, u + 1)
                nc.scalar.activation(squares[:, 0:Q_RANK], pj[:, C_CQ:C_CQ + Q_RANK], ACT.Square,
                                     accum_out=ssq[:, 1:2]).then_inc(act_step, 1)
                act.wait_ge(act_step, b + 1)
                nc.scalar.activation(squares[:, 0:KV_RANK], pj[:, C_CKV:C_CKV + KV_RANK], ACT.Square,
                                     accum_out=ssq[:, 2:3]).then_inc(lat_ssq, 1)
                nc.scalar.activation(kk[:, 0:2, :, :],
                                     pj[:, C_KA:C_KA + P].rearrange("p (g d) -> p g d", g=2).unsqueeze(2)
                                     .to_broadcast([P, 2, 2, HD]), ACT.Copy).then_inc(key_twice, 1)
                nc.scalar.activation(kk[:, 2, :, :], pj[:, C_KI:C_KI + HD].unsqueeze(1).to_broadcast([P, 2, HD]),
                                     ACT.Copy).then_inc(key_twice, 1)

            def latent(s):
                b = s[1]
                u = plan.work0[s]
                v = plan.split0[s]
                if b >= 4:
                    act.wait_ge(pv_done, plan.group0[plan.head_no["A", b - 3, HEADS - 1] + 1])
                nc.scalar.activation(va[:, b % 4, :], pj[:, C_VA:C_VA + P], ACT.Copy)
                if ("scores", b - 2) in plan.work0:
                    act.wait_ge(relu_used, plan.score0[b - 2] + IDX_HEADS * len(key_chunks("B", b - 2)))
                nc.scalar.activation(widx[:, b % 2, :], pj[:, C_WI:C_WI + IDX_HEADS], ACT.Copy, scale=IDX_SCALE)
                act.wait_ge(work_full, u + 1)
                if v:
                    act.wait_ge(split_done, v)
                ps = work[u % 2]
                keys = ps[:, 0:3 * P]
                nc.scalar.activation(ka[0:HD, :, b % 4, :], pairs(keys[0:HD, 0:2 * P]), ACT.Copy)
                nc.scalar.activation(ki[0:HD, b * P:(b + 1) * P], keys[0:HD, 2 * P:], ACT.Copy)
                nc.scalar.activation(k_hi[HD:P, 0:3, :], pairs(keys[HD:P, :]), ACT.Copy)
                nc.scalar.activation(raw[HD:P, 0:3, :], pairs(keys[HD:P, :]), ACT.Copy).then_inc(raw_ready, 1)
                copy_out(latT[:, b % 2, 2, :], ps[:, 3 * P:4 * P])
                act.wait_ge(work_full, u + 2)
                copy_out(latT[:, b % 2, 0:2, :], pairs(work[(u + 1) % 2][:, 0:2 * P]))

            def latent_up(s):
                b = s[1]
                u = plan.work0[s]
                act.wait_ge(work_full, u + 1)
                ps = work[u % 2]
                act.wait_ge(split_done, plan.split0[s])
                nc.scalar.activation(kb[0:HD, b * P:(b + 1) * P], ps[0:HD, 2 * P:3 * P], ACT.Copy)
                nc.scalar.activation(k_hi[HD:P, 0, :], ps[HD:P, 2 * P:3 * P], ACT.Copy)
                nc.scalar.activation(raw[HD:P, 2, :], ps[HD:P, 2 * P:3 * P], ACT.Copy)
                high_twice(qi_hi, pairs(ps[:, 0:2 * P]), 1.0)
                nc.scalar.activation(raw[:, 0:2, :], pairs(ps[:, 0:2 * P]), ACT.Copy).then_inc(raw_ready, 1)
                copy_out(vb[:, b, :], ps[:, 3 * P:3 * P + HD])

            def high_twice(dst, src, scale):
                for r in range(2):
                    for half in range(2):
                        nc.scalar.activation(dst[half * HD:(half + 1) * HD, r::2, :], src[r * HD:(r + 1) * HD],
                                             ACT.Copy, scale=scale)

            def queries(s):
                _, kind, b = s
                u = plan.work0[s]
                act.wait_ge(work_full, u + 1)
                act.wait_ge(split_done, plan.split0[s])
                if b:
                    act.wait_ge(piece_full, plan.last_piece(kind, b - 1))
                src = pairs(work[u % 2][:])
                high_twice(q_hi[kind], src, SCALE)
                copy = nc.scalar.activation(raw[:], src, ACT.Copy, scale=SCALE)
                copy.then_inc(raw_ready, 1)
                act.wait_ge(raw_ready, RAW_COUNT[s])
                act.sem_inc(work_free, 1)

            def scores(s):
                b = s[1]
                u = plan.work0[s]
                r = plan.score0[b]
                for o, n in key_chunks("B", b):
                    for h in range(IDX_HEADS):
                        act.wait_ge(work_full, u + 1)
                        if r >= 2:
                            act.wait_ge(relu_used, r - 1)
                        nc.scalar.activation(relu[:, r % 2, 0:n], work[u % 2][:, 0:n], ACT.Relu).then_inc(work_free, 1)
                        u += 1
                        r += 1

            def exponent(i):
                kind, b, h = plan.heads[i]
                n = P * len(key_tiles(kind, b)) + (kind == "A")
                act.wait_ge(max_ready, i + 1)
                if i >= 2:
                    act.wait_ge(pt_full, plan.group0[i - 1])
                nc.scalar.activation(prob[:, i % 2, 0:n], logit[:, i % 2, 0:n], ACT.Exp,
                                     bias=negmax[:, i % 4:i % 4 + 1],
                                     accum_out=total[:, i % 4:i % 4 + 1]).then_inc(exp_done, 1)

            def normalise(i):
                kind, b, h = plan.heads[i]
                n = P * len(key_tiles(kind, b))
                act.wait_ge(total_inv, i + 1)
                nc.scalar.activation(prob[:, i % 2, 0:n], prob[:, i % 2, 0:n], ACT.Copy,
                                     scale=rtotal[:, i % 4:i % 4 + 1]).then_inc(prob_ready, 1)

            def copy_transposed(i):
                for g, tiles in enumerate(plan.groups(i)):
                    t = plan.group0[i] + g
                    n = P * len(tiles)
                    act.wait_ge(pt_full, t + 1)
                    if t >= 2:
                        act.wait_ge(pv_done, t - 1)
                    nc.scalar.activation(probT[:, t % 2, 0:n], tbank[t % 2][:, 0:n], ACT.Copy).then_inc(pt_ready, 1)

            def copy_output(i):
                kind, b, h = plan.heads[i]
                if h < HEADS - 1:
                    return
                o = OUT_ORDER.index((kind, b))
                act.wait_ge(pv_done, plan.group0[i + 1])
                if o >= 2:
                    act.wait_ge(o_stored[o % 2], 16 * (o // 2))
                nc.scalar.activation(oT[:, o % 2], obank[kind][:], ACT.Copy).then_inc(o_copied, 1)

            def head(i):
                n = len(plan.heads)
                if 1 <= i <= n:
                    exponent(i - 1)
                if i >= 3:
                    copy_output(i - 3)
                if 2 <= i < n + 2:
                    copy_transposed(i - 2)
                if 1 <= i <= n:
                    normalise(i - 1)

            act.wait_ge(weights_in, 16 * N_W)
            i = 0
            for s in engine_order("scalar"):
                if s[0] == "norm":
                    norm(s)
                elif s[0] == "transposes":
                    transposes(s)
                elif s[0] == "proj":
                    proj(s)
                elif s[0] == "latent":
                    latent(s)
                elif s[0] == "latent_up":
                    latent_up(s)
                elif s[0] == "queries":
                    queries(s)
                elif s[0] == "scores":
                    scores(s)
                elif s[0] == "head":
                    head(i)
                    i += 1
            for j in range(3):
                head(i + j)

        @block.vector
        def _(dve):
            step = [0]

            def link(ins):
                step[0] += 1
                ins.then_inc(dve_step, 1)
                dve.wait_ge(dve_step, step[0])

            def norm(s):
                b = s[1]
                dve.wait_ge(x_rstd, b + 1)
                nc.vector.scalar_tensor_tensor(x_in[:], x_in[:], rstd[:, 0:1], pre[:, 0, :],
                                               ALU.mult, ALU.mult).then_inc(h_scaled, 1)

            def gains(s):
                b = s[1]
                dve.wait_ge(work_free, plan.work0["proj", b, 4] + 1)
                dve.wait_ge(lat_rstd, b + 1)
                nc.vector.scalar_tensor_tensor(lat[:, 0:Q_RANK], pj[:, C_CQ:C_CQ + Q_RANK], rstd[:, 1:2], gq[:],
                                               ALU.mult, ALU.mult).then_inc(lat_ready, 1)
                nc.vector.scalar_tensor_tensor(lat[:, Q_RANK:], pj[:, C_CKV:C_CKV + KV_RANK], rstd[:, 2:3], gkv[:],
                                               ALU.mult, ALU.mult).then_inc(lat_ready, 1)

            def latent(s):
                b = s[1]
                dve.wait_ge(raw_ready, RAW_COUNT[s])
                low(ka[HD:P, :, b % 4, :], raw[HD:P, 0:2, :], k_hi[HD:P, 0:2, :])
                low(ki[HD:P, b * P:(b + 1) * P], raw[HD:P, 2, :], k_hi[HD:P, 2, :])

            def latent_up(s):
                b = s[1]
                dve.wait_ge(raw_ready, RAW_COUNT[s])
                low(kb[HD:P, b * P:(b + 1) * P], raw[HD:P, 2, :], k_hi[HD:P, 0, :])
                for r in range(2):
                    low(qi_lo[0:HD, r::2, :], raw[r * HD:(r + 1) * HD, 0:2, :], qi_hi[r * HD:(r + 1) * HD, r::2, :])

            def low(dst, whole, high):
                nc.vector.tensor_tensor(dst, whole, high.bitcast(F32), ALU.subtract).then_inc(split_done, 1)

            def queries(s):
                kind = s[1]
                dve.wait_ge(raw_ready, RAW_COUNT[s])
                for r in range(2):
                    low(q_lo[kind][0:HD, r::2, :], raw[r * HD:(r + 1) * HD],
                        q_hi[kind][r * HD:(r + 1) * HD, r::2, :])

            def scores(s):
                b = s[1]
                r = plan.score0[b]
                u = plan.work0[s]
                for o, n in key_chunks("B", b):
                    for h in range(IDX_HEADS):
                        dve.wait_ge(work_free, u + 1)
                        wh = widx[:, b % 2, h:h + 1]
                        if h == 0:
                            ins = nc.vector.tensor_scalar(score[:, o:o + n], relu[:, r % 2, 0:n], wh, None, ALU.mult)
                        else:
                            ins = nc.vector.scalar_tensor_tensor(score[:, o:o + n], relu[:, r % 2, 0:n], wh,
                                                                 score[:, o:o + n], ALU.mult, ALU.add)
                        ins.then_inc(relu_used, 1)
                        r += 1
                        u += 1
                        dve.wait_ge(relu_used, r)
                L = P * (b + 1)
                link(nc.vector.memset(score[0:CHUNK, L - CHUNK:L], LOWEST))
                link(nc.vector.memset(cand[:], 0))

            def reached(b, values, threshold):
                L = P * (b + 1)
                link(nc.vector.tensor_scalar(above[:, 0:L], values[:, 0:L], threshold, None,
                                             ALU.is_ge, ALU.add, accum_out=count[:]))

            def search(b, action):
                L = P * (b + 1)
                fcand = cand[:].bitcast(F32)
                what, j = action[0], action[-1]
                if what in ("whole", "high"):
                    reached(b, score if what == "whole" else short, fcand)
                    bit = -1.0 if j == 0 else 2.0 ** (31 - j)
                    following = 0 if j == 15 else 1 << (30 - j)
                    link(nc.vector.tensor_scalar(reject[:], count[:], float(TOPK), bit, ALU.is_lt, ALU.mult))
                    link(nc.vector.scalar_tensor_tensor(cand[:], cand[:], following, reject[:],
                                                        ALU.bitwise_xor, ALU.bitwise_xor))
                elif what == "shorten":
                    link(nc.vector.tensor_copy(short[:, 0:L], score[:].bitcast(BF16)[:, 1:2 * L:2]))
                elif what == "rebase":
                    link(nc.vector.tensor_scalar(above_it[:], cand[:], 1, None, ALU.bitwise_xor))
                    link(nc.vector.tensor_tensor(unit[:], above_it[:].bitcast(F32), fcand, ALU.subtract))
                    link(nc.vector.tensor_scalar(digit[:], powers[:], unit[:], None, ALU.mult))
                    link(nc.vector.tensor_scalar(score[:, 0:L], score[:, 0:L], fcand, None, ALU.subtract))
                    link(nc.vector.tensor_copy(fcand, digit[:, 0:1]))
                elif what == "low":
                    reached(b, short, fcand)
                    following = 16 if j in (7, 15) else j + 1
                    link(nc.vector.scalar_tensor_tensor(reject[:].bitcast(F32), count[:], float(TOPK),
                                                        digit[:, j:j + 1], ALU.is_lt, ALU.mult))
                    link(nc.vector.scalar_tensor_tensor(fcand, fcand, digit[:, following:following + 1],
                                                        reject[:].bitcast(F32), ALU.add, ALU.subtract))
                elif what == "last_digits":
                    link(nc.vector.tensor_scalar(short[:, 0:L], score[:, 0:L], fcand, None, ALU.subtract))
                    link(nc.vector.tensor_copy(fcand, digit[:, 8:9]))
                else:
                    ties(b, j)

            def ties(b, part):
                L = P * (b + 1)
                thr = cand[:].bitcast(F32)
                if part == 0:
                    nc.vector.tensor_scalar(equal[:, 0:L], short[:, 0:L], thr, None, ALU.is_equal)
                    link(nc.vector.tensor_scalar(above[:, 0:L], short[:, 0:L], thr, None,
                                                 ALU.is_lt, ALU.add, accum_out=count[:]))
                    link(nc.vector.tensor_tensor_scan(rank[:, 0:L], equal[:, 0:L], equal[:, 0:L], 0.0,
                                                      ALU.add, ALU.max))
                    link(nc.vector.scalar_tensor_tensor(need[:], rank[:, L - 1:L], float(TOPK - L), count[:],
                                                        ALU.add, ALU.add))
                    return
                link(nc.vector.scalar_tensor_tensor(equal[:, 0:L], rank[:, 0:L], need[:], equal[:, 0:L],
                                                    ALU.is_gt, ALU.mult))
                link(nc.vector.tensor_tensor(above[:, 0:L], above[:, 0:L], equal[:, 0:L], ALU.add))
                if b > 2:
                    dve.wait_ge(piece_full, plan.last_piece("B", b - 1))
                nc.vector.scalar_tensor_tensor(bias_b[:, 0:L], above[:, 0:L], -BIG, ndist[:, T - L:],
                                               ALU.mult, ALU.add).then_inc(bias_ready, 1)

            def copy_piece(i, c):
                kind, b, h = plan.heads[i]
                o, n = key_chunks(kind, b)[c]
                m = plan.chunk0[i] + c
                if c == 0 and i >= 2:
                    dve.wait_ge(exp_done, i - 1)
                dve.wait_ge(piece_full, m + 1)
                nc.vector.tensor_scalar(logit[:, i % 2, o:o + n], lbank[m % 2][:, 0:n], 1.0, None,
                                        ALU.mult, ALU.max, accum_out=mx[:, i % 2, c:c + 1]).then_inc(piece_read, 1)

            def maximum(i):
                kind, b, h = plan.heads[i]
                cols = len(key_chunks(kind, b))
                if kind == "A":
                    L = P * len(key_tiles(kind, b))
                    nc.vector.tensor_copy(logit[:, i % 2, L:L + 1], sink[:, h:h + 1])
                    link(nc.vector.tensor_copy(mx[:, i % 2, cols:cols + 1], sink[:, h:h + 1]))
                    cols += 1
                dve.wait_ge(piece_read, plan.chunk0[i + 1])
                nc.vector.tensor_reduce(negmax[:, i % 4:i % 4 + 1], mx[:, i % 2, 0:cols], AX.X, ALU.max,
                                        negate=True).then_inc(max_ready, 1)
                dve.wait_ge(max_ready, i + 1)

            def invert_total(i):
                dve.wait_ge(exp_done, i + 1)
                nc.vector.reciprocal(rtotal[:, i % 4:i % 4 + 1], total[:, i % 4:i % 4 + 1]).then_inc(total_inv, 1)

            dve.wait_ge(weights_in, 16 * N_W)
            for t in (*q_lo.values(), qi_lo):
                nc.vector.memset(t[HD:P, :, :].bitcast(F32), 0.0).then_inc(consts, 1)
            dve.wait_ge(dist_made, 2)
            link(nc.vector.tensor_scalar(logit[:, 0, 0:T], score[:], -1.0, None, ALU.mult))
            link(nc.vector.tensor_tensor(score[:], score[:], logit[:, 0, 0:T], ALU.min))
            nc.vector.tensor_copy(ndist[:], score[:]).then_inc(consts, 1)
            link(nc.vector.tensor_copy(bias_a[:], score[:, T - 2 * P:]))
            link(nc.vector.tensor_copy(bias_v[:], score[:, T - 2 * P:]))
            nc.vector.memset(bias_a[CHUNK:P, 0:P].bitcast(F32), -BIG).then_inc(consts, 1)
            nc.vector.memset(bias_a[0:CHUNK, 0:CHUNK].bitcast(F32), -BIG).then_inc(consts, 1)
            nc.vector.memset(bias_a[0:CHUNK, 2 * P - CHUNK:].bitcast(F32), -BIG).then_inc(consts, 1)
            nc.vector.memset(bias_v[0:CHUNK, 2 * P - CHUNK:].bitcast(F32), -BIG).then_inc(consts, 1)
            for k in range(17):
                nc.vector.memset(powers[:, k:k + 1], 2.0 ** (15 - k) if k < 16 else 0.0).then_inc(consts, 1)
            for h in range(HEADS):
                nc.vector.tensor_scalar(slope_id[:, h, :], ident[:], SLOPES[h], None, ALU.mult).then_inc(consts, 1)
            dve.wait_ge(consts, N_CONST)
            i = 0
            for s in engine_order("vector"):
                if s[0] == "norm":
                    norm(s)
                elif s[0] == "gains":
                    gains(s)
                elif s[0] == "latent":
                    latent(s)
                elif s[0] == "latent_up":
                    latent_up(s)
                elif s[0] == "queries":
                    queries(s)
                elif s[0] == "scores":
                    scores(s)
                elif s[0] == "head":
                    kind, b, h, chosen, actions = s[1:]
                    pieces = len(key_chunks(kind, b))
                    last = [] if not chosen or actions[-1] < len(SEARCH) - 1 else [actions[-1]]
                    actions = actions[0:len(actions) - len(last)] if chosen else []
                    for c in range(pieces):
                        for n in actions[c * len(actions) // pieces:(c + 1) * len(actions) // pieces]:
                            search(chosen, SEARCH[n])
                        copy_piece(i, c)
                    maximum(i)
                    if i >= 1:
                        invert_total(i - 1)
                    for n in last:
                        search(chosen, SEARCH[n])
                    i += 1
            invert_total(i - 1)


def raw_counts():
    out, n = {}, 0
    for s in mixing_steps()[0]:
        n += s[0] in SPLITS
        out[s] = n
    return out


RAW_COUNT = raw_counts()
OUT_ORDER = [("A", 0)] + [o for b in range(NB) for o in (("A", b + 1), ("B", b)) if o[1] < NB]
N_CONST = 25 + HEADS


def output_and_ffn(nc, w):
    NO = D // P
    HALF = KF // 2
    PANELS = NO + 2 * KF + 2 * NO
    with ExitStack() as ctx:
        def sb(name, shape, dt=F32):
            return ctx.enter_context(nc.sbuf_tensor(name, shape, dt))

        def psum(name, shape):
            return ctx.enter_context(nc.psum_tensor(name, shape, F32))

        def sem(name):
            return ctx.enter_context(nc.semaphore(name))

        x_hi = sb("x_hi", [P, KD, TOK], F32R)
        x_lo = sb("x_lo", [P, KD, TOK], F32R)
        a_hi = sb("a_hi", [P, KF, TOK], F32R)
        a_lo = sb("a_lo", [P, KF, TOK], F32R)
        yT = sb("yT", [P, KD, TOK])
        raw = sb("raw", [P, 2, HALF, P])
        p_hi = sb("p_hi", [P, 2, HALF, P], F32R)
        p_lo = sb("p_lo", [P, 2, HALF, P], F32R)
        rows = sb("rows", [P, 4, D])
        res = sb("res", [P, D])
        cur = sb("cur", [P, D])
        ident = sb("ident3", [P, P])
        cols = sb("cols", [P, 3])
        ssq = sb("ssq3", [P, 1])
        rstd = sb("rstd3", [P, 1])
        th = sb("th", [P, TOK])
        act32 = sb("act32", [P, TOK])

        gbank = psum("gbank", [P, TOK])
        ubank = psum("ubank", [P, TOK])
        ybank = [psum("ybank0", [P, TOK]), psum("ybank1", [P, TOK])]
        tbank = [psum("tb0", [P, KD, P]), psum("tb1", [P, KD, P])]

        consts = sem("f_consts")
        rows_in = sem("rows_in")
        mix_in = sem("mix_in")
        x_split = sem("x_split")
        x_high = sem("x_high")
        raw_in = [sem("raw_in0"), sem("raw_in1")]
        raw_given = sem("raw_given")
        panel_used = sem("panel_used")
        panel_high = sem("panel_high")
        panel_ready = sem("panel_ready")
        y_given = sem("y_given")
        tanh_done = sem("tanh_done")
        gated = sem("gated")
        act_made = sem("act_made")
        act_high = sem("act_high")
        act_ready = sem("act_ready")
        t_full = sem("t_full")
        res_in = sem("res_in")
        res_read = sem("res_read")
        sq_done = sem("sq_done")
        root_done = sem("root_done")
        cur_step = sem("cur_step")
        stored = sem("stored")
        pool_step = sem("f_pool_step")
        block = ctx.enter_context(nc.Block())

        NORMS = 3 * TPC

        def used(engine, c, number):
            engine.wait_ge(panel_used, c * PANELS + number + 3)


        @block.sync
        def _(sp):
            nc.sync.sem_inc(stored, 16)
            for i, r in enumerate((2, 3, 4, 5)):
                sp.dma_start(rows[:, i, :], w["mods"][r:r + 1, :].partition_broadcast(P)).then_inc(rows_in, 16)
            wo = w["w_o"].rearrange("(k p) n -> p k n", p=P)
            wgu = w["w_gate_up"].rearrange("(k p) n -> p k n", p=P)
            wd = w["w_down"].rearrange("(s k p) n -> s p k n", p=P, s=2)

            def panel(slot, c, number, kt, src):
                sp.wait_ge(raw_given, c * PANELS + number + 1)
                sp.dma_start(raw[:, slot, 0:kt, :], src).then_inc(raw_in[slot], 16)

            def residual(c, t, phase, src):
                sp.wait_ge(res_read, 1 + (c * 2 + phase) * TPC + t)
                sp.dma_start(res[:], src).then_inc(res_in, 16)

            def store(c, t, phase, dst):
                sp.wait_ge(cur_step, 1 + c * STEPS_C + (STEPS_1 * t + 2 if phase == 0 else STEPS_1 * TPC + STEPS_2 * (t + 1)))
                sp.dma_start(dst, cur[:]).then_inc(stored, 16)

            with sp.Fori(0, NCHUNK) as c:
                sp.wait_ge(t_full, 1 + c * 3 * TPC)
                sp.dma_start(yT[:], w["mixT"].rearrange("(k p) t -> p k t", p=P)[:, :, bass.ts(c, TOK)]
                             ).then_inc(mix_in, 16)
                with sp.Fori(0, NO // 2) as j:
                    for s in range(2):
                        panel(s, c, j * 2 + s, KD, wo[:, :, bass.ts(j * 2 + s, P)])
                panel(0, c, NO, KD, wgu[:, :, 0:P])
                panel(1, c, NO + 1, KD, wgu[:, :, D_FF:D_FF + P])
                for t in range(TPC):
                    residual(c, t, 0, w["x"][bass.ds(c * TOK + t * P, P), :])
                    store(c, t, 0, w["x1"][bass.ds(c * TOK + t * P, P), :])
                with sp.Fori(1, KF) as j:
                    panel(0, c, NO + j * 2, KD, wgu[:, :, bass.ts(j, P)])
                    panel(1, c, NO + j * 2 + 1, KD, wgu[:, :, bass.ds(j * P + D_FF, P)])
                with sp.Fori(0, NO) as j:
                    for s in range(2):
                        panel(s, c, NO + 2 * KF + j * 2 + s, HALF, wd[s][:, :, bass.ts(j, P)])
                sp.wait_ge(stored, 16 + c * (16 * 2 * TPC) + 16 * TPC)
                for t in range(TPC):
                    residual(c, t, 1, w["x1"][bass.ds(c * TOK + t * P, P), :])
                    store(c, t, 1, w["out"][bass.ds(c * TOK + t * P, P), :])
            sp.wait_ge(stored, 16 + 16 * 2 * TPC * NCHUNK)

        @block.gpsimd
        def _(pool):
            nc.gpsimd.memset(ident[:], 0.0).then_inc(pool_step, 1)
            for j, v in enumerate((-0.5, 1.0 / D, EPS)):
                nc.gpsimd.memset(cols[:, j:j + 1], v).then_inc(pool_step, 1)
            pool.wait_ge(pool_step, 4)
            nc.gpsimd.affine_select(out=ident[:], in_=ident[:], compare_op=ALU.not_equal, fill=1.0, base=0,
                                    pattern=[[-1, P]], channel_multiplier=1).then_inc(consts, 1)
            with pool.Fori(0, NCHUNK * NORMS) as n:
                pool.wait_ge(sq_done, n + 1)
                nc.gpsimd.tensor_tensor(rstd[:], ssq[:], cols[:, 1:2], ALU.mult).then_inc(pool_step, 1)
                pool.wait_ge(pool_step, 2 * n + 5)
                nc.gpsimd.tensor_tensor(rstd[:], rstd[:], cols[:, 2:3], ALU.add).then_inc(pool_step, 1)
                pool.wait_ge(pool_step, 2 * n + 6)
                nc.gpsimd.tensor_tensor(rstd[:], rstd[:], cols[:, 0:1], ALU.pow).then_inc(root_done, 1)

        @block.tensor
        def _(pe):
            def product(bank, slot, kt, hi, lo, k0, first, last):
                for k in range(kt):
                    rh, rl = hi[:, k0 + k, :], lo[:, k0 + k, :]
                    wh, wl = p_hi[:, slot, k, :], p_lo[:, slot, k, :]
                    nc.tensor.matmul(bank[:], wh, rh, start=(first and k == 0), stop=False)
                    nc.tensor.matmul(bank[:], wh, rl, start=False, stop=False)
                    mm = nc.tensor.matmul(bank[:], wl, rh, start=False, stop=(last and k == kt - 1))
                return mm.then_inc(panel_used, 1)

            def panel_wait(c, number):
                pe.wait_ge(panel_ready, c * PANELS + number + 1)

            def tokens_first(c, t, order):
                for k in range(KD):
                    mm = nc.tensor.transpose(tbank[t % 2][:, k, :], yT[:, k, t * P:(t + 1) * P], ident[:])
                mm.then_inc(t_full, 1)

            pe.wait_ge(consts, 1)
            nc.tensor.sem_inc(panel_used, 2)
            nc.tensor.sem_inc(t_full, 1)
            with pe.Fori(0, NCHUNK) as c:
                with pe.Fori(0, NO // 2) as j:
                    pe.wait_ge(x_split, c * (2 + TPC) + 2)
                    for s in range(2):
                        panel_wait(c, j * 2 + s)
                        pe.wait_ge(y_given, c * 2 * NO + j * 2 + s + 1)
                        product(ybank[s], s, KD, x_hi, x_lo, 0, True, True)
                pe.wait_ge(y_given, c * 2 * NO + NO + 2)
                for t in range(TPC):
                    pe.wait_ge(x_split, c * (2 + TPC) + 2 + t)
                    pe.wait_ge(cur_step, 1 + c * STEPS_C + STEPS_1 * t)
                    tokens_first(c, t, t)
                    pe.wait_ge(cur_step, 1 + c * STEPS_C + STEPS_1 * (t + 1))
                    for k in range(KD):
                        mm = nc.tensor.transpose(tbank[(t + 1) % 2][:, k, :], cur[:, k * P:(k + 1) * P], ident[:])
                    mm.then_inc(t_full, 1)
                with pe.Fori(0, KF) as j:
                    pe.wait_ge(x_split, (c + 1) * (2 + TPC))
                    panel_wait(c, NO + j * 2)
                    pe.wait_ge(gated, 1 + c * KF + j)
                    product(gbank, 0, KD, x_hi, x_lo, 0, True, True)
                    panel_wait(c, NO + j * 2 + 1)
                    pe.wait_ge(act_made, 1 + c * KF + j)
                    product(ubank, 1, KD, x_hi, x_lo, 0, True, True)
                with pe.Fori(0, NO // 2) as j:
                    pe.wait_ge(act_ready, 1 + (c + 1) * KF)
                    for s in range(2):
                        for half in range(2):
                            panel_wait(c, NO + 2 * KF + j * 4 + 2 * s + half)
                            if half == 0:
                                pe.wait_ge(y_given, c * 2 * NO + NO + j * 2 + s + 1)
                            product(ybank[s], half, HALF, a_hi, a_lo, half * HALF, half == 0, half == 1)
                pe.wait_ge(y_given, (c + 1) * 2 * NO + 2)
                for t in range(TPC):
                    pe.wait_ge(cur_step, 1 + c * STEPS_C + STEPS_1 * TPC + STEPS_2 * t)
                    tokens_first(c, t, t)

        @block.scalar
        def _(act):
            def high_part(c, number, slot, kt, seen):
                act.wait_ge(raw_in[slot], 16 * seen)
                act.wait_ge(panel_used, c * PANELS + number + 1)
                nc.scalar.activation(p_hi[:, slot, 0:kt, :], raw[:, slot, 0:kt, :], ACT.Copy).then_inc(panel_high, 1)

            def empty_y(c, last_panel, out, s):
                used(act, c, last_panel)
                nc.scalar.activation(out, ybank[s][:], ACT.Copy).then_inc(y_given, 1)

            def square(src):
                nc.scalar.activation(sq_out, src, ACT.Square, accum_out=ssq[:]).then_inc(sq_done, 1)

            sq_out = th[:].bitcast(BF16)
            nc.scalar.sem_inc(y_given, 2)
            with act.Fori(0, NCHUNK) as c:
                act.wait_ge(mix_in, (c + 1) * 16)
                act.wait_ge(panel_used, c * PANELS + 2)
                nc.scalar.activation(x_hi[:], yT[:], ACT.Copy).then_inc(x_high, 1)
                seen = c * (PANELS // 2)

                def wo_panel(n, slot, pair):
                    high_part(c, n, slot, KD, seen + pair + 1)

                def wo_tile(n, s):
                    empty_y(c, n, yT[:, bass.ds(n, 1), :].rearrange("p a n -> p (a n)"), s)

                for s in range(2):
                    wo_panel(s, s, 0)
                act.wait_ge(x_split, c * (2 + TPC) + 2)
                with act.Fori(0, NO // 2 - 1) as j:
                    for s in range(2):
                        wo_panel(j * 2 + 2 + s, s, j + 1)
                        wo_tile(j * 2 + s, s)
                for s in range(2):
                    high_part(c, NO + s, s, KD, seen + NO // 2 + 1)
                    wo_tile(NO - 2 + s, s)
                for t in range(TPC):
                    act.wait_ge(t_full, 1 + c * 3 * TPC + 2 * t + 1)
                    square(tbank[t % 2][:].rearrange("p k t -> p (k t)"))
                    act.wait_ge(cur_step, 1 + c * STEPS_C + STEPS_1 * t + 2)
                    act.wait_ge(root_done, c * NORMS + 2 * t + 1)
                    square(cur[:])
                    act.wait_ge(t_full, 1 + c * 3 * TPC + 2 * t + 2)
                    nc.scalar.activation(x_hi[:, :, t * P:(t + 1) * P], tbank[(t + 1) % 2][:], ACT.Copy
                                         ).then_inc(x_high, 1)

                def tanh(j):
                    used(act, c, NO + 2 * j)
                    act.wait_ge(gated, 1 + c * KF + j)
                    nc.scalar.activation(th[:], gbank[:], ACT.Tanh, scale=0.5).then_inc(tanh_done, 1)

                def act_high_part(j):
                    act.wait_ge(act_made, 1 + c * KF + j + 1)
                    nc.scalar.activation(a_hi[:, bass.ds(j, 1), :].rearrange("p a n -> p (a n)"), act32[:],
                                         ACT.Copy).then_inc(act_high, 1)

                with act.Fori(0, KF - 1) as j:
                    tanh(j)
                    for s in range(2):
                        high_part(c, NO + 2 + j * 2 + s, s, KD, seen + NO // 2 + j + 2)
                    act_high_part(j)
                down0 = NO + 2 * KF
                seen_down = seen + NO // 2 + KF
                tanh(KF - 1)
                high_part(c, down0, 0, HALF, seen_down + 1)
                high_part(c, down0 + 1, 1, HALF, seen_down + 1)
                act_high_part(KF - 1)

                def down_tile(n, s):
                    empty_y(c, down0 + 2 * n + 1, yT[:, bass.ds(n, 1), :].rearrange("p a n -> p (a n)"), s)

                with act.Fori(0, NO // 2 - 1) as j:
                    for s in range(2):
                        for half in range(2):
                            high_part(c, down0 + j * 4 + 2 * s + half + 2, half, HALF, seen_down + j * 2 + s + 2)
                        down_tile(j * 2 + s, s)
                for half in range(2):
                    high_part(c, down0 + 2 * NO - 2 + half, half, HALF, seen_down + NO)
                for s in range(2):
                    down_tile(NO - 2 + s, s)
                for t in range(TPC):
                    act.wait_ge(t_full, 1 + c * 3 * TPC + 2 * TPC + t + 1)
                    if t:
                        act.wait_ge(root_done, c * NORMS + 2 * TPC + t)
                    square(tbank[t % 2][:].rearrange("p k t -> p (k t)"))

        @block.vector
        def _(dve):
            def low_part(c, number, slot, kt):
                dve.wait_ge(panel_high, c * PANELS + number + 1)
                nc.vector.tensor_tensor(p_lo[:, slot, 0:kt, :], raw[:, slot, 0:kt, :],
                                        p_hi[:, slot, 0:kt, :].bitcast(F32), ALU.subtract).then_inc(panel_ready, 1)
                dve.wait_ge(panel_ready, c * PANELS + number + 1)
                nc.vector.sem_inc(raw_given, 1)

            def scaled_rows(c, base, t, norm_no, bank, row, res_no):
                src = tbank[bank][:].rearrange("p k t -> p (k t)")
                dve.wait_ge(root_done, norm_no)
                dve.wait_ge(stored, 16 + 16 * res_no)
                nc.vector.scalar_tensor_tensor(cur[:], src, rstd[:], rows[:, row, :], ALU.mult, ALU.mult
                                               ).then_inc(cur_step, 1)
                dve.wait_ge(cur_step, 1 + base + 1)
                dve.wait_ge(res_in, 16 * (res_no + 1))
                nc.vector.tensor_tensor(cur[:], cur[:], res[:], ALU.add).then_inc(cur_step, 1)
                dve.wait_ge(cur_step, 1 + base + 2)
                nc.vector.sem_inc(res_read, 1)

            dve.wait_ge(rows_in, 64)
            nc.vector.sem_inc(raw_given, 2)
            for counter in (res_read, cur_step, gated, act_made, act_ready):
                nc.vector.sem_inc(counter, 1)
            with dve.Fori(0, NCHUNK) as c:
                dve.wait_ge(x_high, c * (1 + TPC) + 1)
                for half in range(2):
                    k0, k1 = half * KD // 2, (half + 1) * KD // 2
                    nc.vector.tensor_tensor(x_lo[:, k0:k1, :], yT[:, k0:k1, :], x_hi[:, k0:k1, :].bitcast(F32),
                                            ALU.subtract).then_inc(x_split, 1)
                with dve.Fori(0, NO // 2) as j:
                    for s in range(2):
                        low_part(c, j * 2 + s, s, KD)
                for s in range(2):
                    low_part(c, NO + s, s, KD)
                for t in range(TPC):
                    base = c * STEPS_C + STEPS_1 * t
                    scaled_rows(c, base, t, c * NORMS + 2 * t + 1, t % 2, 0, c * 2 * TPC + t)
                    dve.wait_ge(root_done, c * NORMS + 2 * t + 2)
                    dve.wait_ge(stored, 16 + 16 * (c * 2 * TPC + t + 1))
                    nc.vector.scalar_tensor_tensor(cur[:], cur[:], rstd[:], rows[:, 1, :], ALU.mult, ALU.mult
                                                   ).then_inc(cur_step, 1)
                    dve.wait_ge(cur_step, 1 + base + 3)
                    nc.vector.tensor_tensor(cur[:], cur[:], rows[:, 2, :], ALU.add).then_inc(cur_step, 1)
                    dve.wait_ge(x_high, c * (1 + TPC) + 2 + t)
                    nc.vector.tensor_tensor(x_lo[:, :, t * P:(t + 1) * P], tbank[(t + 1) % 2][:],
                                            x_hi[:, :, t * P:(t + 1) * P].bitcast(F32), ALU.subtract
                                            ).then_inc(x_split, 1)

                def gate(j):
                    dve.wait_ge(tanh_done, c * KF + j + 1)
                    dve.wait_ge(act_ready, 1 + c * KF + j)
                    nc.vector.scalar_tensor_tensor(act32[:], th[:], 1.0, gbank[:], ALU.add, ALU.mult
                                                   ).then_inc(gated, 1)

                def times_up(j):
                    dve.wait_ge(gated, 1 + c * KF + j + 1)
                    used(dve, c, NO + 2 * j + 1)
                    nc.vector.scalar_tensor_tensor(act32[:], act32[:], 0.5, ubank[:], ALU.mult, ALU.mult
                                                   ).then_inc(act_made, 1)

                def act_low_part(j):
                    dve.wait_ge(act_high, c * KF + j + 1)
                    nc.vector.tensor_tensor(a_lo[:, bass.ds(j, 1), :].rearrange("p a n -> p (a n)"), act32[:],
                                            a_hi[:, bass.ds(j, 1), :].rearrange("p a n -> p (a n)").bitcast(F32),
                                            ALU.subtract).then_inc(act_ready, 1)

                with dve.Fori(0, KF - 1) as j:
                    gate(j)
                    low_part(c, NO + 2 + j * 2, 0, KD)
                    times_up(j)
                    low_part(c, NO + 2 + j * 2 + 1, 1, KD)
                    act_low_part(j)
                gate(KF - 1)
                low_part(c, NO + 2 * KF, 0, HALF)
                times_up(KF - 1)
                low_part(c, NO + 2 * KF + 1, 1, HALF)
                act_low_part(KF - 1)
                with dve.Fori(1, NO) as j:
                    for half in range(2):
                        low_part(c, NO + 2 * KF + j * 2 + half, half, HALF)
                for t in range(TPC):
                    base = c * STEPS_C + STEPS_1 * TPC + STEPS_2 * t
                    scaled_rows(c, base, t, c * NORMS + 2 * TPC + t + 1, t % 2, 3, c * 2 * TPC + TPC + t)


STEPS_1 = 4
STEPS_2 = 2
STEPS_C = TPC * (STEPS_1 + STEPS_2)


_INS = ["x", "c", "w_ada", "b_ada", "g_pre_mix", "g_post_mix", "w_in", "q_norm_g", "kv_norm_g", "w_uq",
        "w_qidx", "w_ukv", "a_sinks", "w_o", "g_pre_ffn", "g_post_ffn", "w_gate_up", "w_down"]


def kernel(**inputs):
    import numpy as _np
    import concourse.bacc as _bacc
    from concourse import mybir as _mybir
    from concourse.bass_utils import run_bass_kernel_spmd as _run

    nc = _bacc.Bacc("TRN2", target_bir_lowering=False, num_devices=1)
    arrays, w = {}, {}
    for name in _INS:
        a = _np.ascontiguousarray(inputs[name])
        if a.ndim == 3:
            a = a[0]
        arrays[f"in_{name}"] = a
        w[name] = nc.dram_tensor(f"in_{name}", a.shape, _mybir.dt.from_np(a.dtype), kind="ExternalInput").ap()
    w["out"] = nc.dram_tensor("out_0", (T, D), F32, kind="ExternalOutput").ap()
    w["mods"] = nc.dram_tensor("mods", (6, D), F32).ap()
    w["mixT"] = nc.dram_tensor("mixT", (D, T), F32).ap()
    w["x1"] = nc.dram_tensor("x1", (T, D), F32).ap()
    modulation(nc, w)
    mixing(nc, w)
    output_and_ffn(nc, w)
    r = _run(nc, [arrays], core_ids=[0])
    return _np.reshape(r.results[0]["out_0"], (1, T, D))
```

```python
from contextlib import ExitStack

import concourse.bass as bass
from concourse import mybir

F32 = mybir.dt.float32
F32R = mybir.dt.float32r
BF16 = mybir.dt.bfloat16
F16 = mybir.dt.float16
I32 = mybir.dt.int32
ALU = mybir.AluOpType
ACT = mybir.ActivationFunctionType
AX = mybir.AxisListType

P = 128
D = 1024
T = 2048
KD = D // P
CHUNK = 64
HD = 64
HEADS = 8
A_KV = 2
Q_RANK = 256
KV_RANK = 128
IDX_HEADS = 4
TOPK = 256
D_FF = 2816
KF = D_FF // P
D_IN = 1220
NB = T // P
EPS = 1e-6
SCALE = HD ** -0.5
IDX_SCALE = IDX_HEADS ** -0.5 * HD ** -0.5
BIG = 2.0 ** 100
LOWEST = -3.0e38
C_KA, C_VA, C_CQ, C_CKV, C_KI, C_WI = 512, 640, 768, 1024, 1152, 1216
BANK = 512
SLOPES = [2.0 ** (-8.0 * (h + 1) / HEADS) for h in range(HEADS)]
TOK = 512
NCHUNK = T // TOK
TPC = TOK // P


def modulation(nc, w):
    with ExitStack() as ctx:
        def sb(name, shape, dt=F32):
            return ctx.enter_context(nc.sbuf_tensor(name, shape, dt))

        def sem(name):
            return ctx.enter_context(nc.semaphore(name))

        NCH = 6 * D // BANK
        ccol = sb("ccol", [P, KD])
        cth = sb("cth", [P, KD])
        chalf = sb("chalf", [P, KD])
        cact = sb("cact", [P, KD])
        ones = sb("ones_mod", [P, P])
        cwide = sb("cwide", [P, KD, P])
        wada = sb("wada", [P, 2, KD, BANK])
        brow = sb("brow", [P, 6 * D])
        gains = sb("gains", [P, 4, D])
        mod = sb("mod", [P, 6 * D])
        out = sb("modout", [P, 6, D])
        ps = ctx.enter_context(nc.psum_tensor("mod_ps", [P, 2, BANK], F32))
        small_in = sem("mod_small_in")
        wada_in = [sem("wada_in0"), sem("wada_in1")]
        c_tanh = sem("c_tanh")
        c_steps = sem("c_steps")
        wide = sem("c_wide")
        prod = sem("mod_prod")
        summed = sem("mod_summed")
        scaled = sem("mod_scaled")
        stored = sem("mod_stored")
        block = ctx.enter_context(nc.Block())

        @block.sync
        def _(sp):
            with nc.allow_non_contiguous_dma(reason="c as one column per 128 channels: 4 KB"):
                sp.dma_start(ccol[:], w["c"].rearrange("a (k p) -> (a p) k", p=P)).then_inc(small_in, 16)
            sp.dma_start(brow[:], w["b_ada"].partition_broadcast(P)).then_inc(small_in, 16)
            for i, g in enumerate(("g_pre_mix", "g_post_mix", "g_pre_ffn", "g_post_ffn")):
                sp.dma_start(gains[:, i, :], w[g].partition_broadcast(P)).then_inc(small_in, 16)
            wa = w["w_ada"].rearrange("(k p) n -> p k n", p=P)
            for n in range(NCH):
                if n >= 2:
                    sp.wait_ge(prod, n - 1)
                sp.dma_start(wada[:, n % 2], wa[:, :, n * BANK:(n + 1) * BANK]).then_inc(wada_in[n % 2], 16)
            sp.wait_ge(scaled, 6)
            sp.dma_start(w["mods"].rearrange("a (p n) -> p a n", p=1), out[0:1, :, :]).then_inc(stored, 16)
            sp.wait_ge(stored, 16)

        @block.scalar
        def _(act):
            act.wait_ge(small_in, 96)
            nc.scalar.activation(cth[:], ccol[:], ACT.Tanh, scale=0.5).then_inc(c_tanh, 1)

        @block.vector
        def _(dve):
            nc.vector.memset(ones[:], 1.0).then_inc(c_steps, 1)
            dve.wait_ge(small_in, 96)
            nc.vector.tensor_scalar(chalf[:], ccol[:], 0.5, None, ALU.mult).then_inc(c_steps, 1)
            dve.wait_ge(c_steps, 2)
            dve.wait_ge(c_tanh, 1)
            nc.vector.scalar_tensor_tensor(cact[:], cth[:], 1.0, chalf[:], ALU.add, ALU.mult).then_inc(c_steps, 1)
            dve.wait_ge(c_steps, 3)
            for k in range(KD):
                nc.vector.tensor_scalar(cwide[:, k, :], ones[:], cact[:, k:k + 1], None, ALU.mult).then_inc(wide, 1)
            for n in range(NCH):
                dve.wait_ge(prod, n + 1)
                nc.vector.tensor_tensor(mod[:, n * BANK:(n + 1) * BANK], ps[:, n % 2, :],
                                        brow[:, n * BANK:(n + 1) * BANK], ALU.add).then_inc(summed, 1)
            dve.wait_ge(summed, NCH)
            for half in range(2):
                sh, sc, gt = (mod[:, (3 * half + i) * D:(3 * half + i + 1) * D] for i in range(3))
                nc.vector.scalar_tensor_tensor(out[:, 3 * half, :], sc, 1.0, gains[:, 2 * half, :],
                                               ALU.add, ALU.mult).then_inc(scaled, 1)
                nc.vector.tensor_copy(out[:, 3 * half + 1, :], sh).then_inc(scaled, 1)
                nc.vector.tensor_tensor(out[:, 3 * half + 2, :], gt, gains[:, 2 * half + 1, :],
                                        ALU.mult).then_inc(scaled, 1)

        @block.tensor
        def _(pe):
            pe.wait_ge(wide, KD)
            for n in range(NCH):
                pe.wait_ge(wada_in[n % 2], 16 * (n // 2 + 1))
                if n >= 2:
                    pe.wait_ge(summed, n - 1)
                for k in range(KD):
                    mm = nc.tensor.matmul(ps[:, n % 2, :], cwide[:, k, :], wada[:, n % 2, k, :],
                                          start=(k == 0), stop=(k == KD - 1))
                mm.then_inc(prod, 1)



SEARCH = ([("whole", 0), ("shorten",)] + [("high", j) for j in range(1, 16)] + [("rebase",), ("shorten",)]
          + [("low", k) for k in range(8)] + [("last_digits",)] + [("low", k) for k in range(8, 16)]
          + [("ties", 0), ("ties", 1)])
BESIDE_A = [2, 3, 3, 3, 3, 3, 3, 2]
BESIDE_B = [2, 2, 2, 2, 2, 2, 2, 2]
assert sum(BESIDE_A) + sum(BESIDE_B) == len(SEARCH)


def mixing_steps():
    steps = ([("norm", 0), ("transposes", 0)] + [("proj", 0, c) for c in range(5)]
             + [("queries", "A", 0), ("gains", 0), ("latent", 0), ("latent_up", 0), ("norm", 1)])
    beside = set()

    def add(*side):
        steps.extend(side)
        beside.update(side)

    def front_a(b, h):
        add(*{0: [("transposes", b)], 2: [("proj", b, 0)], 3: [("proj", b, 1)], 4: [("proj", b, 2)],
              5: [("proj", b, 3)], 6: [("proj", b, 4)]}.get(h, []))

    for h in range(HEADS):
        steps.append(("head", "A", 0, h, None, range(0)))
        front_a(1, h)
    steps += [("queries", "A", 1), ("gains", 1), ("latent", 1), ("latent_up", 1), ("norm", 2)]
    for b in range(NB):
        nxt = b + 1 if b + 1 < NB else None
        chosen = nxt if nxt and P * (nxt + 1) > TOPK else None
        done = 0
        if chosen:
            steps.append(("scores", chosen))
        if not nxt:
            steps.append(("queries", "B", b))
        for h in range(HEADS if nxt else 0):
            steps.append(("head", "A", nxt, h, chosen, range(done, done + BESIDE_A[h])))
            done += BESIDE_A[h]
            if b + 2 < NB:
                front_a(b + 2, h)
            if h == 3:
                add(("queries", "B", b))
        for h in range(HEADS):
            steps.append(("head", "B", b, h, chosen, range(done, done + BESIDE_B[h])))
            done += BESIDE_B[h]
            if b + 2 < NB:
                add(*{0: [("queries", "A", b + 2), ("gains", b + 2)], 2: [("latent", b + 2)],
                      4: [("latent_up", b + 2)]}.get(h, []))
            if b + 3 < NB and h == 6:
                add(("norm", b + 3))
    return steps, beside


LAG = {"scalar": {"transposes": 1, "proj": 1, "latent": 1, "latent_up": 1, "queries": 1},
       "vector": {"norm": 1, "latent": 2, "latent_up": 2, "queries": 2}}
WORK_USES = {"transposes": lambda s: 2, "proj": lambda s: (s[2] + 1) % 2, "latent": lambda s: 2,
             "latent_up": lambda s: 1, "queries": lambda s: 1,
             "scores": lambda s: IDX_HEADS * len(key_chunks("B", s[1]))}
SPLITS = {"latent": 2, "latent_up": 3, "queries": 2}


def engine_order(engine):
    steps, beside = mixing_steps()
    out, late = [], []
    for s in steps:
        lag = LAG[engine].get(s[0], 0)
        if s in beside:
            if lag:
                late.append((lag, s))
            else:
                out.append(s)
            continue
        if s[0] != "head":
            out += [x for _, x in late]
            late = []
        out.append(s)
        late = [(n - 1, x) for n, x in late]
        out += [x for n, x in late if n == 0]
        late = [(n, x) for n, x in late if n > 0]
    return out + [x for _, x in late]


def key_tiles(kind, b):
    if kind == "B":
        return list(range(b + 1))
    return [b - 1, b] if b else [0]


def key_chunks(kind, b):
    cols = P * len(key_tiles(kind, b))
    return [(o, min(BANK, cols - o)) for o in range(0, cols, BANK)]


class Plan:

    def __init__(self):
        self.steps = mixing_steps()[0]
        self.heads = [s[1:4] for s in self.steps if s[0] == "head"]
        self.head_no = {h: i for i, h in enumerate(self.heads)}
        self.chunk0, self.group0 = [], []
        m = t = 0
        for kind, b, h in self.heads:
            self.chunk0.append(m)
            self.group0.append(t)
            m += len(key_chunks(kind, b))
            t += -(-len(key_tiles(kind, b)) // 4)
        self.chunk0.append(m)
        self.group0.append(t)
        self.work0, self.score0, self.split0 = {}, {}, {}
        u = r = v = 0
        for s in self.steps:
            if s[0] in WORK_USES:
                self.work0[s] = u
                u += WORK_USES[s[0]](s)
            if s[0] == "scores":
                self.score0[s[1]] = r
                r += IDX_HEADS * len(key_chunks("B", s[1]))
            if s[0] in SPLITS:
                self.split0[s] = v
                v += SPLITS[s[0]]

    def last_piece(self, kind, b):
        return self.chunk0[self.head_no[kind, b, HEADS - 1] + 1]

    def groups(self, i):
        tiles = key_tiles(*self.heads[i][0:2])
        return [tiles[j:j + 4] for j in range(0, len(tiles), 4)]


def mixing(nc, w):
    plan = Plan()
    with ExitStack() as ctx:
        def sb(name, shape, dt=F32):
            return ctx.enter_context(nc.sbuf_tensor(name, shape, dt))

        def psum(name, shape):
            return ctx.enter_context(nc.psum_tensor(name, shape, F32))

        def sem(name):
            return ctx.enter_context(nc.semaphore(name))

        w_in = sb("w_in", [P, KD, D_IN])
        w_uq = sb("w_uq", [P, Q_RANK // P, HEADS * HD])
        w_qi = sb("w_qi", [P, Q_RANK // P, IDX_HEADS * HD])
        w_uk2 = sb("w_uk2", [P, 2 * HD])
        w_uv = sb("w_uv", [P, HD])
        pre = sb("pre", [P, 2, D])
        gq = sb("gq", [P, Q_RANK])
        gkv = sb("gkv", [P, KV_RANK])
        sink = sb("sink", [P, HEADS])
        ident = sb("ident", [P, P])
        slope_id = sb("slope_id", [P, HEADS, P], F32R)
        neg_half = sb("neg_half", [P, 1])
        ndist = sb("ndist", [P, T], F16)
        bias_a = sb("bias_a", [P, 2 * P], F32R)
        bias_v = sb("bias_v", [P, 2 * P], F32R)
        bias_b = sb("bias_b", [P, T], F32R)
        ka = sb("ka", [P, A_KV, 4, P], F32R)
        ki = sb("ki", [P, T], F32R)
        kb = sb("kb", [P, T], F32R)
        va = sb("va", [P, 4, P])
        vb = sb("vb", [P, NB, HD])
        q_hi = {"A": sb("qa_hi", [P, HEADS, P], F32R), "B": sb("qb_hi", [P, HEADS, P], F32R)}
        q_lo = {"A": sb("qa_lo", [P, HEADS, P], F32R), "B": sb("qb_lo", [P, HEADS, P], F32R)}
        qi_hi = sb("qi_hi", [P, IDX_HEADS, P], F32R)
        qi_lo = sb("qi_lo", [P, IDX_HEADS, P], F32R)
        raw = sb("raw_heads", [P, 4, P])
        k_hi = sb("k_hi", [P, 3, P], F32R)
        x_in = sb("x_in", [P, D])
        h_T = sb("h_T", [P, KD, P])
        pj = sb("pj", [P, D_IN])
        kk = sb("kk", [P, 3, 2, HD])
        lat = sb("lat", [P, Q_RANK + KV_RANK])
        latT = sb("latT", [P, 2, 3, P])
        widx = sb("widx", [P, 2, IDX_HEADS])
        ssq = sb("ssq", [P, 3])
        rstd = sb("rstd", [P, 3])
        relu = sb("relu", [P, 2, BANK])
        score = sb("score", [P, T])
        above = sb("above", [P, T], BF16)
        equal = sb("equal", [P, T], BF16)
        rank = sb("rank", [P, T], F16)
        powers = sb("powers", [P, 17])
        digit = sb("digit", [P, 17])
        cand = sb("cand", [P, 1], I32)
        above_it = sb("above_it", [P, 1], I32)
        unit = sb("unit", [P, 1])
        reject = sb("reject", [P, 1], I32)
        count = sb("count", [P, 1])
        need = sb("need", [P, 1])
        logit = sb("logit", [P, 2, T + 4])
        prob = sb("prob", [P, 2, T + 4])
        probT = sb("probT", [P, 2, BANK])
        mx = sb("mx", [P, 2, 5])
        negmax = sb("negmax", [P, 4])
        total = sb("total", [P, 2, HEADS])
        rtotal = sb("rtotal", [P, HEADS])
        o_norm = sb("o_norm", [P, HEADS, HD])
        oT = sb("oT", [P, 4, P])
        squares = h_T[:].rearrange("p k t -> p (k t)")
        short = rank[:].bitcast(BF16)

        work = [psum("work0", [P, BANK]), psum("work1", [P, BANK])]
        lbank = [psum("lbank0", [P, BANK]), psum("lbank1", [P, BANK])]
        tbank = [psum("tbank0", [P, BANK]), psum("tbank1", [P, BANK])]
        obank = [psum("obank0", [P, BANK]), psum("obank1", [P, BANK])]

        weights_in = sem("weights_in")
        dist_made = sem("dist_made")
        consts = sem("consts")
        x_loaded = sem("x_loaded")
        x_ssq = sem("x_ssq")
        x_rstd = sem("x_rstd")
        h_scaled = sem("h_scaled")
        h_ready = sem("h_ready")
        work_full = sem("work_full")
        work_free = sem("work_free")
        key_twice = sem("key_twice")
        raw_ready = sem("raw_ready")
        split_done = sem("split_done")
        lat_ssq = sem("lat_ssq")
        lat_rstd = sem("lat_rstd")
        lat_ready = sem("lat_ready")
        relu_used = sem("relu_used")
        piece_full = sem("piece_full")
        piece_read = sem("piece_read")
        max_ready = sem("max_ready")
        exp_done = sem("exp_done")
        pt_full = sem("pt_full")
        pt_ready = sem("pt_ready")
        pv_done = sem("pv_done")
        bias_ready = sem("bias_ready")
        o_scaled = sem("o_scaled")
        o_turned = sem("o_turned")
        o_copied = sem("o_copied")
        o_stored = sem("o_stored")
        dve_step = sem("dve_step")
        pool_step = sem("pool_step")
        act_step = sem("act_step")
        block = ctx.enter_context(nc.Block())

        N_W = 11

        def bias_of(kind, b, o, n):
            if kind == "A":
                return bias_a[:, (P if b == 0 else 0) + o:][:, 0:n]
            if b < 2:
                return bias_v[:, 2 * P - P * (b + 1) + o:][:, 0:n]
            return bias_b[:, o:o + n]

        @block.sync
        def _(sp):
            wi = w["w_in"].rearrange("(k p) n -> p k n", p=P)
            sp.dma_start(x_in[:], w["x"][0:P, :]).then_inc(x_loaded, 16)
            sp.dma_start(pre[:, 0, :], w["mods"][0:1, :].partition_broadcast(P)).then_inc(weights_in, 16)
            sp.dma_start(pre[:, 1, :], w["mods"][1:2, :].partition_broadcast(P)).then_inc(weights_in, 16)
            sp.dma_start(w_in[:], wi).then_inc(weights_in, 16)
            sp.dma_start(w_uq[:], w["w_uq"].rearrange("(k p) n -> p k n", p=P)).then_inc(weights_in, 16)
            sp.dma_start(w_qi[:], w["w_qidx"].rearrange("(k p) n -> p k n", p=P)).then_inc(weights_in, 16)
            for i in range(2):
                sp.dma_start(w_uk2[:, i * HD:(i + 1) * HD], w["w_ukv"][:, 0:HD]).then_inc(weights_in, 16)
            sp.dma_start(w_uv[:], w["w_ukv"][:, HD:]).then_inc(weights_in, 16)
            sp.dma_start(gq[:], w["q_norm_g"].partition_broadcast(P)).then_inc(weights_in, 16)
            sp.dma_start(gkv[:], w["kv_norm_g"].partition_broadcast(P)).then_inc(weights_in, 16)
            sp.dma_start(sink[:], w["a_sinks"].partition_broadcast(P)).then_inc(weights_in, 16)

            def load_x(b):
                sp.wait_ge(work_full, plan.work0["transposes", b - 1] + 2)
                sp.dma_start(x_in[:], w["x"][b * P:(b + 1) * P, :]).then_inc(x_loaded, 16)

            for b in (1, 2):
                load_x(b)
            for i, (kind, b) in enumerate(OUT_ORDER):
                if kind == "A" and 1 <= b and b + 2 < NB:
                    load_x(b + 2)
                sp.wait_ge(o_copied, i + 1)
                row0 = 0 if kind == "A" else HEADS * HD
                sp.dma_start(
                    w["mixT"][row0:row0 + HEADS * HD, b * P:(b + 1) * P].rearrange("(j p) t -> p j t", p=P),
                    oT[:]).then_inc(o_stored, 16)
            sp.wait_ge(o_stored, 16 * 2 * NB)

        @block.gpsimd
        def _(pool):
            step = [0]

            def link(ins):
                step[0] += 1
                ins.then_inc(pool_step, 1)
                pool.wait_ge(pool_step, step[0])

            link(nc.gpsimd.memset(ident[:], 0.0))
            nc.gpsimd.affine_select(out=ident[:], in_=ident[:], compare_op=ALU.not_equal, fill=1.0, base=0,
                                    pattern=[[-1, P]], channel_multiplier=1).then_inc(dist_made, 1)
            nc.gpsimd.iota(score[:], [[-1, T]], base=T - P, channel_multiplier=1,
                           allow_small_or_imprecise_dtypes=True).then_inc(dist_made, 1)
            link(nc.gpsimd.memset(neg_half[:], -0.5))
            pool.wait_ge(weights_in, 16 * N_W)
            for s in plan.steps:
                if s[0] not in ("norm", "gains"):
                    continue
                b = s[1]
                if s[0] == "norm":
                    done, out_ready, jobs = x_ssq, x_rstd, ((0, D),)
                else:
                    done, out_ready, jobs = lat_ssq, lat_rstd, ((1, Q_RANK), (2, KV_RANK))
                pool.wait_ge(done, b + 1)
                for j, width in jobs:
                    link(nc.gpsimd.tensor_scalar(rstd[:, j:j + 1], ssq[:, j:j + 1], 1.0 / width, EPS,
                                                 ALU.mult, ALU.add))
                for j, width in jobs:
                    ins = nc.gpsimd.tensor_tensor(rstd[:, j:j + 1], rstd[:, j:j + 1], neg_half[:], ALU.pow)
                    if j == jobs[-1][0]:
                        ins.then_inc(out_ready, 1)
                    else:
                        link(ins)
                if s[0] == "norm":
                    pool.wait_ge(h_scaled, b + 1)
                    nc.gpsimd.tensor_tensor(x_in[:], x_in[:], pre[:, 1, :], ALU.add).then_inc(h_ready, 1)

        @block.tensor
        def _(pe):
            def next_work(u):
                if u >= 2:
                    pe.wait_ge(work_free, u - 1)
                return work[u % 2]

            def transposes(s):
                b = s[1]
                u = plan.work0[s]
                pe.wait_ge(h_ready, b + 1)
                for half in range(2):
                    ps = next_work(u)
                    for j in range(4):
                        k = 4 * half + j
                        mm = nc.tensor.transpose(ps[:, j * P:(j + 1) * P], x_in[:, k * P:(k + 1) * P], ident[:])
                    mm.then_inc(work_full, 1)
                    u += 1

            def proj(s):
                _, b, part = s
                c = part // 2
                u = plan.work0["proj", b, 2 * c]
                if part == 0:
                    pe.wait_ge(work_free, u)
                ps = next_work(u) if part % 2 == 0 else work[u % 2]
                n0, n1 = c * BANK, min((c + 1) * BANK, D_IN)
                for k in range(KD) if c == 2 else range(4 * (part % 2), 4 * (part % 2) + 4):
                    mm = nc.tensor.matmul(ps[:, 0:n1 - n0], h_T[:, k, :], w_in[:, k, n0:n1],
                                          start=(k == 0), stop=(k == KD - 1))
                if part != 0 and part != 2:
                    mm.then_inc(work_full, 1)

            def latent(s):
                b = s[1]
                u = plan.work0[s]
                pe.wait_ge(key_twice, 2 * (b + 1))
                ps = next_work(u)
                for j in range(3):
                    nc.tensor.transpose(ps[:, j * P:(j + 1) * P], kk[:, j, :, :].rearrange("p a d -> p (a d)"),
                                        ident[:])
                pe.wait_ge(lat_ready, 2 * (b + 1))
                mm = nc.tensor.transpose(ps[:, 3 * P:4 * P], lat[:, Q_RANK:], ident[:])
                mm.then_inc(work_full, 1)
                ps = next_work(u + 1)
                for j in range(2):
                    mm = nc.tensor.transpose(ps[:, j * P:(j + 1) * P], lat[:, j * P:(j + 1) * P], ident[:])
                mm.then_inc(work_full, 1)

            def latent_up(s):
                b = s[1]
                u = plan.work0[s]
                pe.wait_ge(work_free, plan.work0["latent", b] + 2)
                ps = next_work(u)
                for n in range(2):
                    for k in range(2):
                        nc.tensor.matmul(ps[:, n * P:(n + 1) * P], w_qi[:, k, n * P:(n + 1) * P],
                                         latT[:, b % 2, k, :], start=(k == 0), stop=(k == 1))
                nc.tensor.matmul(ps[:, 2 * P:3 * P], w_uk2[:], latT[:, b % 2, 2, :], start=True, stop=True)
                mm = nc.tensor.matmul(ps[:, 3 * P:3 * P + HD], latT[:, b % 2, 2, :], w_uv[:], start=True, stop=True)
                mm.then_inc(work_full, 1)

            def queries(s):
                _, kind, b = s
                u = plan.work0[s]
                ps = next_work(u)
                for n in range(4):
                    if kind == "A":
                        pe.wait_ge(work_free, plan.work0["proj", b, 0] + 1)
                        mm = nc.tensor.transpose(ps[:, n * P:(n + 1) * P], pj[:, n * P:(n + 1) * P], ident[:])
                        continue
                    for k in range(2):
                        mm = nc.tensor.matmul(ps[:, n * P:(n + 1) * P], w_uq[:, k, n * P:(n + 1) * P],
                                              latT[:, b % 2, k, :], start=(k == 0), stop=(k == 1))
                mm.then_inc(work_full, 1)

            def scores(s):
                b = s[1]
                u = plan.work0[s]
                pe.wait_ge(split_done, plan.split0["latent_up", b] + SPLITS["latent_up"])
                for o, n in key_chunks("B", b):
                    for h in range(IDX_HEADS):
                        ps = next_work(u)
                        nc.tensor.matmul(ps[:, 0:n], qi_hi[:, h, :], ki[:, o:o + n], start=True, stop=False)
                        nc.tensor.matmul(ps[:, 0:n], qi_lo[:, h, :], ki[:, o:o + n],
                                         start=False, stop=True).then_inc(work_full, 1)
                        u += 1

            def piece(i, c):
                kind, b, h = plan.heads[i]
                g = h // (HEADS // A_KV)
                if c == 0 and h == 0:
                    last = ("latent_up", b) if kind == "A" else ("queries", "B", b)
                    pe.wait_ge(split_done, plan.split0[last] + SPLITS[last[0]])
                    if kind == "B" and b >= 2:
                        pe.wait_ge(bias_ready, b - 1)
                o, n = key_chunks(kind, b)[c]
                m = plan.chunk0[i] + c
                if m >= 2:
                    pe.wait_ge(piece_read, m - 1)
                ps = lbank[m % 2]
                if kind == "B":
                    spans = [(0, n, kb[:, o:o + n])]
                else:
                    spans = [(j * P, P, ka[:, g, t % 4, :]) for j, t in enumerate(key_tiles(kind, b))]
                for at, width, keys in spans:
                    out = ps[:, at:at + width]
                    nc.tensor.matmul(out, q_hi[kind][:, h, :], keys, start=True, stop=False)
                    nc.tensor.matmul(out, q_lo[kind][:, h, :], keys, start=False, stop=False)
                    mm = nc.tensor.matmul(out, slope_id[:, h, :], bias_of(kind, b, o, n)[:, at:at + width],
                                          start=False, stop=True)
                mm.then_inc(piece_full, 1)

            def transpose_group(i, g):
                tiles = plan.groups(i)[g]
                t = plan.group0[i] + g
                if g == 0:
                    pe.wait_ge(exp_done, i + 1)
                if t >= 2:
                    pe.wait_ge(pt_ready, t - 1)
                for j in range(len(tiles)):
                    c = (4 * g + j) * P
                    mm = nc.tensor.transpose(tbank[t % 2][:, j * P:(j + 1) * P], prob[:, i % 2, c:c + P], ident[:])
                mm.then_inc(pt_full, 1)

            def weighted_values(i, g):
                kind, b, h = plan.heads[i]
                tiles = plan.groups(i)[g]
                last = g == len(plan.groups(i)) - 1
                t = plan.group0[i] + g
                pe.wait_ge(pt_ready, t + 1)
                o = OUT_ORDER.index((kind, b))
                if g == 0 and h == 0 and o >= 2:
                    pe.wait_ge(o_copied, o - 1)
                for j, kt in enumerate(tiles):
                    v = vb[:, kt, :] if kind == "B" else va[:, kt % 4, HD * (h // 4):HD * (h // 4 + 1)]
                    mm = nc.tensor.matmul(obank[o % 2][:, h * HD:(h + 1) * HD], probT[:, t % 2, j * P:(j + 1) * P], v,
                                          start=(g == 0 and j == 0), stop=(last and j == len(tiles) - 1))
                mm.then_inc(pv_done, 1)

            def turn_output(i):
                kind, b, h = plan.heads[i]
                if h < HEADS - 1:
                    return
                o = OUT_ORDER.index((kind, b))
                pe.wait_ge(o_scaled, o + 1)
                for j in range(4):
                    mm = nc.tensor.transpose(obank[o % 2][:, j * P:(j + 1) * P],
                                             o_norm[:, 2 * j:2 * j + 2, :].rearrange("p h d -> p (h d)"), ident[:])
                mm.then_inc(o_turned, 1)

            def head(i):
                n = len(plan.heads)
                pieces = len(key_chunks(*plan.heads[i][0:2])) if i < n else 0
                groups = len(plan.groups(i - 2)) if 2 <= i < n + 2 else 0
                for c in range(max(pieces, groups, 1)):
                    if c < pieces:
                        piece(i, c)
                    if c < groups:
                        transpose_group(i - 2, c)
                    if c == 0 and 3 <= i < n + 3:
                        weighted_values(i - 3, len(plan.groups(i - 3)) - 1)
                    if 1 <= c < groups:
                        weighted_values(i - 2, c - 1)
                if i >= 4:
                    turn_output(i - 4)

            pe.wait_ge(weights_in, 16 * N_W)
            pe.wait_ge(dist_made, 2)
            pe.wait_ge(consts, N_CONST)
            i = 0
            for s in plan.steps:
                if s[0] == "transposes":
                    transposes(s)
                elif s[0] == "proj":
                    proj(s)
                elif s[0] == "latent":
                    latent(s)
                elif s[0] == "latent_up":
                    latent_up(s)
                elif s[0] == "queries":
                    queries(s)
                elif s[0] == "scores":
                    scores(s)
                elif s[0] == "head":
                    head(i)
                    i += 1
            for j in range(4):
                head(i + j)

        @block.scalar
        def _(act):
            def copy_out(out, src, scale=1.0):
                nc.scalar.activation(out, src, ACT.Copy, scale=scale).then_inc(work_free, 1)

            def pairs(ap):
                return ap.rearrange("p (j t) -> p j t", t=P)

            def norm(s):
                b = s[1]
                act.wait_ge(x_loaded, 16 * (b + 1))
                if b:
                    act.wait_ge(lat_rstd, b)
                    act.wait_ge(work_full, plan.work0["proj", b - 1, 4] + 1)
                nc.scalar.activation(squares, x_in[:], ACT.Square, accum_out=ssq[:, 0:1]).then_inc(x_ssq, 1)

            def transposes(s):
                u = plan.work0[s]
                for half in range(2):
                    act.wait_ge(work_full, u + half + 1)
                    copy_out(h_T[:, 4 * half:4 * half + 4, :], pairs(work[(u + half) % 2][:]))

            def proj(s):
                _, b, part = s
                if part == 0 or part == 2:
                    return
                c = part // 2
                u = plan.work0["proj", b, 2 * c]
                if c == 0:
                    if b:
                        act.wait_ge(lat_ready, 2 * b)
                        act.wait_ge(work_full, plan.work0["queries", "A", b - 1] + 1)
                act.wait_ge(work_full, u + 1)
                n0, n1 = c * BANK, min((c + 1) * BANK, D_IN)
                copy_out(pj[:, n0:n1], work[u % 2][:, 0:n1 - n0])
                if c < 2:
                    return
                act.wait_ge(work_free, u + 1)
                nc.scalar.activation(squares[:, 0:Q_RANK], pj[:, C_CQ:C_CQ + Q_RANK], ACT.Square,
                                     accum_out=ssq[:, 1:2]).then_inc(act_step, 1)
                act.wait_ge(act_step, b + 1)
                nc.scalar.activation(squares[:, 0:KV_RANK], pj[:, C_CKV:C_CKV + KV_RANK], ACT.Square,
                                     accum_out=ssq[:, 2:3]).then_inc(lat_ssq, 1)
                nc.scalar.activation(kk[:, 0:2, :, :],
                                     pj[:, C_KA:C_KA + P].rearrange("p (g d) -> p g d", g=2).unsqueeze(2)
                                     .to_broadcast([P, 2, 2, HD]), ACT.Copy).then_inc(key_twice, 1)
                nc.scalar.activation(kk[:, 2, :, :], pj[:, C_KI:C_KI + HD].unsqueeze(1).to_broadcast([P, 2, HD]),
                                     ACT.Copy).then_inc(key_twice, 1)

            def latent(s):
                b = s[1]
                u = plan.work0[s]
                v = plan.split0[s]
                if b >= 4:
                    act.wait_ge(pv_done, plan.group0[plan.head_no["A", b - 3, HEADS - 1] + 1])
                nc.scalar.activation(va[:, b % 4, :], pj[:, C_VA:C_VA + P], ACT.Copy)
                if ("scores", b - 2) in plan.work0:
                    act.wait_ge(relu_used, plan.score0[b - 2] + IDX_HEADS * len(key_chunks("B", b - 2)))
                nc.scalar.activation(widx[:, b % 2, :], pj[:, C_WI:C_WI + IDX_HEADS], ACT.Copy, scale=IDX_SCALE)
                act.wait_ge(work_full, u + 1)
                if v:
                    act.wait_ge(split_done, v)
                ps = work[u % 2]
                keys = ps[:, 0:3 * P]
                nc.scalar.activation(ka[0:HD, :, b % 4, :], pairs(keys[0:HD, 0:2 * P]), ACT.Copy)
                nc.scalar.activation(ki[0:HD, b * P:(b + 1) * P], keys[0:HD, 2 * P:], ACT.Copy)
                nc.scalar.activation(k_hi[HD:P, 0:3, :], pairs(keys[HD:P, :]), ACT.Copy)
                nc.scalar.activation(raw[HD:P, 0:3, :], pairs(keys[HD:P, :]), ACT.Copy).then_inc(raw_ready, 1)
                copy_out(latT[:, b % 2, 2, :], ps[:, 3 * P:4 * P])
                act.wait_ge(work_full, u + 2)
                copy_out(latT[:, b % 2, 0:2, :], pairs(work[(u + 1) % 2][:, 0:2 * P]))

            def latent_up(s):
                b = s[1]
                u = plan.work0[s]
                act.wait_ge(work_full, u + 1)
                ps = work[u % 2]
                act.wait_ge(split_done, plan.split0[s])
                nc.scalar.activation(kb[0:HD, b * P:(b + 1) * P], ps[0:HD, 2 * P:3 * P], ACT.Copy)
                nc.scalar.activation(k_hi[HD:P, 0, :], ps[HD:P, 2 * P:3 * P], ACT.Copy)
                nc.scalar.activation(raw[HD:P, 2, :], ps[HD:P, 2 * P:3 * P], ACT.Copy)
                high_twice(qi_hi, pairs(ps[:, 0:2 * P]), 1.0)
                nc.scalar.activation(raw[:, 0:2, :], pairs(ps[:, 0:2 * P]), ACT.Copy).then_inc(raw_ready, 1)
                copy_out(vb[:, b, :], ps[:, 3 * P:3 * P + HD])

            def high_twice(dst, src, scale):
                for r in range(2):
                    for half in range(2):
                        nc.scalar.activation(dst[half * HD:(half + 1) * HD, r::2, :], src[r * HD:(r + 1) * HD],
                                             ACT.Copy, scale=scale)

            def queries(s):
                _, kind, b = s
                u = plan.work0[s]
                act.wait_ge(work_full, u + 1)
                act.wait_ge(split_done, plan.split0[s])
                if b:
                    act.wait_ge(piece_full, plan.last_piece(kind, b - 1))
                src = pairs(work[u % 2][:])
                high_twice(q_hi[kind], src, SCALE)
                copy = nc.scalar.activation(raw[:], src, ACT.Copy, scale=SCALE)
                copy.then_inc(raw_ready, 1)
                act.wait_ge(raw_ready, RAW_COUNT[s])
                act.sem_inc(work_free, 1)

            def scores(s):
                b = s[1]
                u = plan.work0[s]
                r = plan.score0[b]
                for o, n in key_chunks("B", b):
                    for h in range(IDX_HEADS):
                        act.wait_ge(work_full, u + 1)
                        if r >= 2:
                            act.wait_ge(relu_used, r - 1)
                        nc.scalar.activation(relu[:, r % 2, 0:n], work[u % 2][:, 0:n], ACT.Relu).then_inc(work_free, 1)
                        u += 1
                        r += 1

            def exponent(i):
                kind, b, h = plan.heads[i]
                n = P * len(key_tiles(kind, b)) + (kind == "A")
                act.wait_ge(max_ready, i + 1)
                if i >= 2:
                    act.wait_ge(pt_full, plan.group0[i - 1])
                o = OUT_ORDER.index((kind, b))
                if h == 0 and o >= 2:
                    act.wait_ge(o_scaled, o - 1)
                nc.scalar.activation(prob[:, i % 2, 0:n], logit[:, i % 2, 0:n], ACT.Exp,
                                     bias=negmax[:, i % 4:i % 4 + 1],
                                     accum_out=total[:, o % 2, h:h + 1]).then_inc(exp_done, 1)

            def copy_transposed(i, first):
                for g, tiles in enumerate(plan.groups(i)):
                    if (g < 2) != first:
                        continue
                    t = plan.group0[i] + g
                    n = P * len(tiles)
                    act.wait_ge(pt_full, t + 1)
                    if t >= 2:
                        act.wait_ge(pv_done, t - 1)
                    nc.scalar.activation(probT[:, t % 2, 0:n], tbank[t % 2][:, 0:n], ACT.Copy).then_inc(pt_ready, 1)

            def copy_output(i):
                kind, b, h = plan.heads[i]
                if h < HEADS - 1:
                    return
                o = OUT_ORDER.index((kind, b))
                act.wait_ge(o_turned, o + 1)
                if o:
                    act.wait_ge(o_stored, 16 * o)
                nc.scalar.activation(oT[:], pairs(obank[o % 2][:]), ACT.Copy).then_inc(o_copied, 1)

            def head(i):
                n = len(plan.heads)
                if i >= 5:
                    copy_output(i - 5)
                if 2 <= i < n + 2:
                    copy_transposed(i - 2, True)
                if 1 <= i <= n:
                    exponent(i - 1)
                if 2 <= i < n + 2:
                    copy_transposed(i - 2, False)

            act.wait_ge(weights_in, 16 * N_W)
            i = 0
            for s in engine_order("scalar"):
                if s[0] == "norm":
                    norm(s)
                elif s[0] == "transposes":
                    transposes(s)
                elif s[0] == "proj":
                    proj(s)
                elif s[0] == "latent":
                    latent(s)
                elif s[0] == "latent_up":
                    latent_up(s)
                elif s[0] == "queries":
                    queries(s)
                elif s[0] == "scores":
                    scores(s)
                elif s[0] == "head":
                    head(i)
                    i += 1
            for j in range(5):
                head(i + j)

        @block.vector
        def _(dve):
            step = [0]

            def link(ins, between=None):
                step[0] += 1
                done = step[0]
                ins.then_inc(dve_step, 1)
                if between:
                    between()
                dve.wait_ge(dve_step, done)

            def norm(s):
                b = s[1]
                dve.wait_ge(x_rstd, b + 1)
                nc.vector.scalar_tensor_tensor(x_in[:], x_in[:], rstd[:, 0:1], pre[:, 0, :],
                                               ALU.mult, ALU.mult).then_inc(h_scaled, 1)

            def gains(s):
                b = s[1]
                dve.wait_ge(work_free, plan.work0["proj", b, 4] + 1)
                dve.wait_ge(lat_rstd, b + 1)
                nc.vector.scalar_tensor_tensor(lat[:, 0:Q_RANK], pj[:, C_CQ:C_CQ + Q_RANK], rstd[:, 1:2], gq[:],
                                               ALU.mult, ALU.mult).then_inc(lat_ready, 1)
                nc.vector.scalar_tensor_tensor(lat[:, Q_RANK:], pj[:, C_CKV:C_CKV + KV_RANK], rstd[:, 2:3], gkv[:],
                                               ALU.mult, ALU.mult).then_inc(lat_ready, 1)

            def latent(s):
                b = s[1]
                dve.wait_ge(raw_ready, RAW_COUNT[s])
                low(ka[HD:P, :, b % 4, :], raw[HD:P, 0:2, :], k_hi[HD:P, 0:2, :])
                low(ki[HD:P, b * P:(b + 1) * P], raw[HD:P, 2, :], k_hi[HD:P, 2, :])

            def latent_up(s):
                b = s[1]
                dve.wait_ge(raw_ready, RAW_COUNT[s])
                low(kb[HD:P, b * P:(b + 1) * P], raw[HD:P, 2, :], k_hi[HD:P, 0, :])
                for r in range(2):
                    low(qi_lo[0:HD, r::2, :], raw[r * HD:(r + 1) * HD, 0:2, :], qi_hi[r * HD:(r + 1) * HD, r::2, :])

            def low(dst, whole, high):
                nc.vector.tensor_tensor(dst, whole, high.bitcast(F32), ALU.subtract).then_inc(split_done, 1)

            def queries(s):
                kind = s[1]
                dve.wait_ge(raw_ready, RAW_COUNT[s])
                for r in range(2):
                    low(q_lo[kind][0:HD, r::2, :], raw[r * HD:(r + 1) * HD],
                        q_hi[kind][r * HD:(r + 1) * HD, r::2, :])

            def scores(s):
                b = s[1]
                r = plan.score0[b]
                u = plan.work0[s]
                for o, n in key_chunks("B", b):
                    for h in range(IDX_HEADS):
                        dve.wait_ge(work_free, u + 1)
                        wh = widx[:, b % 2, h:h + 1]
                        if h == 0:
                            ins = nc.vector.tensor_scalar(score[:, o:o + n], relu[:, r % 2, 0:n], wh, None, ALU.mult)
                        else:
                            ins = nc.vector.scalar_tensor_tensor(score[:, o:o + n], relu[:, r % 2, 0:n], wh,
                                                                 score[:, o:o + n], ALU.mult, ALU.add)
                        ins.then_inc(relu_used, 1)
                        r += 1
                        u += 1
                        dve.wait_ge(relu_used, r)
                L = P * (b + 1)
                link(nc.vector.memset(score[0:CHUNK, L - CHUNK:L], LOWEST))
                link(nc.vector.memset(cand[:], 0))

            def reached(b, values, threshold, between):
                L = P * (b + 1)
                link(nc.vector.tensor_scalar(above[:, 0:L], values[:, 0:L], threshold, None,
                                             ALU.is_ge, ALU.add, accum_out=count[:]), between)

            def search(b, action, between):
                L = P * (b + 1)
                fcand = cand[:].bitcast(F32)
                what, j = action[0], action[-1]
                if what in ("whole", "high"):
                    reached(b, score if what == "whole" else short, fcand, between)
                    bit = -1.0 if j == 0 else 2.0 ** (31 - j)
                    following = 0 if j == 15 else 1 << (30 - j)
                    link(nc.vector.tensor_scalar(reject[:], count[:], float(TOPK), bit, ALU.is_lt, ALU.mult))
                    link(nc.vector.scalar_tensor_tensor(cand[:], cand[:], following, reject[:],
                                                        ALU.bitwise_xor, ALU.bitwise_xor))
                elif what == "shorten":
                    link(nc.vector.tensor_copy(short[:, 0:L], score[:].bitcast(BF16)[:, 1:2 * L:2]), between)
                elif what == "rebase":
                    link(nc.vector.tensor_scalar(above_it[:], cand[:], 1, None, ALU.bitwise_xor))
                    link(nc.vector.tensor_tensor(unit[:], above_it[:].bitcast(F32), fcand, ALU.subtract))
                    link(nc.vector.tensor_scalar(digit[:], powers[:], unit[:], None, ALU.mult))
                    link(nc.vector.tensor_scalar(score[:, 0:L], score[:, 0:L], fcand, None, ALU.subtract),
                         between)
                    link(nc.vector.tensor_copy(fcand, digit[:, 0:1]))
                elif what == "low":
                    reached(b, short, fcand, between)
                    following = 16 if j in (7, 15) else j + 1
                    link(nc.vector.scalar_tensor_tensor(reject[:].bitcast(F32), count[:], float(TOPK),
                                                        digit[:, j:j + 1], ALU.is_lt, ALU.mult))
                    link(nc.vector.scalar_tensor_tensor(fcand, fcand, digit[:, following:following + 1],
                                                        reject[:].bitcast(F32), ALU.add, ALU.subtract))
                elif what == "last_digits":
                    link(nc.vector.tensor_scalar(short[:, 0:L], score[:, 0:L], fcand, None, ALU.subtract),
                         between)
                    link(nc.vector.tensor_copy(fcand, digit[:, 8:9]))
                else:
                    ties(b, j)
                    between()

            def ties(b, part):
                L = P * (b + 1)
                thr = cand[:].bitcast(F32)
                if part == 0:
                    nc.vector.tensor_scalar(equal[:, 0:L], short[:, 0:L], thr, None, ALU.is_equal)
                    link(nc.vector.tensor_scalar(above[:, 0:L], short[:, 0:L], thr, None,
                                                 ALU.is_lt, ALU.add, accum_out=count[:]))
                    link(nc.vector.tensor_tensor_scan(rank[:, 0:L], equal[:, 0:L], equal[:, 0:L], 0.0,
                                                      ALU.add, ALU.max))
                    link(nc.vector.scalar_tensor_tensor(need[:], rank[:, L - 1:L], float(TOPK - L), count[:],
                                                        ALU.add, ALU.add))
                    return
                link(nc.vector.scalar_tensor_tensor(equal[:, 0:L], rank[:, 0:L], need[:], equal[:, 0:L],
                                                    ALU.is_gt, ALU.mult))
                link(nc.vector.tensor_tensor(above[:, 0:L], above[:, 0:L], equal[:, 0:L], ALU.add))
                if b > 2:
                    dve.wait_ge(piece_full, plan.last_piece("B", b - 1))
                nc.vector.scalar_tensor_tensor(bias_b[:, 0:L], above[:, 0:L], -BIG, ndist[:, T - L:],
                                               ALU.mult, ALU.add).then_inc(bias_ready, 1)

            def copy_piece(i, c):
                kind, b, h = plan.heads[i]
                o, n = key_chunks(kind, b)[c]
                m = plan.chunk0[i] + c
                if c == 0 and i >= 2:
                    dve.wait_ge(exp_done, i - 1)
                    dve.wait_ge(max_ready, i - 1)
                dve.wait_ge(piece_full, m + 1)
                nc.vector.tensor_scalar(logit[:, i % 2, o:o + n], lbank[m % 2][:, 0:n], 1.0, None,
                                        ALU.mult, ALU.max, accum_out=mx[:, i % 2, c:c + 1]).then_inc(piece_read, 1)

            def maximum(i):
                kind, b, h = plan.heads[i]
                cols = len(key_chunks(kind, b))
                if kind == "A":
                    L = P * len(key_tiles(kind, b))
                    nc.vector.tensor_copy(logit[:, i % 2, L:L + 1], sink[:, h:h + 1])
                    link(nc.vector.tensor_copy(mx[:, i % 2, cols:cols + 1], sink[:, h:h + 1]))
                    cols += 1
                dve.wait_ge(piece_read, plan.chunk0[i + 1])
                nc.vector.tensor_reduce(negmax[:, i % 4:i % 4 + 1], mx[:, i % 2, 0:cols], AX.X, ALU.max,
                                        negate=True).then_inc(max_ready, 1)

            def scale_output(i):
                kind, b, h = plan.heads[i]
                if h < HEADS - 1:
                    return
                o = OUT_ORDER.index((kind, b))
                dve.wait_ge(pv_done, plan.group0[i + 1])
                link(nc.vector.reciprocal(rtotal[:], total[:, o % 2, :]))
                if o:
                    dve.wait_ge(o_turned, o)
                nc.vector.tensor_tensor(o_norm[:], obank[o % 2][:].rearrange("p (h d) -> p h d", d=HD),
                                        rtotal[:].unsqueeze(2).to_broadcast([P, HEADS, HD]),
                                        ALU.mult).then_inc(o_scaled, 1)

            def own_work(i, pieces, begin, end):
                for part in range(begin, end):
                    if part < pieces:
                        copy_piece(i, part)
                    elif part == pieces:
                        maximum(i)
                    elif i >= 3:
                        scale_output(i - 3)

            dve.wait_ge(weights_in, 16 * N_W)
            for t in (*q_lo.values(), qi_lo):
                nc.vector.memset(t[HD:P, :, :].bitcast(F32), 0.0).then_inc(consts, 1)
            dve.wait_ge(dist_made, 2)
            link(nc.vector.tensor_scalar(logit[:, 0, 0:T], score[:], -1.0, None, ALU.mult))
            link(nc.vector.tensor_tensor(score[:], score[:], logit[:, 0, 0:T], ALU.min))
            nc.vector.tensor_copy(ndist[:], score[:]).then_inc(consts, 1)
            link(nc.vector.tensor_copy(bias_a[:], score[:, T - 2 * P:]))
            link(nc.vector.tensor_copy(bias_v[:], score[:, T - 2 * P:]))
            nc.vector.memset(bias_a[CHUNK:P, 0:P].bitcast(F32), -BIG).then_inc(consts, 1)
            nc.vector.memset(bias_a[0:CHUNK, 0:CHUNK].bitcast(F32), -BIG).then_inc(consts, 1)
            nc.vector.memset(bias_a[0:CHUNK, 2 * P - CHUNK:].bitcast(F32), -BIG).then_inc(consts, 1)
            nc.vector.memset(bias_v[0:CHUNK, 2 * P - CHUNK:].bitcast(F32), -BIG).then_inc(consts, 1)
            for k in range(17):
                nc.vector.memset(powers[:, k:k + 1], 2.0 ** (15 - k) if k < 16 else 0.0).then_inc(consts, 1)
            for h in range(HEADS):
                nc.vector.tensor_scalar(slope_id[:, h, :], ident[:], SLOPES[h], None, ALU.mult).then_inc(consts, 1)
            dve.wait_ge(consts, N_CONST)
            i = 0
            for s in engine_order("vector"):
                if s[0] == "norm":
                    norm(s)
                elif s[0] == "gains":
                    gains(s)
                elif s[0] == "latent":
                    latent(s)
                elif s[0] == "latent_up":
                    latent_up(s)
                elif s[0] == "queries":
                    queries(s)
                elif s[0] == "scores":
                    scores(s)
                elif s[0] == "head":
                    kind, b, h, chosen, actions = s[1:]
                    pieces = len(key_chunks(kind, b))
                    last = [] if not chosen or actions[-1] < len(SEARCH) - 1 else [actions[-1]]
                    actions = actions[0:len(actions) - len(last)] if chosen else []
                    parts = pieces + 2
                    done = 0
                    for k, n in enumerate(actions):
                        upto = parts * (k + 1) // len(actions)
                        search(chosen, SEARCH[n], lambda: own_work(i, pieces, done, upto))
                        done = upto
                    own_work(i, pieces, done, parts)
                    for n in last:
                        search(chosen, SEARCH[n], lambda: None)
                    i += 1
            for j in range(3):
                scale_output(i + j - 3)


def raw_counts():
    out, n = {}, 0
    for s in mixing_steps()[0]:
        n += s[0] in SPLITS
        out[s] = n
    return out


RAW_COUNT = raw_counts()
OUT_ORDER = [("A", 0)] + [o for b in range(NB) for o in (("A", b + 1), ("B", b)) if o[1] < NB]
N_CONST = 25 + HEADS


def project_output(nc, w):
    with ExitStack() as ctx:
        def sb(name, shape, dt=F32):
            return ctx.enter_context(nc.sbuf_tensor(name, shape, dt))

        def psum(name, shape):
            return ctx.enter_context(nc.psum_tensor(name, shape, F32))

        def sem(name):
            return ctx.enter_context(nc.semaphore(name))

        wo = sb("wo", [P, KD, D])
        wo_hi = sb("wo_hi", [P, KD, D], F32R)
        wo_lo = sb("wo_lo", [P, KD, D], F32R)
        rows = sb("rows", [P, 3, D])
        mix = sb("mix", [P, 2, KD, P])
        mix_hi = sb("mix_hi", [P, 2, KD, P], F32R)
        mix_lo = sb("mix_lo", [P, 2, KD, P], F32R)
        x = sb("x_rows", [P, 2, D])
        x1 = sb("x1_rows", [P, 2, D])
        h2 = sb("h2", [P, 2, D])
        h2T = sb("h2T_tile", [P, 2, KD, P])
        junk = sb("junk", [P, D], BF16)
        ident = sb("ident2", [P, P])
        cols = sb("cols", [P, 3])
        ssq = sb("ssq2", [P, 2, 2])
        rstd = sb("rstd2", [P, 2, 2])
        pbank = [psum("pbank0", [P, D]), psum("pbank1", [P, D])]
        tbank = [psum("turn0", [P, KD, P]), psum("turn1", [P, KD, P])]

        consts = sem("p_consts")
        rows_in = sem("rows_in")
        wo_in = [sem("wo_in%d" % k) for k in range(KD)]
        wo_high = sem("wo_high")
        wo_split = sem("wo_split")
        mix_in = [sem("mix_in0"), sem("mix_in1")]
        mix_high = sem("mix_high")
        mix_split = sem("mix_split")
        x_in = [sem("x_in0"), sem("x_in1")]
        product_done = sem("product_done")
        square_done = sem("square_done")
        root_done = sem("root_done")
        scaled = sem("scaled")
        x1_made = sem("x1_made")
        h2_scaled = sem("h2_scaled")
        h2_made = sem("h2_made")
        turned = sem("turned")
        h2T_made = sem("h2T_made")
        x1_stored = [sem("x1_stored0"), sem("x1_stored1")]
        h2T_stored = [sem("h2T_stored0"), sem("h2T_stored1")]
        pool_step = sem("p_pool_step")
        block = ctx.enter_context(nc.Block())


        @block.sync
        def _(sp):
            mixT = w["mixT"].rearrange("(k p) t -> p k t", p=P)
            h2T_dram = w["h2T"].rearrange("(k p) t -> p k t", p=P)

            def load_mix(t, s):
                sp.dma_start(mix[:, s], mixT[:, :, bass.ts(t, P)]).then_inc(mix_in[s], 16)

            def load_x(t, s):
                sp.dma_start(x[:, s], w["x"][bass.ts(t, P), :]).then_inc(x_in[s], 16)

            def store_h2T(n, s):
                sp.wait_ge(h2T_made, n + 3)
                sp.dma_start(h2T_dram[:, :, bass.ts(n, P)], h2T[:, s]).then_inc(h2T_stored[s], 16)

            def tile(j, s, more):
                t = 2 * j + s
                if more:
                    sp.wait_ge(mix_split, t + 1)
                    load_mix(t + 2, s)
                sp.wait_ge(x1_made, t + 1)
                sp.dma_start(w["x1"][bass.ts(t, P), :], x1[:, s]).then_inc(x1_stored[s], 16)
                if more:
                    load_x(t + 2, s)
                if not isinstance(j, int) or j > 0:
                    store_h2T(t - 2, s)

            nc.sync.sem_inc(h2T_stored[0], 16)
            nc.sync.sem_inc(h2T_stored[1], 16)
            load_mix(0, 0)
            for k in range(KD):
                sp.dma_start(wo[:, k, :], w["w_o"][k * P:(k + 1) * P, :]).then_inc(wo_in[k], 16)
            load_mix(1, 1)
            for i, r in enumerate((2, 3, 4)):
                sp.dma_start(rows[:, i, :], w["mods"][r:r + 1, :].partition_broadcast(P)).then_inc(rows_in, 16)
            load_x(0, 0)
            load_x(1, 1)
            for s in range(2):
                tile(0, s, True)
            with sp.Fori(1, NB // 2 - 1) as j:
                for s in range(2):
                    tile(j, s, True)
            for s in range(2):
                tile(NB // 2 - 1, s, False)
            for s in range(2):
                store_h2T(NB - 2 + s, s)
            for s in range(2):
                sp.wait_ge(x1_stored[s], 16 * NB // 2)
                sp.wait_ge(h2T_stored[s], 16 + 16 * NB // 2)

        @block.gpsimd
        def _(pool):
            nc.gpsimd.memset(ident[:], 0.0).then_inc(pool_step, 1)
            for j, v in enumerate((-0.5, 1.0 / D, EPS)):
                nc.gpsimd.memset(cols[:, j:j + 1], v).then_inc(pool_step, 1)
            pool.wait_ge(pool_step, 4)
            nc.gpsimd.affine_select(out=ident[:], in_=ident[:], compare_op=ALU.not_equal, fill=1.0, base=0,
                                    pattern=[[-1, P]], channel_multiplier=1).then_inc(consts, 1)
            with pool.Fori(0, NB // 2) as j:
                for s in range(2):
                    for i in range(2):
                        n = 4 * j + 2 * s + i
                        pool.wait_ge(square_done, n + 1)
                        root = rstd[:, s, i:i + 1]
                        nc.gpsimd.tensor_tensor(root, ssq[:, s, i:i + 1], cols[:, 1:2], ALU.mult
                                                ).then_inc(pool_step, 1)
                        pool.wait_ge(pool_step, 2 * n + 5)
                        nc.gpsimd.tensor_tensor(root, root, cols[:, 2:3], ALU.add).then_inc(pool_step, 1)
                        pool.wait_ge(pool_step, 2 * n + 6)
                        nc.gpsimd.tensor_tensor(root, root, cols[:, 0:1], ALU.pow).then_inc(root_done, 1)

        @block.tensor
        def _(pe):
            def turn(n, s):
                pe.wait_ge(h2_made, n + 1)
                pe.wait_ge(h2T_made, n + 1)
                for k in range(KD):
                    mm = nc.tensor.transpose(tbank[s][:, k, :], h2[:, s, k * P:(k + 1) * P], ident[:])
                mm.then_inc(turned, 1)

            def tile(j, s):
                t = 2 * j + s
                peeled = isinstance(j, int)
                pe.wait_ge(mix_split, t + 1)
                if not peeled:
                    pe.wait_ge(scaled, t - 1)
                for k in range(KD):
                    if peeled and s == 0:
                        pe.wait_ge(wo_split, k + 1)
                    for half in range(2):
                        out = pbank[s][:, half * BANK:(half + 1) * BANK]
                        wh = wo_hi[:, k, half * BANK:(half + 1) * BANK]
                        wl = wo_lo[:, k, half * BANK:(half + 1) * BANK]
                        nc.tensor.matmul(out, mix_hi[:, s, k, :], wh, start=(k == 0), stop=False)
                        nc.tensor.matmul(out, mix_hi[:, s, k, :], wl, start=False, stop=False)
                        mm = nc.tensor.matmul(out, mix_lo[:, s, k, :], wh, start=False, stop=(k == KD - 1))
                mm.then_inc(product_done, 1)
                if not peeled:
                    turn(t - 2, s)

            pe.wait_ge(consts, 1)
            for s in range(2):
                tile(0, s)
            with pe.Fori(1, NB // 2) as j:
                for s in range(2):
                    tile(j, s)
            for s in range(2):
                turn(NB - 2 + s, s)

        @block.scalar
        def _(act):
            def high(j, s):
                t = 2 * j + s
                act.wait_ge(mix_in[s], 16 * (j + 1))
                if not isinstance(t, int) or t >= 2:
                    act.wait_ge(product_done, t - 1)
                nc.scalar.activation(mix_hi[:, s], mix[:, s], ACT.Copy).then_inc(mix_high, 1)

            def square(i, t, s, src):
                n = 2 * t + i
                if not isinstance(n, int) or n > 0:
                    act.wait_ge(square_done, n)
                nc.scalar.activation(junk[:], src, ACT.Square, accum_out=ssq[:, s, i:i + 1]
                                     ).then_inc(square_done, 1)

            def copy_turned(n, j, s):
                act.wait_ge(turned, n + 1)
                act.wait_ge(h2T_stored[s], 16 * j)
                nc.scalar.activation(h2T[:, s], tbank[s][:], ACT.Copy).then_inc(h2T_made, 1)

            def tile(j, s, more):
                t = 2 * j + s
                if more:
                    high(j + s, 1 - s)
                act.wait_ge(product_done, t + 1)
                square(0, t, s, pbank[s][:])
                if not isinstance(j, int) or j > 0:
                    copy_turned(t - 2, j, s)
                act.wait_ge(x1_made, t + 1)
                square(1, t, s, x1[:, s])

            nc.scalar.sem_inc(h2T_made, 2)
            high(0, 0)
            for k in range(KD):
                act.wait_ge(wo_in[k], 16)
                nc.scalar.activation(wo_hi[:, k, :], wo[:, k, :], ACT.Copy).then_inc(wo_high, 1)
            for s in range(2):
                tile(0, s, True)
            with act.Fori(1, NB // 2 - 1) as j:
                for s in range(2):
                    tile(j, s, True)
            for s in range(2):
                tile(NB // 2 - 1, s, s == 0)
            for s in range(2):
                copy_turned(NB - 2 + s, NB // 2, s)

        @block.vector
        def _(dve):
            def low(t, s):
                dve.wait_ge(mix_high, t + 1)
                nc.vector.tensor_tensor(mix_lo[:, s], mix[:, s], mix_hi[:, s].bitcast(F32), ALU.subtract
                                        ).then_inc(mix_split, 1)

            def tile(j, s, more):
                t = 2 * j + s
                if more:
                    low(t + 1, 1 - s)
                dve.wait_ge(root_done, 2 * t + 1)
                if not isinstance(j, int) or j > 0:
                    dve.wait_ge(x1_stored[s], 16 * j)
                    dve.wait_ge(turned, t - 1)
                nc.vector.scalar_tensor_tensor(x1[:, s], pbank[s][:], rstd[:, s, 0:1], rows[:, 0, :],
                                               ALU.mult, ALU.mult).then_inc(scaled, 1)
                dve.wait_ge(scaled, t + 1)
                dve.wait_ge(x_in[s], 16 * (j + 1))
                nc.vector.tensor_tensor(x1[:, s], x1[:, s], x[:, s], ALU.add).then_inc(x1_made, 1)
                dve.wait_ge(root_done, 2 * t + 2)
                nc.vector.scalar_tensor_tensor(h2[:, s], x1[:, s], rstd[:, s, 1:2], rows[:, 1, :],
                                               ALU.mult, ALU.mult).then_inc(h2_scaled, 1)
                dve.wait_ge(h2_scaled, t + 1)
                nc.vector.tensor_tensor(h2[:, s], h2[:, s], rows[:, 2, :], ALU.add).then_inc(h2_made, 1)

            low(0, 0)
            for k in range(KD):
                dve.wait_ge(wo_high, k + 1)
                nc.vector.tensor_tensor(wo_lo[:, k, :], wo[:, k, :], wo_hi[:, k, :].bitcast(F32), ALU.subtract
                                        ).then_inc(wo_split, 1)
            dve.wait_ge(rows_in, 16 * 3)
            for s in range(2):
                tile(0, s, True)
            with dve.Fori(1, NB // 2 - 1) as j:
                for s in range(2):
                    tile(j, s, True)
            for s in range(2):
                tile(NB // 2 - 1, s, s == 0)


def ffn(nc, w):
    HALF = D // 2
    UP = 2 * KF
    DOWN = KF // 2
    PANELS = UP + 2 * DOWN
    with ExitStack() as ctx:
        def sb(name, shape, dt=F32):
            return ctx.enter_context(nc.sbuf_tensor(name, shape, dt))

        def psum(name, shape):
            return ctx.enter_context(nc.psum_tensor(name, shape, F32))

        def sem(name):
            return ctx.enter_context(nc.semaphore(name))

        x_hi = sb("x_hi", [P, KD, TOK], F32R)
        x_lo = sb("x_lo", [P, KD, TOK], F32R)
        a_hi = sb("a_hi", [P, KF, TOK], F32R)
        a_lo = sb("a_lo", [P, KF, TOK], F32R)
        raw = sb("raw", [P, 2, D])
        p_hi = sb("p_hi", [P, 2, D], F32R)
        p_lo = sb("p_lo", [P, 2, D], F32R)
        row = sb("row", [P, D])
        x1 = sb("x1_in", [P, 2, D])
        out = sb("out_rows", [P, 2, D])
        first_half = sb("first_half", [P, TPC, HALF])
        cols = sb("cols3", [P, 3, TPC])
        ssq = sb("ssq3", [P, 2, TPC])
        rstd = sb("rstd3", [P, TPC])
        th = sb("th", [P, 2, TOK])
        act32 = sb("act32", [P, 2, TOK])
        junk = sb("junk3", [P, HALF], BF16)

        gbank = [psum("gbank0", [P, TOK]), psum("gbank1", [P, TOK])]
        ubank = [psum("ubank0", [P, TOK]), psum("ubank1", [P, TOK])]
        dbank = [psum("dbank%d" % t, [P, HALF]) for t in range(TPC)]

        row_in = sem("row_in")
        x_loaded = sem("f_x_loaded")
        x_high = sem("x_high")
        x_split = sem("x_split")
        raw_in = [sem("raw_in0"), sem("raw_in1")]
        raw_given = sem("raw_given")
        panel_used = sem("panel_used")
        panel_high = sem("panel_high")
        panel_ready = sem("panel_ready")
        tanh_done = sem("tanh_done")
        gated = sem("gated")
        act_made = sem("act_made")
        act_high = sem("act_high")
        act_ready = sem("act_ready")
        half_copied = sem("half_copied")
        square_done = sem("f_square_done")
        root_done = sem("f_root_done")
        x1_in = [sem("x1_in0"), sem("x1_in1")]
        out_scaled = sem("out_scaled")
        out_made = sem("out_made")
        out_stored = [sem("out_stored0"), sem("out_stored1")]
        pool_step = sem("f_pool_step")
        block = ctx.enter_context(nc.Block())

        def chunks(engine, chunk):
            chunk(0, True, False)
            with engine.Fori(1, NCHUNK - 1) as c:
                chunk(c, False, False)
            chunk(NCHUNK - 1, False, True)

        def used(engine, c, n):
            engine.wait_ge(panel_used, c * PANELS + n + 1)

        @block.sync
        def _(sp):
            wgu = w["w_gate_up"].rearrange("(k p) n -> p k n", p=P)
            wd = w["w_down"].rearrange("(m k p) n -> m p k n", p=P, k=2)
            h2T = w["h2T"].rearrange("(k p) t -> p k t", p=P)

            def panel(c, n, s, dst, src):
                if not isinstance(c * PANELS + n, int) or c * PANELS + n >= 2:
                    sp.wait_ge(raw_given, c * PANELS + n - 1)
                sp.dma_start(dst, src).then_inc(raw_in[s], 16)

            def up_pair(c, j):
                for s in range(2):
                    panel(c, 2 * j + s, s, raw[:, s].rearrange("p (k n) -> p k n", n=P),
                          wgu[:, :, bass.ds(j * P + s * D_FF, P)])

            def down_panel(c, n, s, m, half):
                panel(c, UP + n, s, raw[:, s].rearrange("p (k n) -> p k n", n=HALF),
                      wd[bass.ds(m, 1), :, :, half * HALF:(half + 1) * HALF].rearrange("a p k n -> p (a k) n"))

            def load_x(c):
                sp.dma_start(x_lo[:].bitcast(F32), h2T[:, :, bass.ts(c, TOK)]).then_inc(x_loaded, 16)

            def load_x1(c, t):
                if t < 2 and (not isinstance(c, int) or c > 0):
                    sp.wait_ge(out_made, c * TPC - 1 + t)
                sp.dma_start(x1[:, t % 2], w["x1"][bass.ds(c * TOK + t * P, P), :]).then_inc(x1_in[t % 2], 16)

            def store(c, t):
                sp.wait_ge(out_made, c * TPC + t + 1)
                sp.dma_start(w["out"][bass.ds(c * TOK + t * P, P), :], out[:, t % 2]).then_inc(out_stored[t % 2], 16)
                if t + 2 < TPC:
                    load_x1(c, t + 2)

            def chunk(c, first, last):
                for j in range(1, 3):
                    up_pair(c, j)
                    if not first:
                        store(c - 1, 2 * j - 2)
                        store(c - 1, 2 * j - 1)
                with sp.Fori(3, KF) as j:
                    up_pair(c, j)
                with sp.Fori(0, DOWN // 2) as q:
                    for s in range(2):
                        down_panel(c, q * 2 + s, s, q * 2 + s, 0)
                if not last:
                    used(sp, c, UP - 1)
                    load_x(c + 1)
                down_panel(c, DOWN - 1, 0, DOWN - 1, 0)
                down_panel(c, DOWN, 1, 0, 1)
                with sp.Fori(0, DOWN // 2) as q:
                    for s in range(2):
                        down_panel(c, q * 2 + s + DOWN + 1, s, q * 2 + s + 1, 1)
                if not last:
                    up_pair(c + 1, 0)
                for t in range(2):
                    load_x1(c, t)

            load_x(0)
            up_pair(0, 0)
            sp.dma_start(row[:], w["mods"][5:6, :].partition_broadcast(P)).then_inc(row_in, 16)
            chunks(sp, chunk)
            for t in range(TPC):
                store(NCHUNK - 1, t)
            for s in range(2):
                sp.wait_ge(out_stored[s], 16 * NCHUNK * TPC // 2)

        @block.gpsimd
        def _(pool):
            for j, v in enumerate((-0.5, 1.0 / D, EPS)):
                nc.gpsimd.memset(cols[:, j, :], v).then_inc(pool_step, 1)
            pool.wait_ge(pool_step, 3)

            def roots(c):
                pool.wait_ge(square_done, (c + 1) * 2 * TPC)
                nc.gpsimd.tensor_tensor(rstd[:], ssq[:, 0, :], ssq[:, 1, :], ALU.add).then_inc(pool_step, 1)
                pool.wait_ge(pool_step, 3 * c + 4)
                nc.gpsimd.tensor_tensor(rstd[:], rstd[:], cols[:, 1, :], ALU.mult).then_inc(pool_step, 1)
                pool.wait_ge(pool_step, 3 * c + 5)
                nc.gpsimd.tensor_tensor(rstd[:], rstd[:], cols[:, 2, :], ALU.add).then_inc(pool_step, 1)
                pool.wait_ge(pool_step, 3 * c + 6)
                nc.gpsimd.tensor_tensor(rstd[:], rstd[:], cols[:, 0, :], ALU.pow).then_inc(root_done, 1)

            with pool.Fori(0, NCHUNK) as c:
                roots(c)

        @block.tensor
        def _(pe):
            def up_product(c, j, s, which):
                n = 2 * j + which
                bank = (gbank, ubank)[which][s]
                pe.wait_ge(panel_ready, c * PANELS + n + 1)
                pe.wait_ge((gated, act_made)[which], c * KF + j + 1)
                for k in range(KD):
                    wh, wl = p_hi[:, which, k * P:(k + 1) * P], p_lo[:, which, k * P:(k + 1) * P]
                    nc.tensor.matmul(bank[:], wh, x_hi[:, k, :], start=(k == 0), stop=False)
                    nc.tensor.matmul(bank[:], wh, x_lo[:, k, :], start=False, stop=False)
                    mm = nc.tensor.matmul(bank[:], wl, x_hi[:, k, :], start=False, stop=(k == KD - 1))
                mm.then_inc(panel_used, 1)

            def down_product(c, n, s, m, start, stop, refill=False):
                pe.wait_ge(panel_ready, c * PANELS + UP + n + 1)
                for i in range(2):
                    wh, wl = p_hi[:, s, i * HALF:(i + 1) * HALF], p_lo[:, s, i * HALF:(i + 1) * HALF]
                    for t in range(TPC):
                        if refill and i == 0:
                            pe.wait_ge(half_copied, c * TPC + t + 1)
                        ah = a_hi[:, m * 2 + i, t * P:(t + 1) * P]
                        al = a_lo[:, m * 2 + i, t * P:(t + 1) * P]
                        begin, end = start and i == 0, stop and i == 1
                        nc.tensor.matmul(dbank[t][:], ah, wh, start=begin, stop=False)
                        nc.tensor.matmul(dbank[t][:], ah, wl, start=False, stop=False)
                        mm = nc.tensor.matmul(dbank[t][:], al, wh, start=False, stop=end)
                mm.then_inc(panel_used, 1)

            def chunk(c, first, last):
                with pe.Fori(0, KF // 2) as jj:
                    pe.wait_ge(x_split, 2 * (c + 1))
                    for s in range(2):
                        for which in range(2):
                            up_product(c, jj * 2 + s, s, which)
                pe.wait_ge(act_ready, (c + 1) * KF + 2)
                if not first:
                    pe.wait_ge(out_made, c * TPC)
                for n in range(2 * DOWN):
                    m = n % DOWN
                    down_product(c, n, n % 2, m, m == 0, m == DOWN - 1, refill=(n == DOWN))

            chunks(pe, chunk)

        @block.scalar
        def _(act):
            def panel_high_part(c, pair, s):
                act.wait_ge(raw_in[s], (c * (PANELS // 2) + pair + 1) * 16)
                if not isinstance(c * PANELS + 2 * pair, int) or c * PANELS + 2 * pair > 0:
                    act.wait_ge(panel_used, c * PANELS + 2 * pair + s - 1)
                nc.scalar.activation(p_hi[:, s], raw[:, s], ACT.Copy).then_inc(panel_high, 1)

            def x_high_part(c):
                act.wait_ge(x_loaded, 16 * (c + 1))
                nc.scalar.activation(x_hi[:], x_lo[:].bitcast(F32), ACT.Copy).then_inc(x_high, 1)

            def square(src, c, half, t):
                n = (c * 2 + half) * TPC + t
                if not isinstance(n, int) or n > 0:
                    act.wait_ge(square_done, n)
                nc.scalar.activation(junk[:], src, ACT.Square, accum_out=ssq[:, half, t:t + 1]
                                     ).then_inc(square_done, 1)

            def up_step(c, j, s):
                used(act, c, 2 * j)
                act.wait_ge(gated, c * KF + j + 1)
                nc.scalar.activation(th[:, s], gbank[s][:], ACT.Tanh, scale=0.5).then_inc(tanh_done, 1)
                for which in range(2):
                    panel_high_part(c, j + 1, which)
                act.wait_ge(act_made, c * KF + j + 3)
                nc.scalar.activation(a_hi[:, bass.ds(j, 1), :].rearrange("p a n -> p (a n)"), act32[:, s],
                                     ACT.Copy).then_inc(act_high, 1)

            def second_squares(c):
                used(act, c, PANELS - 1)
                for t in range(TPC):
                    square(dbank[t][:], c, 1, t)

            def chunk(c, first, last):
                if not first:
                    second_squares(c - 1)
                with act.Fori(0, KF // 2) as jj:
                    for s in range(2):
                        up_step(c, jj * 2 + s, s)
                with act.Fori(0, DOWN // 2) as q:
                    for s in range(2):
                        panel_high_part(c, q + KF + 1, s)
                used(act, c, UP + DOWN - 1)
                for t in range(TPC):
                    nc.scalar.activation(first_half[:, t, :], dbank[t][:], ACT.Copy).then_inc(half_copied, 1)
                for s in range(2):
                    panel_high_part(c, KF + DOWN // 2 + 1, s)
                if not first:
                    act.wait_ge(root_done, c)
                for t in range(TPC):
                    act.wait_ge(half_copied, c * TPC + t + 1)
                    square(first_half[:, t, :], c, 0, t)
                with act.Fori(DOWN // 2 + 2, DOWN - 1) as q:
                    for s in range(2):
                        panel_high_part(c, q + KF, s)
                if not last:
                    x_high_part(c + 1)
                for s in range(2):
                    panel_high_part(c, KF + DOWN - 1, s)
                if not last:
                    for s in range(2):
                        panel_high_part(c + 1, 0, s)

            nc.scalar.sem_inc(gated, 2)
            x_high_part(0)
            for s in range(2):
                panel_high_part(0, 0, s)
            chunks(act, chunk)
            second_squares(NCHUNK - 1)

        @block.vector
        def _(dve):
            def low_part(number, s):
                dve.wait_ge(panel_high, number + 1)
                nc.vector.tensor_tensor(p_lo[:, s], raw[:, s], p_hi[:, s].bitcast(F32), ALU.subtract
                                        ).then_inc(panel_ready, 1)
                dve.wait_ge(panel_ready, number + 1)
                nc.vector.sem_inc(raw_given, 1)

            def x_low_part(c):
                dve.wait_ge(x_high, c + 1)
                for half in range(2):
                    k = slice(half * KD // 2, (half + 1) * KD // 2)
                    nc.vector.tensor_tensor(x_lo[:, k, :], x_lo[:, k, :].bitcast(F32), x_hi[:, k, :].bitcast(F32),
                                            ALU.subtract).then_inc(x_split, 1)

            def up_step(c, j, s):
                dve.wait_ge(tanh_done, c * KF + j + 1)
                dve.wait_ge(act_ready, c * KF + j + 1)
                nc.vector.scalar_tensor_tensor(act32[:, s], th[:, s], 1.0, gbank[s][:], ALU.add, ALU.mult
                                               ).then_inc(gated, 1)
                low_part(c * PANELS + 2 * j + 2, 0)
                dve.wait_ge(gated, c * KF + j + 3)
                used(dve, c, 2 * j + 1)
                nc.vector.scalar_tensor_tensor(act32[:, s], act32[:, s], 0.5, ubank[s][:], ALU.mult, ALU.mult
                                               ).then_inc(act_made, 1)
                low_part(c * PANELS + 2 * j + 3, 1)
                dve.wait_ge(act_high, c * KF + j + 1)
                a = a_hi[:, bass.ds(j, 1), :].rearrange("p a n -> p (a n)").bitcast(F32)
                nc.vector.tensor_tensor(a_lo[:, bass.ds(j, 1), :].rearrange("p a n -> p (a n)"), act32[:, s], a,
                                        ALU.subtract).then_inc(act_ready, 1)

            def tail_tile(c, t):
                s = t % 2
                dve.wait_ge(root_done, c + 1)
                n = c * TPC + t
                if not isinstance(n, int) or n >= 2:
                    dve.wait_ge(out_stored[s], (c * (TPC // 2) + t // 2) * 16)
                for half, src in enumerate((first_half[:, t, :], dbank[t][:])):
                    at = slice(half * HALF, (half + 1) * HALF)
                    nc.vector.scalar_tensor_tensor(out[:, s, at], src, rstd[:, t:t + 1], row[:, at],
                                                   ALU.mult, ALU.mult).then_inc(out_scaled, 1)
                dve.wait_ge(out_scaled, 2 * n + 2)
                dve.wait_ge(x1_in[s], (c * (TPC // 2) + t // 2 + 1) * 16)
                nc.vector.tensor_tensor(out[:, s], out[:, s], x1[:, s], ALU.add).then_inc(out_made, 1)

            def chunk(c, first, last):
                for s in range(2):
                    if not first:
                        tail_tile(c - 1, 2 * s)
                        tail_tile(c - 1, 2 * s + 1)
                    up_step(c, s, s)
                with dve.Fori(1, KF // 2) as jj:
                    for s in range(2):
                        up_step(c, jj * 2 + s, s)
                with dve.Fori(1, DOWN - 1) as q:
                    for s in range(2):
                        low_part(c * PANELS + UP + q * 2 + s, s)
                if not last:
                    x_low_part(c + 1)
                for s in range(2):
                    low_part(c * PANELS + PANELS - 2 + s, s)
                if not last:
                    for s in range(2):
                        low_part((c + 1) * PANELS + s, s)

            nc.vector.sem_inc(act_made, 2)
            nc.vector.sem_inc(act_ready, 2)
            x_low_part(0)
            for s in range(2):
                low_part(s, s)
            dve.wait_ge(row_in, 16)
            chunks(dve, chunk)
            for t in range(TPC):
                tail_tile(NCHUNK - 1, t)


_INS = ["x", "c", "w_ada", "b_ada", "g_pre_mix", "g_post_mix", "w_in", "q_norm_g", "kv_norm_g", "w_uq",
        "w_qidx", "w_ukv", "a_sinks", "w_o", "g_pre_ffn", "g_post_ffn", "w_gate_up", "w_down"]


def kernel(**inputs):
    import numpy as _np
    import concourse.bacc as _bacc
    from concourse import mybir as _mybir
    from concourse.bass_utils import run_bass_kernel_spmd as _run

    nc = _bacc.Bacc("TRN2", target_bir_lowering=False, num_devices=1)
    arrays, w = {}, {}
    for name in _INS:
        a = _np.ascontiguousarray(inputs[name])
        if a.ndim == 3:
            a = a[0]
        arrays[f"in_{name}"] = a
        w[name] = nc.dram_tensor(f"in_{name}", a.shape, _mybir.dt.from_np(a.dtype), kind="ExternalInput").ap()
    w["out"] = nc.dram_tensor("out_0", (T, D), F32, kind="ExternalOutput").ap()
    w["mods"] = nc.dram_tensor("mods", (6, D), F32).ap()
    w["mixT"] = nc.dram_tensor("mixT", (D, T), F32).ap()
    w["h2T"] = nc.dram_tensor("h2T", (D, T), F32).ap()
    w["x1"] = nc.dram_tensor("x1", (T, D), F32).ap()
    modulation(nc, w)
    mixing(nc, w)
    project_output(nc, w)
    ffn(nc, w)
    r = _run(nc, [arrays], core_ids=[0])
    return _np.reshape(r.results[0]["out_0"], (1, T, D))
```
